# Optimizing a Trainium2 kernel written in Bass

```python
import math
import jax, jax.numpy as jnp
from jax import lax
import numpy as np

D_MODEL = 1024
BATCH = 1
SEQ = 1024
DEPTH = 1

GRID_W = 64
CTX_LEN = 256
D_MIX = D_MODEL
F_WIDTH = D_MIX // 4
N_FGROUPS = 4
FGROUP_DIM = F_WIDTH // N_FGROUPS
SSD_WIDTH = D_MIX - F_WIDTH
SSD_HEAD_DIM = 64
SSD_HEADS = SSD_WIDTH // SSD_HEAD_DIM
SSD_GROUPS = 4
HEADS_PER_GROUP = SSD_HEADS // SSD_GROUPS
D_STATE = 128
BC_WIDTH = SSD_GROUPS * D_STATE
CONV_DIM = SSD_WIDTH + 2 * BC_WIDTH
D_CONV = 7
CHUNK = 128
XBC_OFF = F_WIDTH + SSD_WIDTH
IN_WIDTH = XBC_OFF + CONV_DIM + 2 * SSD_HEADS
D_FF = -(-8 * D_MODEL // (3 * 256)) * 256
N_MOD = 6
EPS = 1e-6


def rms_norm(x, g):
    xf = x.astype(jnp.float32)
    y = xf * lax.rsqrt(jnp.mean(xf * xf, axis=-1, keepdims=True) + EPS)
    return (y * g.astype(jnp.float32)).astype(x.dtype)

def modulate(h, shift, scale):
    return h * (1 + scale) + shift

def conv_rows(u, w, bias, rows, row_len):
    b, L, ch = u.shape
    half = D_CONV // 2
    up = jnp.pad(u.reshape(b, rows, row_len, ch), ((0, 0), (0, 0), (half, half), (0, 0)))
    out = bias
    for k in range(D_CONV):
        out = out + up[:, :, k:k + row_len, :] * w[:, k]
    return out.reshape(b, L, ch)

def fourier_mix(u):
    b, L, _ = u.shape
    ug = u.reshape(b, L, N_FGROUPS, FGROUP_DIM).astype(jnp.float32)
    yf = jnp.fft.fft2(ug, axes=(1, 3), norm='ortho').real
    return yf.reshape(b, L, F_WIDTH).astype(u.dtype)

def ssd_scan(xdt, dA, Bm, Cm, h0, with_output):
    b, L = xdt.shape[:2]
    nc = L // CHUNK
    xq = xdt.reshape(b, nc, CHUNK, SSD_GROUPS, HEADS_PER_GROUP, SSD_HEAD_DIM)
    aq = dA.reshape(b, nc, CHUNK, SSD_GROUPS, HEADS_PER_GROUP)
    Bq = Bm.reshape(b, nc, CHUNK, SSD_GROUPS, D_STATE)
    Cq = Cm.reshape(b, nc, CHUNK, SSD_GROUPS, D_STATE)
    a_cs = jnp.cumsum(aq, axis=2)
    a_end = a_cs[:, :, -1]
    st = jnp.einsum('bcsgn,bcsgr,bcsgrp->bcgrpn', Bq, jnp.exp(a_end[:, :, None] - a_cs), xq)

    def step(h, inp):
        s_c, a_c = inp
        return jnp.exp(a_c)[..., None, None] * h + s_c, h

    h_fin, h_in = lax.scan(step, h0, (jnp.moveaxis(st, 1, 0), jnp.moveaxis(a_end, 1, 0)))
    if not with_output:
        return None, h_fin
    h_in = jnp.moveaxis(h_in, 0, 1)
    seg = a_cs[:, :, :, None] - a_cs[:, :, None]
    lower = jnp.tril(jnp.ones((CHUNK, CHUNK), dtype=bool))[:, :, None, None]
    decay = jnp.exp(jnp.where(lower, seg, -jnp.inf))
    scores = jnp.einsum('bcqgn,bcsgn->bcqsg', Cq, Bq)
    y_diag = jnp.einsum('bcqsg,bcqsgr,bcsgrp->bcqgrp', scores, decay, xq)
    y_off = jnp.einsum('bcqgn,bcgrpn,bcqgr->bcqgrp', Cq, h_in, jnp.exp(a_cs))
    return (y_diag + y_off).reshape(b, L, SSD_HEADS, SSD_HEAD_DIM), h_fin

def ssd_direction(xs, Bm, Cm, dt_raw, dt_bias, a_log, h0, with_output):
    b, L, _ = xs.shape
    dt = jax.nn.softplus(dt_raw.astype(jnp.float32) + dt_bias.astype(jnp.float32))
    dA = dt * -jnp.exp(a_log.astype(jnp.float32))
    xdt = xs.reshape(b, L, SSD_HEADS, SSD_HEAD_DIM) * dt[..., None]
    return ssd_scan(xdt, dA, Bm.reshape(b, L, SSD_GROUPS, D_STATE),
                    Cm.reshape(b, L, SSD_GROUPS, D_STATE), h0, with_output)

def ssd_bidir(xs, Bm, Cm, dt_raw, dt_bias, a_log, h0_fwd, h0_bwd, with_output):
    flip = lambda t: jnp.flip(t, axis=1)
    y_f, h_f = ssd_direction(xs, Bm, Cm, dt_raw[..., :SSD_HEADS], dt_bias[0], a_log[0], h0_fwd, with_output)
    y_b, h_b = ssd_direction(flip(xs), flip(Bm), flip(Cm), flip(dt_raw[..., SSD_HEADS:]),
                             dt_bias[1], a_log[1], h0_bwd, with_output)
    y = y_f + flip(y_b) if with_output else None
    return y, h_f, h_b

def mixer_inputs(h, w_in, conv_w, conv_b, rows, row_len, full):
    p = h @ (w_in if full else w_in[:, XBC_OFF:])
    if full:
        u_f, z, rest = p[..., :F_WIDTH], p[..., F_WIDTH:XBC_OFF], p[..., XBC_OFF:]
    else:
        u_f, z, rest = None, None, p
    xbc = jax.nn.silu(conv_rows(rest[..., :CONV_DIM], conv_w, conv_b, rows, row_len))
    dt_raw = rest[..., CONV_DIM:]
    xs = xbc[..., :SSD_WIDTH]
    Bm = xbc[..., SSD_WIDTH:SSD_WIDTH + BC_WIDTH]
    Cm = xbc[..., SSD_WIDTH + BC_WIDTH:]
    return u_f, z, xs, Bm, Cm, dt_raw

def mixer_output(u_f, z, xs, y, d_skip, g_ssd, w_out):
    b, L, _ = xs.shape
    y = y + xs.reshape(b, L, SSD_HEADS, SSD_HEAD_DIM) * d_skip[:, None]
    y = y.reshape(b, L, SSD_WIDTH).astype(xs.dtype)
    y = rms_norm(y * jax.nn.silu(z), g_ssd)
    return jnp.concatenate([fourier_mix(u_f), y], axis=-1) @ w_out

def swiglu(h, w_gate, w_up, w_down):
    return (jax.nn.silu(h @ w_gate) * (h @ w_up)) @ w_down

def first_inputs(seed: int = 0) -> dict:
    key = jax.random.key(seed)
    ks = jax.random.split(key, 24)
    nrm = lambda k, shape, fan_in: jax.random.normal(k, shape, jnp.float32) * fan_in ** -0.5
    gain = lambda k, n: 1.0 + 0.05 * jax.random.normal(k, (DEPTH, n), jnp.float32)
    dt0 = jnp.exp(jax.random.uniform(ks[10], (DEPTH, 2, SSD_HEADS), jnp.float32)
                  * (math.log(0.1) - math.log(0.001)) + math.log(0.001))
    return {
        'x': jax.random.normal(ks[0], (BATCH, SEQ, D_MODEL), jnp.float32),
        'c': jax.random.normal(ks[1], (BATCH, D_MODEL), jnp.float32),
        'ctx': jax.random.normal(ks[2], (BATCH, CTX_LEN, D_MODEL), jnp.float32),
        'c_ctx': jax.random.normal(ks[3], (D_MODEL,), jnp.float32),
        'w_ada': nrm(ks[4], (DEPTH, D_MODEL, N_MOD * D_MODEL), D_MODEL),
        'b_ada': 0.01 * jax.random.normal(ks[5], (DEPTH, N_MOD * D_MODEL), jnp.float32),
        'g_pre_mix': gain(ks[6], D_MODEL),
        'g_post_mix': gain(ks[7], D_MODEL),
        'g_pre_ffn': gain(ks[8], D_MODEL),
        'g_post_ffn': gain(ks[9], D_MODEL),
        'w_in': nrm(ks[11], (DEPTH, D_MODEL, IN_WIDTH), D_MODEL),
        'conv_w': nrm(ks[12], (DEPTH, CONV_DIM, D_CONV), D_CONV),
        'conv_b': 0.01 * jax.random.normal(ks[13], (DEPTH, CONV_DIM), jnp.float32),
        'dt_bias': dt0 + jnp.log(-jnp.expm1(-dt0)),
        'a_log': jnp.log(jax.random.uniform(ks[14], (DEPTH, 2, SSD_HEADS), jnp.float32, 1.0, 16.0)),
        'd_skip': 1.0 + 0.1 * jax.random.normal(ks[15], (DEPTH, SSD_HEADS), jnp.float32),
        'g_ssd': gain(ks[16], SSD_WIDTH),
        'w_out': nrm(ks[17], (DEPTH, D_MIX, D_MODEL), D_MIX),
        'w_gate': nrm(ks[18], (DEPTH, D_MODEL, D_FF), D_MODEL),
        'w_up': nrm(ks[19], (DEPTH, D_MODEL, D_FF), D_MODEL),
        'w_down': nrm(ks[20], (DEPTH, D_FF, D_MODEL), D_FF),
    }

def first_block(x, c, ctx, c_ctx, w_ada, b_ada, g_pre_mix, g_post_mix, g_pre_ffn, g_post_ffn,
              w_in, conv_w, conv_b, dt_bias, a_log, d_skip, g_ssd, w_out, w_gate, w_up, w_down):
    b = x.shape[0]
    rows = x.shape[1] // GRID_W
    ctx_len = ctx.shape[1]
    h0 = jnp.zeros((b, SSD_GROUPS, HEADS_PER_GROUP, SSD_HEAD_DIM, D_STATE), jnp.float32)
    for l in range(DEPTH):
        keep_ctx = l + 1 < DEPTH
        mx = (jax.nn.silu(c) @ w_ada[l] + b_ada[l])[:, None, :]
        sm_x, cm_x, gm_x, sf_x, cf_x, gf_x = jnp.split(mx, N_MOD, axis=-1)
        mc = jax.nn.silu(c_ctx) @ w_ada[l] + b_ada[l]
        sm_c, cm_c, gm_c, sf_c, cf_c, gf_c = jnp.split(mc, N_MOD, axis=-1)

        hc = modulate(rms_norm(ctx, g_pre_mix[l]), sm_c, cm_c)
        uf_c, z_c, xs_c, B_c, C_c, dt_c = mixer_inputs(hc, w_in[l], conv_w[l], conv_b[l], 1, ctx_len, keep_ctx)
        y_c, hf_c, hb_c = ssd_bidir(xs_c, B_c, C_c, dt_c, dt_bias[l], a_log[l], h0, h0, keep_ctx)

        hx = modulate(rms_norm(x, g_pre_mix[l]), sm_x, cm_x)
        uf_x, z_x, xs_x, B_x, C_x, dt_x = mixer_inputs(hx, w_in[l], conv_w[l], conv_b[l], rows, GRID_W, True)
        y_x, _, _ = ssd_bidir(xs_x, B_x, C_x, dt_x, dt_bias[l], a_log[l], hf_c, hb_c, True)
        x = x + gm_x * rms_norm(mixer_output(uf_x, z_x, xs_x, y_x, d_skip[l], g_ssd[l], w_out[l]), g_post_mix[l])

        hx2 = modulate(rms_norm(x, g_pre_ffn[l]), sf_x, cf_x)
        x = x + gf_x * rms_norm(swiglu(hx2, w_gate[l], w_up[l], w_down[l]), g_post_ffn[l])

        if keep_ctx:
            out_c = mixer_output(uf_c, z_c, xs_c, y_c, d_skip[l], g_ssd[l], w_out[l])
            ctx = ctx + gm_c * rms_norm(out_c, g_post_mix[l])
            hc2 = modulate(rms_norm(ctx, g_pre_ffn[l]), sf_c, cf_c)
            ctx = ctx + gf_c * rms_norm(swiglu(hc2, w_gate[l], w_up[l], w_down[l]), g_post_ffn[l])
    return x


DEPTH_2 = 2

N_MIXERS = 2
N_ATTN_LAYERS = (DEPTH_2 + 1) // 2
N_POOL_LAYERS = DEPTH_2 // 2
N_HEADS = 16
QK_NOPE_DIM = 64
QK_ROPE_DIM = 32
V_HEAD_DIM = 64
Q_LORA_RANK = 256
KV_LORA_RANK = 128
ROPE_THETA = 10000.0
Q_BLOCK = 128
POOL_WINDOWS = (2, 4, 8, 16)
N_POOL_GROUPS = 4
POOL_GROUP_DIM = D_MODEL // N_POOL_GROUPS
N_EXPERT_GROUPS = 8
EXPERTS_PER_GROUP = 8
N_EXPERTS = N_EXPERT_GROUPS * EXPERTS_PER_GROUP
TOP_K_IN_GROUP = 2
D_EXPERT = 256
EXPERT_BLOCK = 128
DEEPNORM_ALPHA = (2 * DEPTH_2) ** 0.25
DEEPNORM_BETA = (8 * DEPTH_2) ** -0.25
LN_EPS = 1e-5
RMS_EPS = 1e-6


def layer_norm(x, g, b):
    xf = x.astype(jnp.float32)
    mu = jnp.mean(xf, axis=-1, keepdims=True)
    var = jnp.mean(jnp.square(xf - mu), axis=-1, keepdims=True)
    y = (xf - mu) * lax.rsqrt(var + LN_EPS) * g.astype(jnp.float32) + b.astype(jnp.float32)
    return y.astype(x.dtype)

def rms_norm_2(x, g):
    xf = x.astype(jnp.float32)
    y = xf * lax.rsqrt(jnp.mean(jnp.square(xf), axis=-1, keepdims=True) + RMS_EPS)
    return (y * g.astype(jnp.float32)).astype(x.dtype)

def rope_tables(positions):
    inv_freq = ROPE_THETA ** (-jnp.arange(0, QK_ROPE_DIM, 2, dtype=jnp.float32) / QK_ROPE_DIM)
    ang = positions.astype(jnp.float32)[..., None] * inv_freq
    return jnp.cos(ang), jnp.sin(ang)

def apply_rope(x, cos, sin):
    xf = x.astype(jnp.float32)
    half = xf.shape[-1] // 2
    x1, x2 = xf[..., :half], xf[..., half:]
    y = jnp.concatenate([x1 * cos - x2 * sin, x2 * cos + x1 * sin], axis=-1)
    return y.astype(x.dtype)

def mla_mixer(x, cos, sin, w_in, q_norm, w_uq, kv_norm, w_ukv, w_o):
    B, S, _ = x.shape
    lat = x @ w_in
    c_q = rms_norm_2(lat[..., :Q_LORA_RANK], q_norm)
    c_kv = rms_norm_2(lat[..., Q_LORA_RANK:Q_LORA_RANK + KV_LORA_RANK], kv_norm)
    k_rope = apply_rope(lat[..., Q_LORA_RANK + KV_LORA_RANK:], cos, sin)
    q = (c_q @ w_uq).reshape(B, S, N_HEADS, QK_NOPE_DIM + QK_ROPE_DIM)
    q_nope = q[..., :QK_NOPE_DIM]
    q_rope = apply_rope(q[..., QK_NOPE_DIM:], cos[:, :, None, :], sin[:, :, None, :])
    kv = (c_kv @ w_ukv).reshape(B, S, N_HEADS, QK_NOPE_DIM + V_HEAD_DIM)
    k_nope, v = kv[..., :QK_NOPE_DIM], kv[..., QK_NOPE_DIM:]
    scale = (QK_NOPE_DIM + QK_ROPE_DIM) ** -0.5
    outs = []
    for qs in range(0, S, Q_BLOCK):
        qe = qs + Q_BLOCK
        s = (jnp.einsum('bqhd,bkhd->bhqk', q_nope[:, qs:qe], k_nope[:, :qe],
                        preferred_element_type=jnp.float32)
             + jnp.einsum('bqhr,bkr->bhqk', q_rope[:, qs:qe], k_rope[:, :qe],
                          preferred_element_type=jnp.float32)) * scale
        causal = jnp.arange(qe)[None, :] <= jnp.arange(qs, qe)[:, None]
        s = jnp.where(causal, s, -jnp.inf)
        p = jax.nn.softmax(s, axis=-1).astype(v.dtype)
        outs.append(jnp.einsum('bhqk,bkhd->bqhd', p, v[:, :qe]))
    o = jnp.concatenate(outs, axis=1).reshape(B, S, N_HEADS * V_HEAD_DIM)
    return o @ w_o

def pool_mixer(x, w, b, scale):
    B, S, D = x.shape
    xf = x.astype(jnp.float32)
    cs = jnp.concatenate([jnp.zeros((B, 1, D), jnp.float32), jnp.cumsum(xf, axis=1)], axis=1)
    t = jnp.arange(S)
    means = []
    for gi, win in enumerate(POOL_WINDOWS):
        sl = slice(gi * POOL_GROUP_DIM, (gi + 1) * POOL_GROUP_DIM)
        hi = cs[:, 1:, sl]
        lo = cs[:, jnp.maximum(t + 1 - win, 0), sl]
        cnt = jnp.minimum(t + 1, win).astype(jnp.float32)[:, None]
        means.append((hi - lo) / cnt)
    pooled = jnp.concatenate(means, axis=-1) - xf
    y = jnp.einsum('bsgc,gcd->bsgd', pooled.reshape(B, S, N_POOL_GROUPS, POOL_GROUP_DIM),
                   w.astype(jnp.float32)).reshape(B, S, D) + b.astype(jnp.float32)
    return (y * scale.astype(jnp.float32)).astype(x.dtype)

def hier_moe(h, w_grp, b_grp, w_exp, b_exp, w1, w3, w2):
    B, S, D = h.shape
    tok = h.reshape(-1, D)
    N = tok.shape[0]
    hf = tok.astype(jnp.float32)
    g_logits = hf @ w_grp.astype(jnp.float32) + b_grp.astype(jnp.float32)
    g_prob = jax.nn.softmax(g_logits, axis=-1)
    g_sel = jnp.argmax(g_logits, axis=-1)
    g_gate = jnp.take_along_axis(g_prob, g_sel[:, None], axis=-1)
    e_logits = (hf @ w_exp.astype(jnp.float32) + b_exp.astype(jnp.float32)).reshape(N, N_EXPERT_GROUPS, EXPERTS_PER_GROUP)
    e_logits = jnp.take_along_axis(e_logits, g_sel[:, None, None], axis=1)[:, 0]
    e_prob = jax.nn.softmax(e_logits, axis=-1)
    top_p, top_i = lax.top_k(e_prob, TOP_K_IN_GROUP)
    gate = g_gate * top_p / jnp.sum(top_p, axis=-1, keepdims=True)
    expert = g_sel[:, None] * EXPERTS_PER_GROUP + top_i
    A = N * TOP_K_IN_GROUP
    flat_e = expert.reshape(-1).astype(jnp.int32)
    flat_tok = jnp.repeat(jnp.arange(N, dtype=jnp.int32), TOP_K_IN_GROUP)
    flat_gate = gate.reshape(-1)
    order = jnp.argsort(flat_e)
    e_sorted, tok_sorted, gate_sorted = flat_e[order], flat_tok[order], flat_gate[order]
    counts = jnp.bincount(flat_e, length=N_EXPERTS)
    padded = (counts + EXPERT_BLOCK - 1) // EXPERT_BLOCK * EXPERT_BLOCK
    start = jnp.cumsum(counts) - counts
    pend = jnp.cumsum(padded)
    pstart = pend - padded
    dest = pstart[e_sorted] + (jnp.arange(A, dtype=jnp.int32) - start[e_sorted])
    n_blocks = (A + N_EXPERTS * (EXPERT_BLOCK - 1) + EXPERT_BLOCK - 1) // EXPERT_BLOCK
    rows = jnp.zeros((n_blocks * EXPERT_BLOCK, D), tok.dtype).at[dest].set(tok[tok_sorted])
    blk_e = jnp.minimum(jnp.searchsorted(pend, jnp.arange(n_blocks) * EXPERT_BLOCK, side='right'), N_EXPERTS - 1)

    def expert_block(args):
        xb, e = args
        hb = jax.nn.silu(xb @ w1[e]) * (xb @ w3[e])
        return hb @ w2[e]

    y_rows = lax.map(expert_block, (rows.reshape(n_blocks, EXPERT_BLOCK, D), blk_e)).reshape(-1, D)
    y = y_rows[dest].astype(jnp.float32) * gate_sorted[:, None]
    out = jnp.zeros((N, D), jnp.float32).at[tok_sorted].add(y)
    return out.reshape(B, S, D).astype(h.dtype)

def second_inputs(seed: int = 0) -> dict:
    key = jax.random.key(seed)
    ks = jax.random.split(key, 24)
    f32 = jnp.float32
    nrm = lambda k, shape, s: jax.random.normal(k, shape, f32) * s
    LAT = Q_LORA_RANK + KV_LORA_RANK + QK_ROPE_DIM
    return {
        'x': jax.random.normal(ks[0], (BATCH, SEQ, D_MODEL), f32),
        'positions': (jnp.arange(SEQ, dtype=jnp.int32)[None, :]
                      + jax.random.randint(ks[1], (BATCH, 1), 0, 4096, dtype=jnp.int32)),
        'ln_g': 1.0 + nrm(ks[2], (DEPTH_2, 2, D_MODEL), 0.02),
        'ln_b': nrm(ks[3], (DEPTH_2, 2, D_MODEL), 0.02),
        'mla_w_in': nrm(ks[4], (N_ATTN_LAYERS, D_MODEL, LAT), D_MODEL ** -0.5),
        'mla_q_norm': 1.0 + nrm(ks[5], (N_ATTN_LAYERS, Q_LORA_RANK), 0.02),
        'mla_w_uq': nrm(ks[6], (N_ATTN_LAYERS, Q_LORA_RANK, N_HEADS * (QK_NOPE_DIM + QK_ROPE_DIM)), Q_LORA_RANK ** -0.5),
        'mla_kv_norm': 1.0 + nrm(ks[7], (N_ATTN_LAYERS, KV_LORA_RANK), 0.02),
        'mla_w_ukv': nrm(ks[8], (N_ATTN_LAYERS, KV_LORA_RANK, N_HEADS * (QK_NOPE_DIM + V_HEAD_DIM)), KV_LORA_RANK ** -0.5),
        'mla_w_o': nrm(ks[9], (N_ATTN_LAYERS, N_HEADS * V_HEAD_DIM, D_MODEL), (N_HEADS * V_HEAD_DIM) ** -0.5 * DEEPNORM_BETA),
        'pool_w': nrm(ks[10], (N_POOL_LAYERS, N_POOL_GROUPS, POOL_GROUP_DIM, POOL_GROUP_DIM), POOL_GROUP_DIM ** -0.5 * DEEPNORM_BETA),
        'pool_b': nrm(ks[11], (N_POOL_LAYERS, D_MODEL), 0.02),
        'pool_scale': 1.0 + nrm(ks[12], (N_POOL_LAYERS, D_MODEL), 0.1),
        'moe_w_grp': nrm(ks[13], (DEPTH_2, D_MODEL, N_EXPERT_GROUPS), D_MODEL ** -0.5),
        'moe_b_grp': nrm(ks[14], (DEPTH_2, N_EXPERT_GROUPS), 0.01),
        'moe_w_exp': nrm(ks[15], (DEPTH_2, D_MODEL, N_EXPERTS), D_MODEL ** -0.5),
        'moe_b_exp': nrm(ks[16], (DEPTH_2, N_EXPERTS), 0.01),
        'moe_w1': nrm(ks[17], (DEPTH_2, N_EXPERTS, D_MODEL, D_EXPERT), D_MODEL ** -0.5),
        'moe_w3': nrm(ks[18], (DEPTH_2, N_EXPERTS, D_MODEL, D_EXPERT), D_MODEL ** -0.5),
        'moe_w2': nrm(ks[19], (DEPTH_2, N_EXPERTS, D_EXPERT, D_MODEL), D_EXPERT ** -0.5 * DEEPNORM_BETA),
    }

def second_block(x, positions, ln_g, ln_b, mla_w_in, mla_q_norm, mla_w_uq, mla_kv_norm, mla_w_ukv, mla_w_o,
              pool_w, pool_b, pool_scale, moe_w_grp, moe_b_grp, moe_w_exp, moe_b_exp, moe_w1, moe_w3, moe_w2):
    cos, sin = rope_tables(positions)
    for i in range(DEPTH_2):
        j = i // N_MIXERS
        if i % N_MIXERS == 0:
            f = mla_mixer(x, cos, sin, mla_w_in[j], mla_q_norm[j], mla_w_uq[j],
                          mla_kv_norm[j], mla_w_ukv[j], mla_w_o[j])
        else:
            f = pool_mixer(x, pool_w[j], pool_b[j], pool_scale[j])
        x = layer_norm(DEEPNORM_ALPHA * x + f, ln_g[i, 0], ln_b[i, 0])
        f = hier_moe(x, moe_w_grp[i], moe_b_grp[i], moe_w_exp[i], moe_b_exp[i],
                     moe_w1[i], moe_w3[i], moe_w2[i])
        x = layer_norm(DEEPNORM_ALPHA * x + f, ln_g[i, 1], ln_b[i, 1])
    return x


def setup_inputs(seed=0):
    out = dict(first_inputs(seed))
    for name, value in second_inputs(seed + 1).items():
        if name != "x":
            out[name + "_2"] = value
    return out


def reference(
    x, c, ctx, c_ctx, w_ada, b_ada, g_pre_mix, g_post_mix, g_pre_ffn, g_post_ffn, w_in, conv_w,
    conv_b, dt_bias, a_log, d_skip, g_ssd, w_out, w_gate, w_up, w_down, positions_2, ln_g_2,
    ln_b_2, mla_w_in_2, mla_q_norm_2, mla_w_uq_2, mla_kv_norm_2, mla_w_ukv_2, mla_w_o_2,
    pool_w_2, pool_b_2, pool_scale_2, moe_w_grp_2, moe_b_grp_2, moe_w_exp_2, moe_b_exp_2,
    moe_w1_2, moe_w3_2, moe_w2_2,
):
    x = first_block(
        x, c, ctx, c_ctx, w_ada, b_ada, g_pre_mix, g_post_mix, g_pre_ffn, g_post_ffn, w_in,
        conv_w, conv_b, dt_bias, a_log, d_skip, g_ssd, w_out, w_gate, w_up, w_down,
    )
    return second_block(
        x, positions_2, ln_g_2, ln_b_2, mla_w_in_2, mla_q_norm_2, mla_w_uq_2, mla_kv_norm_2,
        mla_w_ukv_2, mla_w_o_2, pool_w_2, pool_b_2, pool_scale_2, moe_w_grp_2, moe_b_grp_2,
        moe_w_exp_2, moe_b_exp_2, moe_w1_2, moe_w3_2, moe_w2_2,
    )


_drawn_inputs = setup_inputs


def setup_inputs(seed=0):
    import zlib

    import numpy as np

    out = dict(_drawn_inputs(seed))
    spreads = {}
    factors = {'ctx': 3.363,
     'b_ada': 2.746,
     'conv_b': 6.462,
     'd_skip': 7.714,
     'mla_q_norm_2': 8.0,
     'mla_kv_norm_2': 8.0,
     'pool_b_2': 3.255,
     'moe_b_grp_2': 21.82,
     'moe_b_exp_2': 24.087}
    for name, (base, spread) in spreads.items():
        noise = np.random.default_rng([zlib.crc32(name.encode()), seed]).standard_normal(out[name].shape)
        drawn = base * np.exp(spread * noise) if base else spread * noise
        out[name] = __import__('jax').numpy.asarray(drawn.astype(out[name].dtype))
    for name, factor in factors.items():
        out[name] = (out[name] * factor).astype(out[name].dtype)
    return out
```

```python
from contextlib import ExitStack

import numpy as np

import concourse.bass as bass
from concourse import mybir

F32 = mybir.dt.float32
I32 = mybir.dt.int32
U32 = mybir.dt.uint32
BF16 = mybir.dt.bfloat16
ALU = mybir.AluOpType
ACT = mybir.ActivationFunctionType
AX = mybir.AxisListType
ds = bass.ds

P = 128
L = 1024
D = 1024
LC = 256
NT = L // P
NTC = LC // P
KD = D // P
NMOD = 6
FW = 256
SW = 768
HD = 64
NH = 12
NG = 4
HPG = NH // NG
CONV = 1792
NCV = CONV // P
TAPS = 7
HALF = TAPS // 2
ROW = 64
DT0 = FW + SW + CONV
INW = DT0 + 2 * NH
DFF = 2816
KF = DFF // P
EPS = 1e-6
LN_EPS = 1e-5
ALPHA = 4 ** 0.25
NEG = -1e30
AH = 16
QL, KVL, RD = 256, 128, 32
LAT = QL + KVL + RD
SCALE = 96.0 ** -0.5
NE = 64
DE = 256
MAIN = NE
OVER = 16
NB = MAIN + OVER
WINS = (2, 4, 8, 16)

C_ID, C_UP, C_LO, C_SUP, C_NEG, C_IOTA, C_TOK, C_CB, C_SB, C_FREQ = 0, 128, 256, 384, 512, 640, 768, 784, 912, 1040
C_POOL = 1056
C_THR = C_POOL + 16
C_W = C_THR + 8

NCOL = 8 + 8 + 8 + 8 + 6 + 2 + 1 + NCV
COL_GSSD, COL_QN, COL_KVN, COL_CB = 32, 38, 40, 41


def constant_table():
    t = np.zeros((P, C_W), np.float32)
    i = np.arange(P)
    t[:, C_ID:C_ID + P] = np.eye(P)
    t[:, C_UP:C_UP + P] = i[:, None] <= i[None]
    t[:, C_LO:C_LO + P] = i[:, None] >= i[None]
    t[:, C_SUP:C_SUP + P] = i[:, None] < i[None]
    t[:, C_NEG:C_NEG + P] = np.where(i[None] <= i[:, None], 0.0, NEG)
    t[:, C_IOTA:C_IOTA + P] = i[None]
    for k in range(2):
        for m in range(NT):
            t[:, C_TOK + k * NT + m] = 2 * (m * P + i) + k + 1
    a = 2 * np.pi * np.outer(np.arange(64), np.arange(64)) / 64
    for g in range(2):
        s = slice(64 * g, 64 * g + 64)
        t[s, C_CB + 64 * g:C_CB + 64 * g + 64] = np.cos(a) / 256
        t[s, C_SB + 64 * g:C_SB + 64 * g + 64] = -np.sin(a) / 256
    t[:, C_FREQ:C_FREQ + 16] = (10000.0 ** (-np.arange(0, 32, 2, dtype=np.float32) / np.float32(32))).astype(np.float32)
    t[:, C_POOL:C_POOL + 16] = 1.0 / (np.arange(16) + 1)
    t[:, C_THR:C_THR + 8] = P * (np.arange(8) + 1)
    return t


def dft_table():
    n = np.arange(L)
    a = 2 * np.pi * (np.outer(n, n) % L) / L
    return np.stack([np.cos(a), np.sin(a)], 1).astype(np.float32)


def modulation(nc, K, A):
    NCH, W, NBUF = NMOD * D // 512, 512, 3
    with ExitStack() as ctx:
        def sb(n, s, d=F32):
            return ctx.enter_context(nc.sbuf_tensor("ada_" + n, s, d))

        wbuf = sb("w", [P, NBUF, KD, W])
        rows = sb("rows", [NCOL, P])
        mod = sb("mod", [2, NMOD * D])
        bada = sb("bada", [2, NMOD * D])
        cT = sb("cT", [P, 16])
        modT = sb("modT", [P, 48, 2])
        small, rows_t, cols_ok, silu_ok = K.sem("small_in"), K.sem("rows_t"), K.sem("cols_ok"), K.sem("silu_ok")
        w_in = [K.sem(f"ada_w{i}") for i in range(NBUF)]
        mm, ev = K.sem("ada_mm"), K.sem("ada_ev")
        tr, br, ok = K.sem("ada_tr"), K.sem("ada_br"), K.sem("ada_ok")
        w_dram = A["w_ada"][0].rearrange("(k p) n -> p k n", p=P)
        vecs = [("c", 8), ("c_ctx", 8), ("g_pre_mix", 8), ("g_pre_ffn", 8), ("g_ssd", 6),
                ("mla_q_norm_2", 2), ("mla_kv_norm_2", 1), ("conv_b", NCV)]
        ident = K.cst[:, C_ID:C_ID + P]

        with nc.Block() as block:
            @block.sync
            def _(sp):
                sp.dma_start(K.cst[:, :], A["consts"]).then_inc(small, 16)
                at = 0
                for name, n in vecs:
                    v = A[name]
                    flat = v if len(v.shape) == 1 else v.rearrange("a n -> (a n)")
                    sp.dma_start(rows[at:at + n, :], flat.rearrange("(a p) -> a p", p=P)).then_inc(small, 16)
                    at += n
                for r in range(2):
                    sp.dma_start(bada[r:r + 1, :], A["b_ada"]).then_inc(small, 16)
                sp.dma_start(K.G1[:, :], A["g_post_mix"].to_broadcast([P, D])).then_inc(small, 16)
                sp.dma_start(K.G2[:, :], A["g_post_ffn"].to_broadcast([P, D])).then_inc(small, 16)
                with sp.Fori(0, NCH // NBUF) as i:
                    for s in range(NBUF):
                        sp.wait_ge(mm, i * NBUF + s + 1)
                        sp.dma_start(wbuf[:, s], w_dram[:, :, ds((i * NBUF + s) * W, W)]).then_inc(w_in[s], 16)

            @block.tensor
            def _(pe):
                pe.sem_inc(mm, NBUF)
                pe.wait_ge(small, 16 * (len(vecs) + 5))
                pe.transpose(K.ps[7][:, 0:NCOL], rows[:, :], ident[0:NCOL, 0:NCOL]).then_inc(rows_t, 1)
                pe.wait_ge(silu_ok, 1)
                with pe.Fori(0, NCH // NBUF) as i:
                    for s in range(NBUF):
                        pe.wait_ge(w_in[s], 16 * (i + 1))
                        pe.wait_ge(ev, i * NBUF + s + 1)
                        for k in range(KD):
                            last = pe.matmul(K.ps[s][0:2, :], cT[:, k:16:8], wbuf[:, s, k, :], start=k == 0, stop=k == KD - 1)
                        last.then_inc(mm, 1)
                pe.wait_ge(ev, NCH + NBUF)
                for j in range(48):
                    last = pe.transpose(K.ps[4][:, 2 * j:2 * j + 2], mod[:, j * P:(j + 1) * P], ident[0:2, 0:2])
                last.then_inc(tr, 1)
                for n, (bank, src) in enumerate(((5, 2 * D), (6, 2 * D + 512), (7, 5 * D), (3, 5 * D + 512))):
                    last = pe.matmul(K.ps[bank][:, :], K.cst[0:1, C_UP:C_UP + P], mod[0:1, src:src + 512], start=True, stop=True)
                last.then_inc(br, 1)

            @block.scalar
            def _(act):
                act.wait_ge(cols_ok, 1)
                act.activation(cT[:, :], K.cols[:, 0:16], ACT.Silu).then_inc(silu_ok, 1)

            @block.vector
            def _(dve):
                dve.sem_inc(ev, NBUF)
                dve.wait_ge(rows_t, 1)
                dve.tensor_copy(K.cols[:, :], K.ps[7][:, 0:NCOL]).then_inc(cols_ok, 1)
                with dve.Fori(0, NCH // NBUF) as i:
                    for s in range(NBUF):
                        dve.wait_ge(mm, i * NBUF + s + 1 + NBUF)
                        at = ds((i * NBUF + s) * 512, 512)
                        dve.tensor_tensor(mod[:, at], K.ps[s][0:2, :], bada[:, at], ALU.add).then_inc(ev, 1)
                dve.wait_ge(tr, 1)
                dve.tensor_copy(modT[:, :, :], K.ps[4][:, 0:96].rearrange("p (j v) -> p j v", v=2)).then_inc(ok, 1)
                dve.wait_ge(ok, 1)
                for dst, j, v, g in ((K.A1, 8, 0, 16), (K.A1c, 8, 1, 16), (K.A2, 32, 0, 24)):
                    dve.scalar_tensor_tensor(out=dst[:, :], in0=modT[:, j:j + 8, v], scalar=1.0, in1=K.cols[:, g:g + 8],
                                             op0=ALU.add, op1=ALU.mult)
                for dst, j, v in ((K.B1, 0, 0), (K.B1c, 0, 1), (K.B2, 24, 0)):
                    dve.tensor_copy(dst[:, :], modT[:, j:j + 8, v])
                dve.wait_ge(br, 1)
                for G, banks in ((K.G1, (5, 6)), (K.G2, (7, 3))):
                    for h, b in enumerate(banks):
                        dve.tensor_tensor(G[:, h * 512:(h + 1) * 512], K.ps[b][:, :], G[:, h * 512:(h + 1) * 512], ALU.mult)


def rms_to_feature_major(nc, K, tag, src, norm, jobs, load=None):
    n_tiles = sum(j[1] for j in jobs)
    groups = [(k, t0, t, min(4, n - t), dst, A_, B_) for t0, n, dst, A_, B_ in jobs
              for t in range(0, n, 4) for k in range(KD)]
    NBK = 4
    with ExitStack() as ctx:
        ss = ctx.enter_context(nc.sbuf_tensor(tag + "_ss", [P, n_tiles], F32))
        rs = ctx.enter_context(nc.sbuf_tensor(tag + "_rs", [P, n_tiles], F32))
        junk = ctx.enter_context(nc.sbuf_tensor(tag + "_junk", [P, D], F32))
        x_in = [K.sem(f"{tag}_in{t}") for t in range(n_tiles)] if load else None
        sq, var, root, inv, scaled = (K.sem(tag + n) for n in ("_sq", "_var", "_root", "_inv", "_scaled"))
        tr, ev_v, ev_a = K.sem(tag + "_tr"), K.sem(tag + "_ev_v"), K.sem(tag + "_ev_a")

        def bank(g):
            return K.ps[g % NBK]

        with nc.Block() as block:
            @block.sync
            def _(sp):
                if load:
                    for t in range(n_tiles):
                        sp.dma_start(src[:, t, :], load(t)).then_inc(x_in[t], 16)

            @block.scalar
            def _(act):
                for t in range(n_tiles):
                    if load:
                        act.wait_ge(x_in[t], 16)
                    act.activation(junk[:, :], src[:, t, :], ACT.Square, accum_out=ss[:, t:t + 1]).then_inc(sq, 1)
                    act.drain()
                act.wait_ge(var, 1)
                act.activation(rs[:, :], ss[:, :], ACT.Sqrt).then_inc(root, 1)
                for g, (k, t0, t, n, dst, A_, B_) in enumerate(groups):
                    if g % 2 == 1:
                        act.wait_ge(tr, g + 1)
                        act.activation(dst[:, k, t * P:(t + n) * P], bank(g)[:, 0:n * P], ACT.Identity,
                                       scale=A_[:, k:k + 1], bias=B_[:, k:k + 1]).then_inc(ev_a, 1)

            @block.vector
            def _(dve):
                dve.wait_ge(sq, n_tiles)
                dve.tensor_scalar(ss[:, :], ss[:, :], 1.0 / D, EPS, ALU.mult, ALU.add).then_inc(var, 1)
                dve.wait_ge(root, 1)
                dve.reciprocal(rs[:, :], rs[:, :]).then_inc(inv, 1)
                dve.wait_ge(inv, 1)
                for t in range(n_tiles):
                    dve.tensor_scalar(norm[:, t, :], src[:, t, :], rs[:, t:t + 1], None, ALU.mult).then_inc(scaled, 1)
                for g, (k, t0, t, n, dst, A_, B_) in enumerate(groups):
                    if g % 2 == 0:
                        dve.wait_ge(tr, g + 1)
                        dve.tensor_scalar(dst[:, k, t * P:(t + n) * P], bank(g)[:, 0:n * P],
                                          A_[:, k:k + 1], B_[:, k:k + 1], ALU.mult, ALU.add).then_inc(ev_v, 1)

            @block.tensor
            def _(pe):
                for g, (k, t0, t, n, dst, A_, B_) in enumerate(groups):
                    if g >= NBK:
                        pe.wait_ge(ev_v if g % 2 == 0 else ev_a, (g - NBK) // 2 + 1)
                    pe.wait_ge(scaled, t0 + t + n)
                    for j in range(n):
                        last = pe.transpose(bank(g)[:, j * P:(j + 1) * P], norm[:, t0 + t + j, k * P:(k + 1) * P],
                                            K.cst[:, C_ID:C_ID + P])
                    last.then_inc(tr, 1)


def projections(nc, K, A):
    w_dram = A["w_in"][0].rearrange("(k p) n -> p k n", p=P)
    XF, XFc, HT, HTc, ZT, V = K.XF, K.XFc, K.HT, K.HTc, K.ZT, K.V
    ps = K.ps
    wz = XF[:, 0:6, :].rearrange("p a b -> p (a b)").rearrange("p (k n) -> p k n", k=KD)
    wu = XF[:, 6:8, :].rearrange("p a b -> p (a b)").rearrange("p (k n) -> p k n", k=KD)
    uT = XF[:, 8:10, :]
    NCTX = 5
    with ExitStack() as ctx:
        def sb(n, s, d=F32):
            return ctx.enter_context(nc.sbuf_tensor("pj_" + n, s, d))

        wbuf = sb("w", [P, 2, KD, P])
        wdt = sb("wdt", [P, KD, 24])
        cw = sb("cw", [P, NCV, TAPS])
        cb = K.cols[:, COL_CB:COL_CB + NCV]
        RW = ROW + 2 * HALF
        pad = [sb(f"pad{s}", [P, L // ROW, RW]) for s in range(2)]
        padc = [sb(f"padc{s}", [P, LC + 2 * HALF]) for s in range(2)]
        acc = [sb(f"acc{s}", [P, L // ROW, ROW]) for s in range(2)]
        accc = [sb(f"accc{s}", [P, LC]) for s in range(2)]
        z_in, u_in, s_in = K.sem("pj_z_in"), K.sem("pj_u_in"), K.sem("pj_s_in")
        w_in = [K.sem(f"pj_w{s}") for s in range(2)]
        dt_mm, z_mm, z_ev, u_mm, u_ev, v_mm, v_ev = (K.sem("pj_" + n) for n in ("dtmm", "zmm", "zev", "umm", "uev", "vmm", "vev"))
        mm = [K.sem(f"pj_mm{s}") for s in range(2)]
        padded = [K.sem(f"pj_padded{s}") for s in range(2)]
        convd = [K.sem(f"pj_conv{s}") for s in range(2)]
        silud = [K.sem(f"pj_silu{s}") for s in range(2)]
        zero = K.sem("pj_zero")

        with nc.Block() as block:
            @block.sync
            def _(sp):
                sp.dma_start(wdt[:, :, :], w_dram[:, :, DT0:INW]).then_inc(s_in, 16)
                sp.dma_start(cw[:, :, :], A["conv_w"][0].rearrange("(m p) t -> p m t", p=P)).then_inc(s_in, 16)
                for h in range(2):
                    ks = slice(4 * h, 4 * h + 4)
                    sp.dma_start(wz[:, ks, :], w_dram[:, ks, FW:FW + SW]).then_inc(z_in, 16)
                sp.dma_start(wu, w_dram[:, :, 0:FW]).then_inc(u_in, 16)
                sp.dma_start(K.dtb[:, :], A["dt_bias"].rearrange("a d n -> a (d n)").to_broadcast([P, 24])).then_inc(s_in, 16)
                sp.dma_start(K.alog[:, :], A["a_log"].rearrange("a d n -> a (d n)").to_broadcast([P, 24])).then_inc(s_in, 16)
                sp.dma_start(K.dskip[:, :], A["d_skip"].to_broadcast([P, NH])).then_inc(s_in, 16)

                def pair(i, base):
                    for s in range(2):
                        sp.wait_ge(mm[s], i + base + 1)
                        sp.dma_start(wbuf[:, s], w_dram[:, :, ds(FW + SW + (i + base) * 2 * P + s * P, P)]).then_inc(w_in[s], 16)

                with sp.Fori(0, NCTX) as i:
                    pair(i, 0)
                with sp.Fori(0, NCV // 2 - NCTX) as i:
                    pair(i, NCTX)

            @block.tensor
            def _(pe):
                for s in range(2):
                    pe.sem_inc(mm[s], 1)
                pe.wait_ge(s_in, 16 * 5)
                for t in range(NT + NTC):
                    h = HT[:, :, t * P:(t + 1) * P] if t < NT else HTc[:, :, (t - NT) * P:(t - NT + 1) * P]
                    for k in range(KD):
                        last = pe.matmul(ps[6][:, t * 24:(t + 1) * 24], h[:, k, :], wdt[:, k, :], start=k == 0, stop=k == KD - 1)
                last.then_inc(dt_mm, 1)
                pe.wait_ge(z_in, 32)
                for t in range(NT):
                    if t >= 2:
                        pe.wait_ge(z_ev, t - 1)
                    for h, n in ((0, 512), (1, 256)):
                        for k in range(KD):
                            last = pe.matmul(ps[2 * (t % 2) + h][:, 0:n], HT[:, k, t * P:(t + 1) * P],
                                             wz[:, k, h * 512:h * 512 + n], start=k == 0, stop=k == KD - 1)
                    last.then_inc(z_mm, 1)
                pe.wait_ge(u_in, 16)
                pe.wait_ge(z_ev, NT)
                for m in range(2):
                    for h in range(2):
                        for k in range(KD):
                            last = pe.matmul(ps[2 * m + h][:, :], wu[:, k, m * P:(m + 1) * P], HT[:, k, h * 512:(h + 1) * 512],
                                             start=k == 0, stop=k == KD - 1)
                        last.then_inc(u_mm, 1)
                pe.wait_ge(u_ev, 4)
                for t in range(NT):
                    if t >= 2:
                        pe.wait_ge(v_ev, t - 1)
                    for m in range(2):
                        last = pe.matmul(ps[4 + t % 2][:, m * 256:(m + 1) * 256], uT[:, m, t * P:(t + 1) * P],
                                         K.cst[:, C_CB:C_CB + 256], start=True, stop=True)
                    last.then_inc(v_mm, 1)

                def pair(i, base, with_ctx):
                    for s in range(2):
                        pe.wait_ge(w_in[s], (i + base + 1) * 16)
                        pe.wait_ge(padded[s], i + base + 1)
                        for h in range(2):
                            for k in range(KD):
                                last = pe.matmul(ps[3 * s + h][:, :], wbuf[:, s, k, :], HT[:, k, h * 512:(h + 1) * 512],
                                                 start=k == 0, stop=k == KD - 1)
                        if with_ctx:
                            for k in range(KD):
                                last = pe.matmul(ps[3 * s + 2][:, 0:LC], wbuf[:, s, k, :], HTc[:, k, :],
                                                 start=k == 0, stop=k == KD - 1)
                        last.then_inc(mm[s], 1)

                with pe.Fori(0, NCTX) as i:
                    pair(i, 0, True)
                with pe.Fori(0, NCV // 2 - NCTX) as i:
                    pair(i, NCTX, False)

            @block.scalar
            def _(act):
                for t in range(NT):
                    act.wait_ge(z_mm, t + 1)
                    act.activation(ZT[:, t, 0:512], ps[2 * (t % 2)][:, :], ACT.Silu)
                    act.activation(ZT[:, t, 512:768], ps[2 * (t % 2) + 1][:, 0:256], ACT.Silu).then_inc(z_ev, 1)
                for n in range(4):
                    act.wait_ge(u_mm, n + 1)
                    act.activation(uT[:, n // 2, (n % 2) * 512:(n % 2) * 512 + 512], ps[n][:, :], ACT.Copy).then_inc(u_ev, 1)
                for t in range(NT):
                    act.wait_ge(v_mm, t + 1)
                    act.activation(V[:, t, :], ps[4 + t % 2][:, :], ACT.Copy).then_inc(v_ev, 1)
                act.wait_ge(zero, 1)
                act.wait_ge(v_ev, NT)
                for s in range(2):
                    act.sem_inc(padded[s], 1)

                def pair(i, base, with_ctx):
                    for s in range(2):
                        act.wait_ge(mm[s], i + base + 2)
                        act.wait_ge(convd[s], i + base + 1)
                        for h in range(2):
                            last = act.activation(pad[s][:, 8 * h:8 * h + 8, HALF:HALF + ROW],
                                                  ps[3 * s + h][:, :].rearrange("p (r n) -> p r n", n=ROW), ACT.Copy)
                        if with_ctx:
                            last = act.activation(padc[s][:, HALF:HALF + LC], ps[3 * s + 2][:, 0:LC], ACT.Copy)
                        last.then_inc(padded[s], 1)
                        act.wait_ge(convd[s], i + base + 2)
                        m = (i + base) * 2 + s
                        last = act.activation(XF[:, ds(m, 1), :], acc[s][:, :, :].rearrange("p (o r) n -> p o (r n)", o=1), ACT.Silu)
                        if with_ctx:
                            last = act.activation(XFc[:, ds(m, 1), :], accc[s][:, :].rearrange("p (o n) -> p o n", o=1), ACT.Silu)
                        last.then_inc(silud[s], 1)

                with act.Fori(0, NCTX) as i:
                    pair(i, 0, True)
                with act.Fori(0, NCV // 2 - NCTX) as i:
                    pair(i, NCTX, False)

            @block.gpsimd
            def _(pool):
                for s in range(2):
                    pool.memset(pad[s][:, :, :], 0.0)
                    last = pool.memset(padc[s][:, :], 0.0)
                pool.drain()
                pool.sem_inc(zero, 1)

            @block.vector
            def _(dve):
                dve.wait_ge(s_in, 16 * 5)
                dve.wait_ge(dt_mm, 1)
                dve.tensor_copy(K.dtr[:, :, :], ps[6][:, 0:240].rearrange("p (t n) -> p t n", n=24))
                for s in range(2):
                    dve.sem_inc(convd[s], 1)
                    dve.sem_inc(silud[s], 1)

                def pair(i, base, with_ctx):
                    for s in range(2):
                        m = (i + base) * 2 + s
                        dve.wait_ge(padded[s], i + base + 2)
                        dve.wait_ge(silud[s], i + base + 1)
                        for tap in range(TAPS):
                            w = cw[:, ds(m, 1), tap]
                            if tap == 0:
                                last = dve.tensor_scalar(acc[s][:, :, :], pad[s][:, :, 0:ROW], w, cb[:, ds(m, 1)], ALU.mult, ALU.add)
                                if with_ctx:
                                    last = dve.tensor_scalar(accc[s][:, :], padc[s][:, 0:LC], w, cb[:, ds(m, 1)], ALU.mult, ALU.add)
                            else:
                                last = dve.scalar_tensor_tensor(out=acc[s][:, :, :], in0=pad[s][:, :, tap:tap + ROW], scalar=w,
                                                         in1=acc[s][:, :, :], op0=ALU.mult, op1=ALU.add)
                                if with_ctx:
                                    last = dve.scalar_tensor_tensor(out=accc[s][:, :], in0=padc[s][:, tap:tap + LC], scalar=w,
                                                             in1=accc[s][:, :], op0=ALU.mult, op1=ALU.add)
                            if tap < TAPS - 1:
                                dve.drain()
                        last.then_inc(convd[s], 1)

                with dve.Fori(0, NCTX) as i:
                    pair(i, 0, True)
                with dve.Fori(0, NCV // 2 - NCTX) as i:
                    pair(i, NCTX, False)


def ssd(nc, K, A):
    XF, XFc, TOK, ps, cst = K.XF, K.XFc, K.TOK, K.ps, K.cst
    Y = XF[:, 0:6, :].rearrange("p a b -> p (a b)").rearrange("p (t n) -> p t n", n=SW)
    K.Y = Y
    ident = cst[:, C_ID:C_ID + P]
    xfc = XFc[:, :, :].rearrange("p a b -> p (a b)")
    NTT = NT + NTC
    fwd = [NT + c for c in range(NTC)] + list(range(NT))
    bwd = [NT + c for c in reversed(range(NTC))] + list(reversed(range(NT)))
    units = [(d, (fwd, bwd)[d][i]) for i in range(NTT) for d in range(2)]
    NU, NUC = len(units), 2 * NTC
    turns = [(NT + c, c) for c in range(NTC)] + [(t, t) for t in range(NTC, NT)] + [(t, t) for t in range(NTC)]

    def slot(t):
        return t - NT if t >= NT else t

    with ExitStack() as ctx:
        def sb(n, s, d=F32):
            return ctx.enter_context(nc.sbuf_tensor("sd_" + n, s, d))

        dt, dA, cs, ecs, W, Eend = (sb(n, [P, NTT, 24]) for n in ("dt", "dA", "cs", "ecs", "W", "Eend"))
        ones = sb("ones", [P, P])
        E = [sb("E0", [P, NH, P]), xfc[:, 0:NH * P].rearrange("p (h q) -> p h q", q=P)]
        SCM = [xfc[:, NH * P + 512 * i:NH * P + 512 * i + 512].rearrange("p (g q) -> p g q", q=P) for i in range(2)]
        M = sb("M", [P, NH, P])
        Hs = [sb(f"H{d}", [P, SW]) for d in range(2)]
        tmp = sb("tmp", [P, SW])
        XW = [sb(f"xw{i}", [P, NH, HD]) for i in range(2)]
        XDT = sb("xdt", [P, NH, HD])
        (tr, ev_a, ev_v, pre, pre_a, one, csmm, ready, hz, a_mm, a_v, e_ok, m_ok, xw_ok, xd_ok, st_mm, yo_mm, yd_mm,
         st_v, yo_v, yd_v, dec, y0, y2) = (K.sem("sd_" + n) for n in (
             "tr", "eva", "evv", "pre", "prea", "one", "csmm", "ready", "hz", "amm", "av", "eok", "mok", "xwok", "xdok",
             "stmm", "yomm", "ydmm", "stv", "yov", "ydv", "dec", "y0", "y2"))

        def feat(t, f):
            return XF[:, f, t * P:(t + 1) * P] if t < NT else XFc[:, f, (t - NT) * P:(t - NT + 1) * P]

        def per_head(a, d, t, n):
            return a[:, t, d * NH:(d + 1) * NH].unsqueeze(2).to_broadcast([P, NH, n])

        def xi(u):
            return u - NUC

        with nc.Block() as block:
            @block.tensor
            def _(pe):
                def to_tokens(n):
                    t, sl = turns[n]
                    if n >= 2:
                        pe.wait_ge(ev_a, n - 1)
                        pe.wait_ge(ev_v, n - 1)
                    for f in range(10):
                        last = pe.transpose(ps[3 * (n % 2) + f // 4][:, (f % 4) * P:(f % 4 + 1) * P], feat(t, f), ident)
                    last.then_inc(tr, 1)

                def stage_a(u):
                    d, t = units[u]
                    tri = cst[:, (C_UP, C_LO)[d]:(C_UP, C_LO)[d] + P]
                    for b in range(4):
                        n = 4 * xi(u) + b
                        if n >= 2:
                            pe.wait_ge(a_v, n - 1)
                        if b == 0:
                            for g in range(NG):
                                last = pe.matmul(ps[n % 2][:, g * P:(g + 1) * P], feat(t, 6 + g), feat(t, 10 + g), start=True, stop=True)
                        else:
                            for j in range(4):
                                h = d * NH + 4 * (b - 1) + j
                                last = pe.matmul(ps[n % 2][:, j * P:(j + 1) * P], dA[:, t, h:h + 1].to_broadcast([P, P]), tri, start=True, stop=True)
                        last.then_inc(a_mm, 1)

                def stage_b(u):
                    d, t = units[u]
                    pe.wait_ge(xw_ok, u + 1)
                    if u >= 1:
                        pe.wait_ge(st_v, u)
                    for g in range(NG):
                        last = pe.matmul(ps[6 + g // 2][:, (g % 2) * 192:(g % 2) * 192 + 192], TOK[:, slot(t), SW + g * P:SW + (g + 1) * P],
                                         XW[u % 2][:, :, :].rearrange("p h e -> p (h e)")[:, g * 192:(g + 1) * 192], start=True, stop=True)
                    last.then_inc(st_mm, 1)
                    if u < NUC:
                        return
                    pe.wait_ge(st_v, u - 1)
                    if xi(u) >= 1:
                        pe.wait_ge(yo_v, xi(u))
                    for g in range(NG):
                        last = pe.matmul(ps[4 + g // 2][:, (g % 2) * 192:(g % 2) * 192 + 192], feat(t, 10 + g),
                                         Hs[d][:, g * 192:(g + 1) * 192], start=True, stop=True)
                    last.then_inc(yo_mm, 1)
                    pe.wait_ge(m_ok, xi(u) + 1)
                    pe.wait_ge(xd_ok, xi(u) + 1)
                    if xi(u) >= 1:
                        pe.wait_ge(yd_v, xi(u))
                    for h in range(NH):
                        last = pe.matmul(ps[2 + h // 6][:, (h % 6) * HD:(h % 6 + 1) * HD], M[:, h, :], XDT[:, h, :], start=True, stop=True)
                    last.then_inc(yd_mm, 1)

                for n in range(NT):
                    to_tokens(n)
                pe.wait_ge(pre, 5)
                pe.wait_ge(one, 1)
                pe.matmul(ps[6][:, 0:120], cst[:, C_UP:C_UP + P], dA[:, :, 0:NH], start=True, stop=True)
                pe.matmul(ps[6][:, 120:240], cst[:, C_LO:C_LO + P], dA[:, :, NH:24], start=True, stop=True)
                pe.matmul(ps[6][:, 240:480], ones[:, :], dA[:, :, :], start=True, stop=True).then_inc(csmm, 1)
                for u in range(NUC):
                    stage_b(u)
                for n in range(NT, NTT):
                    to_tokens(n)
                pe.wait_ge(ev_a, NTT)
                pe.wait_ge(ev_v, NTT)
                for u in range(NUC, NU + 1):
                    if u < NU:
                        stage_a(u)
                    if u > NUC:
                        stage_b(u - 1)

            @block.scalar
            def _(act):
                act.activation(W[:, 0, :], K.alog[:, :], ACT.Exp).then_inc(pre_a, 1)
                act.wait_ge(pre, 2)
                act.activation(ecs[:, :, :], dA[:, :, :], ACT.Exp)
                act.drain()
                act.activation(ecs[:, :, :], ecs[:, :, :], ACT.Ln, bias=1.0).then_inc(pre_a, 1)

                def to_tokens(n):
                    act.wait_ge(tr, n + 1)
                    for b in range(2):
                        last = act.activation(TOK[:, turns[n][1], b * 512:(b + 1) * 512], ps[3 * (n % 2) + b][:, :], ACT.Copy)
                    last.then_inc(ev_a, 1)

                for n in range(NT):
                    to_tokens(n)
                act.wait_ge(ready, 2)
                act.activation(ecs[:, :, :], cs[:, :, :], ACT.Exp)
                act.activation(W[:, :, :], W[:, :, :], ACT.Exp)
                act.activation(Eend[:, :, :], Eend[:, :, :], ACT.Exp).then_inc(pre_a, 1)
                for n in range(NT, NTT):
                    to_tokens(n)
                for u in range(NUC, NU):
                    act.wait_ge(a_v, 4 * xi(u) + 4)
                    act.activation(E[u % 2][:, :, :], E[u % 2][:, :, :], ACT.Relu, scale=-1.0)
                    act.drain()
                    act.activation(E[u % 2][:, :, :], E[u % 2][:, :, :], ACT.Exp, scale=-1.0).then_inc(e_ok, 1)

            @block.gpsimd
            def _(pool):
                pool.memset(ones[:, :], 1.0).then_inc(one, 1)
                for d in range(2):
                    last = pool.memset(Hs[d][:, :], 0.0)
                pool.drain()
                pool.wait_ge(ready, 3)
                pool.wait_ge(ev_a, NTC)
                pool.wait_ge(ev_v, NTC)
                for u, (d, t) in enumerate(units):
                    if u == NUC:
                        pool.wait_ge(ready, 4)
                        pool.wait_ge(ev_a, NTT)
                    xs = TOK[:, slot(t), 0:SW].rearrange("p (h e) -> p h e", e=HD)
                    if u >= 2:
                        pool.wait_ge(st_mm, u - 1)
                    pool.tensor_tensor(XW[u % 2][:, :, :], xs, per_head(W, d, t, HD), ALU.mult).then_inc(xw_ok, 1)
                    if u >= NUC:
                        if xi(u) >= 1:
                            pool.wait_ge(yd_mm, xi(u))
                        pool.tensor_tensor(XDT[:, :, :], xs, per_head(dt, d, t, HD), ALU.mult).then_inc(xd_ok, 1)
                        pool.wait_ge(yo_mm, xi(u) + 1)
                    if u >= 2:
                        pool.wait_ge(st_v, u - 1)
                    h3 = Hs[d][:, :].rearrange("p (h e) -> p h e", e=HD)
                    pool.tensor_tensor(h3, h3, per_head(Eend, d, t, HD), ALU.mult).then_inc(dec, 1)
                    if u >= NUC:
                        pool.wait_ge(yo_v, xi(u) + 1)
                        pool.wait_ge(yd_v, xi(u) + 1)
                        pool.tensor_tensor(Y[:, t, :], Y[:, t, :], tmp[:, :], ALU.add).then_inc(y2, 1)

            @block.vector
            def _(dve):
                n24 = [P, NTT, 24]
                dve.tensor_tensor(dt[:, :, :], K.dtr[:, :, :], K.dtb[:, :].unsqueeze(1).to_broadcast(n24), ALU.add).then_inc(pre, 1)
                dve.wait_ge(pre, 1)
                dve.scalar_tensor_tensor(out=dA[:, :, :], in0=dt[:, :, :], scalar=-1.0, in1=dt[:, :, :],
                                         op0=ALU.mult, op1=ALU.min).then_inc(pre, 1)
                dve.wait_ge(pre, 2)
                dve.tensor_single_scalar(dt[:, :, :], dt[:, :, :], 0.0, ALU.max).then_inc(pre, 1)
                dve.wait_ge(pre_a, 2)
                dve.wait_ge(pre, 3)
                dve.tensor_tensor(dt[:, :, :], dt[:, :, :], ecs[:, :, :], ALU.add).then_inc(pre, 1)
                dve.wait_ge(pre, 4)
                dve.scalar_tensor_tensor(out=dA[:, :, :], in0=dt[:, :, :], scalar=-1.0,
                                         in1=W[:, 0, :].unsqueeze(1).to_broadcast(n24), op0=ALU.mult, op1=ALU.mult).then_inc(pre, 1)

                def to_tokens(n):
                    dve.wait_ge(tr, n + 1)
                    dve.tensor_copy(TOK[:, turns[n][1], 1024:1280], ps[3 * (n % 2) + 2][:, 0:256]).then_inc(ev_v, 1)

                for n in range(NT):
                    to_tokens(n)
                dve.wait_ge(csmm, 1)
                for d in range(2):
                    dve.tensor_copy(cs[:, :, d * NH:(d + 1) * NH], ps[6][:, d * 120:d * 120 + 120].rearrange("p (t h) -> p t h", h=NH))
                dve.tensor_copy(Eend[:, :, :], ps[6][:, 240:480].rearrange("p (t h) -> p t h", h=24)).then_inc(ready, 1)
                dve.drain()
                dve.tensor_tensor(W[:, :, :], Eend[:, :, :], cs[:, :, :], ALU.subtract).then_inc(ready, 1)
                dve.wait_ge(pre_a, 3)
                dve.tensor_tensor(W[:, :, :], W[:, :, :], dt[:, :, :], ALU.mult).then_inc(ready, 1)
                def stage_a(u):
                    d, t = units[u]
                    for b in range(4):
                        n = 4 * xi(u) + b
                        dve.wait_ge(a_mm, n + 1)
                        if b == 0:
                            tri = cst[:, (C_UP, C_LO)[d]:(C_UP, C_LO)[d] + P].unsqueeze(1).to_broadcast([P, NG, P])
                            dve.tensor_tensor(SCM[u % 2], ps[n % 2][:, :].rearrange("p (g q) -> p g q", q=P), tri, ALU.mult).then_inc(a_v, 1)
                        else:
                            h = 4 * (b - 1)
                            dve.tensor_tensor(E[u % 2][:, h:h + 4, :], ps[n % 2][:, :].rearrange("p (g q) -> p g q", q=P),
                                              cs[:, t, d * NH + h:d * NH + h + 4].unsqueeze(2).to_broadcast([P, 4, P]), ALU.subtract).then_inc(a_v, 1)

                def state(u):
                    d, t = units[u]
                    dve.wait_ge(st_mm, u + 1)
                    dve.wait_ge(dec, u + 1)
                    for b in range(2):
                        last = dve.tensor_tensor(Hs[d][:, b * 384:(b + 1) * 384], ps[6 + b][:, 0:384], Hs[d][:, b * 384:(b + 1) * 384], ALU.add)
                    last.then_inc(st_v, 1)

                def stage_b(u):
                    d, t = units[u]
                    dve.wait_ge(e_ok, xi(u) + 1)
                    if xi(u) >= 1:
                        dve.wait_ge(yd_mm, xi(u))
                    dve.tensor_tensor(M[:, :, :].rearrange("p (g r) q -> p g r q", r=HPG), E[u % 2][:, :, :].rearrange("p (g r) q -> p g r q", r=HPG),
                                      SCM[u % 2].unsqueeze(2).to_broadcast([P, NG, HPG, P]), ALU.mult).then_inc(m_ok, 1)
                    dve.wait_ge(yo_mm, xi(u) + 1)
                    if xi(u) >= 1:
                        dve.wait_ge(y2, xi(u))
                    for b in range(2):
                        last = dve.tensor_tensor(tmp[:, b * 384:(b + 1) * 384].rearrange("p (h e) -> p h e", e=HD),
                                                 ps[4 + b][:, 0:384].rearrange("p (h e) -> p h e", e=HD),
                                                 ecs[:, t, d * NH + 6 * b:d * NH + 6 * b + 6].unsqueeze(2).to_broadcast([P, 6, HD]), ALU.mult)
                    last.then_inc(yo_v, 1)
                    state(u)
                    dve.wait_ge(yd_mm, xi(u) + 1)
                    for b in range(2):
                        last = dve.tensor_tensor(Y[:, t, b * 384:(b + 1) * 384], ps[2 + b][:, 0:384], Y[:, t, b * 384:(b + 1) * 384], ALU.add)
                    last.then_inc(yd_v, 1)

                for u in range(NUC):
                    state(u)
                for n in range(NT, NTT):
                    to_tokens(n)
                dve.wait_ge(ev_a, NTT)
                for t in range(NT):
                    last = dve.tensor_tensor(Y[:, t, :].rearrange("p (h e) -> p h e", e=HD), TOK[:, t, 0:SW].rearrange("p (h e) -> p h e", e=HD),
                                             K.dskip[:, :].unsqueeze(2).to_broadcast([P, NH, HD]), ALU.mult)
                last.then_inc(ready, 1)
                for u in range(NUC, NU + 1):
                    if u < NU:
                        stage_a(u)
                    if u > NUC:
                        stage_b(u - 1)


def mixer_output(nc, K, A):
    Y, ZT, V, HT, X, ps = K.Y, K.ZT, K.V, K.HT, K.X, K.ps
    ident = K.cst[:, C_ID:C_ID + P]
    wo = K.XF[:, 6:14, :]
    NJ = SW // P
    with ExitStack() as ctx:
        def sb(n, s, d=F32):
            return ctx.enter_context(nc.sbuf_tensor("mo_" + n, s, d))

        dft = sb("dft", [P, 2, 2, L])
        junk = sb("junk", [P, D])
        st = sb("st", [P, 3, NT])
        xin = sb("xin", [P, 2, D])
        dft_in = [K.sem(f"mo_dft{s}") for s in range(2)]
        x_in = [K.sem(f"mo_x{s}") for s in range(2)]
        (wo_in, four, gat, sq, sqd, rt, inv, nrm, tr, eva, evv, f_ev, mm, cpy, sq2, var2, rt2, fin, addd) = (K.sem("mo_" + n) for n in (
            "woin", "four", "gat", "sq", "sqd", "rt", "inv", "nrm", "tr", "eva", "evv", "fev", "mm", "cpy", "sq2", "var2", "rt2", "fin", "addd"))
        dft_dram = A["dft"].rearrange("(t p) c k -> t p (c k)", p=P)

        with nc.Block() as block:
            @block.sync
            def _(sp):
                for t in range(NT):
                    if t >= 2:
                        sp.wait_ge(four, t - 1)
                    sp.dma_start(dft[:, t % 2], dft_dram[t]).then_inc(dft_in[t % 2], 16)
                    if t == 1:
                        sp.dma_start(wo, A["w_out"][0].rearrange("(k p) n -> p k n", p=P)).then_inc(wo_in, 16)
                for t in range(NT):
                    if t >= 2:
                        sp.wait_ge(addd, t - 1)
                    sp.dma_start(xin[:, t % 2], A["x"][0, t * P:(t + 1) * P, :]).then_inc(x_in[t % 2], 16)

            @block.tensor
            def _(pe):
                for t in range(NT):
                    pe.wait_ge(dft_in[t % 2], 16 * (t // 2 + 1))
                    for m in range(2):
                        for c in range(2):
                            for h in range(2):
                                last = pe.matmul(ps[2 * m + h][:, :], V[:, t, m * 256 + c * P:m * 256 + (c + 1) * P],
                                                 dft[:, t % 2, c, h * 512:(h + 1) * 512], start=t == 0 and c == 0, stop=t == NT - 1 and c == 1)
                    last.then_inc(four, 1)
                for g in range(2 * NJ):
                    j, half = g // 2, g % 2
                    if g >= 4:
                        pe.wait_ge(eva if g % 2 == 0 else evv, (g - 4) // 2 + 1)
                    pe.wait_ge(nrm, 4 * half + 4)
                    for i in range(4):
                        last = pe.transpose(ps[4 + g % 4][:, i * P:(i + 1) * P], Y[:, 4 * half + i, j * P:(j + 1) * P], ident)
                    last.then_inc(tr, 1)
                pe.wait_ge(wo_in, 16)
                pe.wait_ge(f_ev, 4)
                pe.wait_ge(eva, NJ)
                pe.wait_ge(evv, NJ)
                for t in range(NT):
                    if t >= 4:
                        pe.wait_ge(cpy, t - 3)
                    for h in range(2):
                        for k in range(KD):
                            last = pe.matmul(ps[2 * (t % 4) + h][:, :], HT[:, k, t * P:(t + 1) * P], wo[:, k, h * 512:(h + 1) * 512],
                                             start=k == 0, stop=k == KD - 1)
                    last.then_inc(mm, 1)

            @block.scalar
            def _(act):
                for t in range(NT):
                    act.wait_ge(gat, t + 1)
                    act.activation(junk[:, 0:SW], Y[:, t, :], ACT.Square, accum_out=st[:, 0, t:t + 1]).then_inc(sq, 1)
                    act.drain()
                act.wait_ge(sqd, 1)
                act.activation(st[:, 1, :], st[:, 0, :], ACT.Sqrt).then_inc(rt, 1)
                act.wait_ge(four, NT)
                for n in range(4):
                    act.activation(HT[:, n // 2, (n % 2) * 512:(n % 2) * 512 + 512], ps[n][:, :], ACT.Copy).then_inc(f_ev, 1)
                for g in range(0, 2 * NJ, 2):
                    act.wait_ge(tr, g + 1)
                    act.activation(HT[:, 2 + g // 2, 0:512], ps[4 + g % 4][:, :], ACT.Identity,
                                   scale=K.cols[:, COL_GSSD + g // 2:COL_GSSD + g // 2 + 1], bias=0.0).then_inc(eva, 1)
                for t in range(NT):
                    act.wait_ge(cpy, t + 1)
                    act.activation(junk[:, :], X[:, t, :], ACT.Square, accum_out=st[:, 2, t:t + 1]).then_inc(sq2, 1)
                    act.drain()
                act.wait_ge(var2, 1)
                act.activation(st[:, 1, :], st[:, 0, :], ACT.Sqrt).then_inc(rt2, 1)

            @block.vector
            def _(dve):
                for t in range(NT):
                    dve.tensor_tensor(Y[:, t, :], Y[:, t, :], ZT[:, t, :], ALU.mult).then_inc(gat, 1)
                dve.wait_ge(sq, NT)
                dve.tensor_scalar(st[:, 0, :], st[:, 0, :], 1.0 / SW, EPS, ALU.mult, ALU.add).then_inc(sqd, 1)
                dve.wait_ge(rt, 1)
                dve.reciprocal(st[:, 1, :], st[:, 1, :]).then_inc(inv, 1)
                dve.wait_ge(inv, 1)
                for t in range(NT):
                    dve.tensor_scalar(Y[:, t, :], Y[:, t, :], st[:, 1, t:t + 1], None, ALU.mult).then_inc(nrm, 1)
                for g in range(1, 2 * NJ, 2):
                    dve.wait_ge(tr, g + 1)
                    dve.tensor_scalar(HT[:, 2 + g // 2, 512:1024], ps[4 + g % 4][:, :],
                                      K.cols[:, COL_GSSD + g // 2:COL_GSSD + g // 2 + 1], None, ALU.mult).then_inc(evv, 1)
                for t in range(NT):
                    dve.wait_ge(mm, t + 1)
                    for h in range(2):
                        last = dve.tensor_copy(X[:, t, h * 512:(h + 1) * 512], ps[2 * (t % 4) + h][:, :])
                    last.then_inc(cpy, 1)
                dve.wait_ge(sq2, NT)
                dve.tensor_scalar(st[:, 0, :], st[:, 2, :], 1.0 / D, EPS, ALU.mult, ALU.add).then_inc(var2, 1)
                dve.wait_ge(rt2, 1)
                dve.reciprocal(st[:, 1, :], st[:, 1, :]).then_inc(inv, 1)
                dve.wait_ge(inv, 2)
                for t in range(NT):
                    dve.scalar_tensor_tensor(out=X[:, t, :], in0=X[:, t, :], scalar=st[:, 1, t:t + 1], in1=K.G1[:, :],
                                             op0=ALU.mult, op1=ALU.mult).then_inc(fin, 1)

            @block.gpsimd
            def _(pool):
                for t in range(NT):
                    pool.wait_ge(fin, t + 1)
                    pool.wait_ge(x_in[t % 2], 16 * (t // 2 + 1))
                    pool.tensor_tensor(X[:, t, :], X[:, t, :], xin[:, t % 2, :], ALU.add).then_inc(addd, 1)


def swiglu(nc, K, A):
    HT, X, ps = K.HT, K.X, K.ps
    NRING, GRP = 6, 4
    wslot = [K.XC[:, NT:NT + 2, :].rearrange("p a b -> p (a b)").rearrange("p (s k n) -> p s k n", s=2, k=KD),
             K.hreg[:, KD * L:10 * D].rearrange("p (s k n) -> p s k n", s=2, k=KD)]
    gu_dram = [A[n][0].rearrange("(k p) n -> p k n", p=P) for n in ("w_gate", "w_up")]
    wd_dram = A["w_down"][0].rearrange("(f p) n -> f p n", p=P)
    with ExitStack() as ctx:
        def sb(n, s, d=F32):
            return ctx.enter_context(nc.sbuf_tensor("sw_" + n, s, d))

        mid = sb("mid", [P, KF, L])
        ring = sb("ring", [P, NRING, D])
        junk = K.HT
        st = sb("st", [P, 4, NT])
        w_in = [K.sem(f"sw_w{s}") for s in range(2)]
        ring_in = [K.sem(f"sw_ring{s}") for s in range(NRING)]
        mm = [K.sem(f"sw_mm{s}") for s in range(2)]
        gate = [K.sem(f"sw_gate{s}") for s in range(2)]
        up = [K.sem(f"sw_up{s}") for s in range(2)]
        down, tile_mm, sq, var, rt, inv, fin, scl = (K.sem("sw_" + n) for n in ("down", "tilemm", "sq", "var", "rt", "inv", "fin", "scl"))
        T = K.hreg[:, KD * L:10 * D].rearrange("p (s n) -> p s n", s=2)

        with nc.Block() as block:
            @block.sync
            def _(sp):
                with sp.Fori(0, KF // 2) as i:
                    for s in range(2):
                        sp.wait_ge(mm[s], i + 1)
                        for j in range(2):
                            sp.dma_start(wslot[j][:, s], gu_dram[j][:, :, ds(i * 2 * P + s * P, P)]).then_inc(w_in[s], 16)
                for n in range(2 * KF):
                    if n >= NRING:
                        sp.wait_ge(down, n - NRING + 1)
                    sp.dma_start(ring[:, n % NRING, :], wd_dram[n % KF]).then_inc(ring_in[n % NRING], 16)

            @block.tensor
            def _(pe):
                for s in range(2):
                    pe.sem_inc(mm[s], 1)
                with pe.Fori(0, KF // 2) as i:
                    for s in range(2):
                        pe.wait_ge(w_in[s], i * 32 + 32)
                        pe.wait_ge(gate[s], i + 1)
                        pe.wait_ge(up[s], i + 1)
                        for j in range(2):
                            for h in range(2):
                                for k in range(KD):
                                    last = pe.matmul(ps[4 * s + 2 * j + h][:, :], wslot[j][:, s, k, :], HT[:, k, h * 512:(h + 1) * 512],
                                                     start=k == 0, stop=k == KD - 1)
                        last.then_inc(mm[s], 1)
                for s in range(2):
                    pe.wait_ge(up[s], KF // 2 + 1)
                for n in range(2 * KF):
                    q, f = n // KF, n % KF
                    if f == 0 and q == 1:
                        pe.wait_ge(fin, GRP)
                    pe.wait_ge(ring_in[n % NRING], 16 * (n // NRING + 1))
                    for t in range(GRP):
                        for h in range(2):
                            last = pe.matmul(ps[2 * t + h][:, :], mid[:, f, (q * GRP + t) * P:(q * GRP + t + 1) * P],
                                             ring[:, n % NRING, h * 512:(h + 1) * 512], start=f == 0, stop=f == KF - 1)
                    last.then_inc(down, 1)

            @block.scalar
            def _(act):
                for s in range(2):
                    act.sem_inc(gate[s], 1)
                with act.Fori(0, KF // 2) as i:
                    for s in range(2):
                        act.wait_ge(mm[s], i + 2)
                        for h in range(2):
                            last = act.activation(mid[:, ds(i * 2 + s, 1), h * 512:(h + 1) * 512],
                                                  ps[4 * s + h][:, :].unsqueeze(1), ACT.Silu)
                        last.then_inc(gate[s], 1)
                for t in range(NT):
                    if t % GRP == 0:
                        act.wait_ge(down, KF * (t // GRP + 1))
                    for h in range(2):
                        last = act.activation(junk[:, h, 0:512], ps[2 * (t % GRP) + h][:, :], ACT.Square, accum_out=st[:, h, t:t + 1])
                    act.drain()
                    act.sem_inc(sq, 1)
                    act.wait_ge(var, 2 * t + 2)
                    act.activation(st[:, 3, t:t + 1], st[:, 2, t:t + 1], ACT.Sqrt).then_inc(rt, 1)

            @block.vector
            def _(dve):
                for s in range(2):
                    dve.sem_inc(up[s], 1)
                with dve.Fori(0, KF // 2) as i:
                    for s in range(2):
                        dve.wait_ge(gate[s], i + 2)
                        for h in range(2):
                            m = mid[:, ds(i * 2 + s, 1), h * 512:(h + 1) * 512]
                            last = dve.tensor_tensor(m, m, ps[4 * s + 2 + h][:, :].unsqueeze(1), ALU.mult)
                        last.then_inc(up[s], 1)
                for t in range(NT):
                    dve.wait_ge(sq, t + 1)
                    dve.tensor_tensor(st[:, 2, t:t + 1], st[:, 0, t:t + 1], st[:, 1, t:t + 1], ALU.add).then_inc(var, 1)
                    dve.wait_ge(var, 2 * t + 1)
                    dve.tensor_scalar(st[:, 2, t:t + 1], st[:, 2, t:t + 1], 1.0 / D, EPS, ALU.mult, ALU.add).then_inc(var, 1)
                    dve.wait_ge(rt, t + 1)
                    dve.reciprocal(st[:, 3, t:t + 1], st[:, 3, t:t + 1]).then_inc(inv, 1)
                    dve.wait_ge(inv, t + 1)
                    if t >= 2:
                        dve.wait_ge(scl, t - 1)
                    for h in range(2):
                        last = dve.scalar_tensor_tensor(out=T[:, t % 2, h * 512:(h + 1) * 512], in0=ps[2 * (t % GRP) + h][:, :],
                                                        scalar=st[:, 3, t:t + 1], in1=K.G2[:, h * 512:(h + 1) * 512], op0=ALU.mult, op1=ALU.mult)
                    last.then_inc(fin, 1)

            @block.gpsimd
            def _(pool):
                for t in range(NT):
                    pool.wait_ge(fin, t + 1)
                    pool.tensor_tensor(X[:, t, :], X[:, t, :], T[:, t % 2, :], ALU.add).then_inc(scl, 1)


def first_block(nc, K, A):
    with ExitStack() as ctx:
        def sb(n, s, d=F32):
            return ctx.enter_context(nc.sbuf_tensor(n, s, d))

        K.G1, K.G2 = sb("G1", [P, D]), sb("G2", [P, D])
        modulation(nc, K, A)

        def load(t):
            return A["x"][0, t * P:(t + 1) * P, :] if t < NT else A["ctx"][0, (t - NT) * P:(t - NT + 1) * P, :]

        rms_to_feature_major(nc, K, "pre", K.XC, K.XC, [(0, NT, K.HT, K.A1, K.B1), (NT, NTC, K.HTc, K.A1c, K.B1c)], load)
        with ExitStack() as ssd_ctx:
            def sb2(n, s, d=F32):
                return ssd_ctx.enter_context(nc.sbuf_tensor(n, s, d))

            K.XF, K.XFc = sb2("XF", [P, NCV, L]), sb2("XFc", [P, 10, LC])
            K.dtr, K.dtb, K.alog, K.dskip = sb2("dtr", [P, NT + NTC, 24]), sb2("dtb", [P, 24]), sb2("alog", [P, 24]), sb2("dskip", [P, NH])
            projections(nc, K, A)
            ssd(nc, K, A)
            mixer_output(nc, K, A)
        with nc.sbuf_tensor("ffn_norm", [P, NT, D], F32) as xn:
            rms_to_feature_major(nc, K, "ffn", K.X, xn, [(0, NT, K.HT, K.A2, K.B2)])
        swiglu(nc, K, A)


def layer_norm(nc, K, A, tag, i, j, store, transpose=True, combine=False, router=None):
    X, HT, ps = K.X, K.HT, K.ps
    NR = 8 + NE
    with ExitStack() as ctx:
        def sb(n, s, d=F32):
            return ctx.enter_context(nc.sbuf_tensor(tag + n, s, d))

        g, b = sb("g", [P, D]), sb("b", [P, D])
        stats = sb("stats", [P, NT, 2, 6])
        mv = sb("mv", [P, NT, 2])
        sd, nm = sb("sd", [P, NT]), sb("nm", [P, NT])
        NY = 3
        y = sb("y", [P, NY, 2, D]) if combine else None
        wr = sb("wr", [P, KD, NR]) if router is not None else None
        gb_in, var, root, rstd, normed, scaled, bd, stored, tr, ev, g0, used, wr_in, lg = (K.sem(tag + n) for n in (
            "gb_in", "var", "root", "rstd", "normed", "scaled", "bd", "stored", "tr", "ev", "g0", "used", "wr_in", "lg"))
        y_in = [K.sem(tag + f"y_in{s}") for s in range(NY)]

        with nc.Block() as block:
            @block.sync
            def _(sp):
                if combine:
                    src = K.yrow.rearrange("(t p c) n -> t p c n", p=P, c=2)
                    for t in range(NY):
                        sp.dma_start(y[:, t], src[t]).then_inc(y_in[t], 16)
                sp.dma_start(g[:, :], A["ln_g_2"][i, j:j + 1, :].to_broadcast([P, D])).then_inc(gb_in, 16)
                sp.dma_start(b[:, :], A["ln_b_2"][i, j:j + 1, :].to_broadcast([P, D])).then_inc(gb_in, 16)
                if router is not None:
                    sp.dma_start(wr[:, :, 0:8], A["moe_w_grp_2"][router].rearrange("(k p) n -> p k n", p=P)).then_inc(wr_in, 16)
                    sp.dma_start(wr[:, :, 8:NR], A["moe_w_exp_2"][router].rearrange("(k p) n -> p k n", p=P)).then_inc(wr_in, 16)
                for t in range(NT):
                    if combine and t + NY < NT:
                        sp.wait_ge(used, t + 1)
                        sp.dma_start(y[:, t % NY], src[t + NY]).then_inc(y_in[t % NY], 16)
                    if store is not None and t >= 2:
                        sp.wait_ge(bd, t - 1)
                        sp.dma_start(store[(t - 2) * P:(t - 1) * P, :], X[:, t - 2, :]).then_inc(stored, 16)
                if store is not None:
                    for t in range(NT - 2, NT):
                        sp.wait_ge(bd, t + 1)
                        sp.dma_start(store[t * P:(t + 1) * P, :], X[:, t, :]).then_inc(stored, 16)
                    sp.wait_ge(stored, 16 * NT)

            @block.vector
            def _(dve):
                def moments(t):
                    if combine:
                        dve.wait_ge(g0, t + 1)
                        dve.scalar_tensor_tensor(out=X[:, t, :], in0=X[:, t, :], scalar=ALPHA, in1=y[:, t % NY, 0, :], op0=ALU.mult, op1=ALU.add)
                        dve.drain()
                        dve.scalar_tensor_tensor(out=X[:, t, :], in0=y[:, t % NY, 1, :], scalar=K.GT[:, 1, t:t + 1], in1=X[:, t, :],
                                                 op0=ALU.mult, op1=ALU.add).then_inc(used, 1)
                        dve.drain()
                    for h in range(2):
                        dve.bn_stats(stats[:, t, h, :], X[:, t, h * 512:(h + 1) * 512])
                    dve.drain()
                    dve.bn_aggr(mv[:, t, :], stats[:, t, :, :].rearrange("p h c -> p (h c)"))
                    dve.drain()
                    dve.tensor_single_scalar(mv[:, t, 1:2], mv[:, t, 1:2], LN_EPS, ALU.add).then_inc(var, 1)

                def reciprocal(t):
                    dve.wait_ge(root, t + 1)
                    dve.reciprocal(sd[:, t:t + 1], sd[:, t:t + 1])
                    dve.drain()
                    dve.scalar_tensor_tensor(out=nm[:, t:t + 1], in0=mv[:, t, 0:1], scalar=-1.0, in1=sd[:, t:t + 1], op0=ALU.mult, op1=ALU.mult).then_inc(rstd, 1)

                def add_bias(t):
                    dve.wait_ge(scaled, t + 1)
                    dve.tensor_tensor(X[:, t, :], X[:, t, :], b[:, :], ALU.add).then_inc(bd, 1)

                for t in range(NT + 2):
                    if t < NT:
                        moments(t)
                    if 1 <= t <= NT:
                        reciprocal(t - 1)
                    if t == 2:
                        dve.wait_ge(gb_in, 32)
                    if t >= 2:
                        add_bias(t - 2)

            @block.gpsimd
            def _(pool):
                pool.wait_ge(gb_in, 32)
                for t in range(NT):
                    pool.wait_ge(normed, t + 1)
                    pool.tensor_tensor(X[:, t, :], X[:, t, :], g[:, :], ALU.mult).then_inc(scaled, 1)

            @block.scalar
            def _(act):
                def copy_turned(t):
                    for h in range(2):
                        n = 2 * t + h
                        act.wait_ge(tr, n + 1)
                        act.activation(HT[:, 4 * h:4 * h + 4, t * P:(t + 1) * P], ps[n % 4][:, :].rearrange("p (k q) -> p k q", q=P), ACT.Copy).then_inc(ev, 1)

                def gate(t):
                    act.wait_ge(y_in[t % NY], 16 * (t // NY + 1))
                    act.activation(y[:, t % NY, 0, :], y[:, t % NY, 0, :], ACT.Identity, scale=K.GT[:, 0, t:t + 1], bias=0.0).then_inc(g0, 1)

                if combine:
                    gate(0)
                for t in range(NT + 3):
                    if combine and t + 1 < NT:
                        gate(t + 1)
                    if t < NT:
                        act.wait_ge(var, t + 1)
                        act.activation(sd[:, t:t + 1], mv[:, t, 1:2], ACT.Sqrt).then_inc(root, 1)
                    if 1 <= t <= NT:
                        u = t - 1
                        act.wait_ge(rstd, u + 1)
                        act.activation(X[:, u, :], X[:, u, :], ACT.Identity, scale=sd[:, u:u + 1], bias=nm[:, u:u + 1]).then_inc(normed, 1)
                    if transpose and t >= 3:
                        copy_turned(t - 3)

            @block.tensor
            def _(pe):
                def logits(t):
                    if t == 0:
                        pe.wait_ge(wr_in, 32)
                    pe.wait_ge(ev, 2 * t + 2)
                    for k in range(KD):
                        last = pe.matmul(ps[4 + t // 4][:, (t % 4) * NR:(t % 4 + 1) * NR], HT[:, k, t * P:(t + 1) * P], wr[:, k, :],
                                         start=k == 0, stop=k == KD - 1)
                    last.then_inc(lg, 1)

                if transpose:
                    for t in range(NT):
                        pe.wait_ge(bd, t + 1)
                        if t >= 2:
                            pe.wait_ge(ev, 2 * t - 2)
                        for h in range(2):
                            for k in range(4):
                                last = pe.transpose(ps[(2 * t + h) % 4][:, k * P:(k + 1) * P], X[:, t, (4 * h + k) * P:(4 * h + k + 1) * P], K.cst[:, C_ID:C_ID + P])
                            last.then_inc(tr, 1)
                        if router is not None and t >= 1:
                            logits(t - 1)
                    if router is not None:
                        logits(NT - 1)


def latents(nc, K, A):
    X, HT, ps, cst = K.X, K.HT, K.ps, K.cst
    ident = cst[:, C_ID:C_ID + P]
    TWO_PI_HI = 6.28125
    TWO_PI_LO = 2 * np.pi - TWO_PI_HI
    PI = 3.1415925
    with ExitStack() as ctx:
        def sb(n, s, d=F32):
            return ctx.enter_context(nc.sbuf_tensor("la_" + n, s, d))

        w = sb("w", [P, KD, LAT])
        lat = sb("lat", [P, NT, LAT])
        T3, KR = sb("T3", [P, NT, P]), sb("KR", [P, NT, P])
        junk = sb("junk", [P, QL])
        ss = sb("ss", [P, 2, NT])
        posr, posi = sb("posr", [NT, P]), sb("posi", [NT, P], I32)
        pos = sb("pos", [P, NT])
        ang, turn, co, si, tm = (sb(n, [P, NT, 16]) for n in ("ang", "turn", "co", "si", "tm"))
        ki = sb("ki", [P, NT, 16], I32)
        (w_in, p_in, pr, tr0, ev0, mm, ev, sq, var, rt, rc, nm, rope, sins, tr, eva, evv, vmm, ve, one) = (K.sem("la_" + n) for n in (
            "w_in", "p_in", "pr", "tr0", "ev0", "mm", "ev", "sq", "var", "rt", "rc", "nm", "rope", "sins", "tr", "eva", "evv", "vmm", "ve", "one"))
        src = [(lat, 0), (lat, P), (lat, QL), (KR, 0), (T3, 0)]

        with nc.Block() as block:
            @block.sync
            def _(sp):
                sp.dma_start(posi[:, :], A["positions_2"][0].rearrange("(a p) -> a p", p=P)).then_inc(p_in, 16)
                sp.dma_start(w[:, :, :], A["mla_w_in_2"][0].rearrange("(k p) n -> p k n", p=P)).then_inc(w_in, 16)
                sp.dma_start(K.WKV[:, :, :], A["mla_w_ukv_2"][0].rearrange("p (h n) -> p h n", n=P)).then_inc(w_in, 16)

            @block.tensor
            def _(pe):
                for n in range(2 * NT):
                    t, h = n // 2, n % 2
                    if n >= 4:
                        pe.wait_ge(ev0, n - 3)
                    for k in range(4):
                        last = pe.transpose(ps[n % 4][:, k * P:(k + 1) * P], X[:, t, (4 * h + k) * P:(4 * h + k + 1) * P], ident)
                    last.then_inc(tr0, 1)
                pe.wait_ge(pr, 1)
                pe.transpose(ps[6][:, 0:NT], posr[:, :], ident[0:NT, 0:NT]).then_inc(pr, 1)
                pe.wait_ge(w_in, 32)
                for t in range(NT):
                    pe.wait_ge(ev0, 2 * t + 2)
                    if t >= 2:
                        pe.wait_ge(ev, t - 1)
                    for k in range(KD):
                        last = pe.matmul(ps[4 + t % 2][:, 0:LAT], HT[:, k, t * P:(t + 1) * P], w[:, k, :], start=k == 0, stop=k == KD - 1)
                    last.then_inc(mm, 1)
                pe.wait_ge(nm, 2)
                pe.wait_ge(rope, 1)
                for n in range(10):
                    s, c = src[n // 2]
                    if n >= 4:
                        pe.wait_ge(eva if n % 2 == 0 else evv, (n - 4) // 2 + 1)
                    for i in range(4):
                        last = pe.transpose(ps[n % 4][:, i * P:(i + 1) * P], s[:, 4 * (n % 2) + i, c:c + P], ident)
                    last.then_inc(tr, 1)
                pe.wait_ge(eva, 5)
                pe.wait_ge(evv, 5)
                for n in range(2 * NT):
                    t, h = n // 2, n % 2
                    if n >= 4:
                        pe.wait_ge(ve, n - 3)
                    pe.matmul(ps[4 + n % 4][:, :], K.CKV[:, t * P:(t + 1) * P], K.WKV[:, 8 * h:8 * h + 8, 64:P],
                              start=True, stop=True).then_inc(vmm, 1)

            @block.scalar
            def _(act):
                for n in range(2 * NT):
                    t, h = n // 2, n % 2
                    act.wait_ge(tr0, n + 1)
                    act.activation(HT[:, 4 * h:4 * h + 4, t * P:(t + 1) * P], ps[n % 4][:, :].rearrange("p (k q) -> p k q", q=P), ACT.Copy).then_inc(ev0, 1)
                for t in range(NT):
                    act.wait_ge(mm, t + 1)
                    act.activation(lat[:, t, :], ps[4 + t % 2][:, 0:LAT], ACT.Copy).then_inc(ev, 1)
                    act.drain()
                    act.activation(junk[:, :], lat[:, t, 0:QL], ACT.Square, accum_out=ss[:, 0, t:t + 1])
                    act.drain()
                    act.activation(junk[:, 0:KVL], lat[:, t, QL:QL + KVL], ACT.Square, accum_out=ss[:, 1, t:t + 1]).then_inc(sq, 1)
                    act.drain()
                act.wait_ge(var, 1)
                act.activation(ss[:, :, :], ss[:, :, :], ACT.Sqrt).then_inc(rt, 1)
                act.wait_ge(sins, 1)
                act.activation(si[:, :, :], si[:, :, :], ACT.Sin)
                act.activation(co[:, :, :], co[:, :, :], ACT.Sin).then_inc(sins, 1)
                scales = [K.cols[:, COL_QN:COL_QN + 1], K.cols[:, COL_QN + 1:COL_QN + 2], K.cols[:, COL_KVN:COL_KVN + 1]]
                for n in range(0, 10, 2):
                    act.wait_ge(tr, n + 1)
                    f = n // 2
                    if f < 3:
                        dst = K.CQ[:, f, 0:512] if f < 2 else K.CKV[:, 0:512]
                        act.activation(dst, ps[n % 4][:, :], ACT.Identity, scale=scales[f], bias=0.0).then_inc(eva, 1)
                    elif f == 3:
                        act.activation(K.KT[64:P, 0:512], ps[n % 4][64:P, :], ACT.Copy).then_inc(eva, 1)
                    else:
                        act.activation(K.CS[:, 0:512], ps[n % 4][:, :], ACT.Copy).then_inc(eva, 1)
                for n in range(2 * NT):
                    act.wait_ge(vmm, n + 1)
                    act.activation(K.VV[:, n // 2, (n % 2) * 512:(n % 2) * 512 + 512], ps[4 + n % 4][:, :], ACT.Copy).then_inc(ve, 1)

            @block.gpsimd
            def _(pool):
                pool.memset(T3[:, :, 0:64], SCALE)
                pool.memset(KR[:, :, 0:64], 0.0).then_inc(one, 1)

            @block.vector
            def _(dve):
                f16 = [P, NT, 16]
                dve.wait_ge(p_in, 16)
                dve.tensor_copy(posr[:, :], posi[:, :]).then_inc(pr, 1)
                dve.wait_ge(pr, 2)
                dve.tensor_copy(pos[:, :], ps[6][:, 0:NT])
                dve.drain()
                dve.tensor_tensor(ang[:, :, :], pos[:, :].unsqueeze(2).to_broadcast(f16), cst[:, C_FREQ:C_FREQ + 16].unsqueeze(1).to_broadcast(f16), ALU.mult)
                dve.drain()
                dve.tensor_single_scalar(turn[:, :, :], ang[:, :, :], 1 / (2 * np.pi), ALU.mult)
                dve.drain()
                dve.tensor_copy(ki[:, :, :], turn[:, :, :])
                dve.drain()
                dve.tensor_copy(turn[:, :, :], ki[:, :, :])
                dve.drain()
                for part in (TWO_PI_HI, TWO_PI_LO):
                    dve.scalar_tensor_tensor(out=ang[:, :, :], in0=turn[:, :, :], scalar=-part, in1=ang[:, :, :], op0=ALU.mult, op1=ALU.add)
                    dve.drain()
                dve.tensor_scalar(si[:, :, :], ang[:, :, :], PI, -PI, ALU.min, ALU.max)
                dve.tensor_single_scalar(co[:, :, :], ang[:, :, :], np.pi / 2, ALU.add)
                dve.drain()
                dve.tensor_scalar(tm[:, :, :], co[:, :, :], PI, 2 * np.pi, ALU.is_gt, ALU.mult)
                dve.drain()
                dve.tensor_tensor(co[:, :, :], co[:, :, :], tm[:, :, :], ALU.subtract)
                dve.drain()
                dve.tensor_scalar(co[:, :, :], co[:, :, :], PI, -PI, ALU.min, ALU.max).then_inc(sins, 1)
                dve.wait_ge(sq, NT)
                dve.tensor_scalar(ss[:, 0, :], ss[:, 0, :], 1.0 / QL, EPS, ALU.mult, ALU.add)
                dve.tensor_scalar(ss[:, 1, :], ss[:, 1, :], 1.0 / KVL, EPS, ALU.mult, ALU.add).then_inc(var, 1)
                dve.wait_ge(rt, 1)
                dve.reciprocal(ss[:, :, :], ss[:, :, :]).then_inc(rc, 1)
                dve.wait_ge(rc, 1)
                dve.tensor_tensor(lat[:, :, 0:QL], lat[:, :, 0:QL], ss[:, 0, :].unsqueeze(2).to_broadcast([P, NT, QL]), ALU.mult).then_inc(nm, 1)
                dve.tensor_tensor(lat[:, :, QL:QL + KVL], lat[:, :, QL:QL + KVL], ss[:, 1, :].unsqueeze(2).to_broadcast([P, NT, KVL]), ALU.mult).then_inc(nm, 1)
                dve.wait_ge(sins, 2)
                dve.wait_ge(one, 1)
                x1, x2 = lat[:, :, QL + KVL:QL + KVL + 16], lat[:, :, QL + KVL + 16:LAT]
                dve.tensor_tensor(KR[:, :, 64:80], x1, co[:, :, :], ALU.mult)
                dve.tensor_tensor(KR[:, :, 80:96], x2, co[:, :, :], ALU.mult)
                dve.tensor_tensor(tm[:, :, :], x2, si[:, :, :], ALU.mult)
                dve.tensor_tensor(ang[:, :, :], x1, si[:, :, :], ALU.mult)
                dve.drain()
                dve.tensor_tensor(KR[:, :, 64:80], KR[:, :, 64:80], tm[:, :, :], ALU.subtract)
                dve.tensor_tensor(KR[:, :, 80:96], KR[:, :, 80:96], ang[:, :, :], ALU.add)
                dve.drain()
                dve.tensor_copy(KR[:, :, 96:128], KR[:, :, 64:96])
                for r in range(2):
                    dve.tensor_single_scalar(T3[:, :, 64 + 16 * r:80 + 16 * r], co[:, :, :], SCALE, ALU.mult)
                    last = dve.tensor_single_scalar(T3[:, :, 96 + 16 * r:112 + 16 * r], si[:, :, :], SCALE, ALU.mult)
                last.then_inc(rope, 1)
                for n in range(1, 10, 2):
                    dve.wait_ge(tr, n + 1)
                    f = n // 2
                    if f < 3:
                        dst = K.CQ[:, f, 512:1024] if f < 2 else K.CKV[:, 512:1024]
                        c = COL_QN + f if f < 2 else COL_KVN
                        dve.tensor_scalar(dst, ps[n % 4][:, :], K.cols[:, c:c + 1], None, ALU.mult).then_inc(evv, 1)
                    elif f == 3:
                        dve.tensor_copy(K.KT[64:P, 512:1024], ps[n % 4][64:P, :]).then_inc(evv, 1)
                    else:
                        dve.tensor_copy(K.CS[:, 512:1024], ps[n % 4][:, :]).then_inc(evv, 1)


def attention(nc, K, A):
    ps, cst = K.ps, K.cst
    ident = cst[:, C_ID:C_ID + P]
    OT = K.HT
    cT = [2, 4, 6, 8, 9, 10, 11, 12]
    with ExitStack() as ctx:
        def sb(n, s, d=F32):
            return ctx.enter_context(nc.sbuf_tensor("at_" + n, s, d))

        wq = [sb(f"wq{s}", [P, 2, P]) for s in range(2)]
        wk = [sb(f"wk{s}", [P, 64]) for s in range(2)]
        QT = sb("QT", [P, L])
        zero = sb("zero", [P, 2, 16])
        mask = sb("mask", [P, 2, P], mybir.dt.bfloat16)
        m_ok = K.sem("at_mask")
        PR = [sb(f"PR{i}", [P, L]) for i in range(2)]
        PT = [sb(f"PT{i}", [P, L]) for i in range(2)]
        mxc, nmx, sums, rs = (sb(n, [P, NT]) for n in ("mxc", "nmx", "sums", "rs"))
        w_in = [K.sem(f"at_w{s}") for s in range(2)]
        w_ok = [K.sem(f"at_wok{s}") for s in range(2)]
        item, q_ev, k_ev, mx, ex, tT, tv, ta, pv, ov = (K.sem("at_" + n) for n in ("item", "qev", "kev", "mx", "ex", "tT", "tv", "ta", "pv", "ov"))
        wuq = A["mla_w_uq_2"][0].rearrange("(k p) n -> p k n", p=P)
        wukv = A["mla_w_ukv_2"][0]

        def pair(j):
            return K.psum[:, 2 * (j % 2):2 * (j % 2) + 2, :].rearrange("p b n -> p (b n)")

        with nc.Block() as block:
            @block.sync
            def _(sp):
                sp.dma_start(K.WO[:, :, :], A["mla_w_o_2"][0].rearrange("(k p) n -> p k n", p=P)).then_inc(K.wo_in, 16)
                with sp.Fori(0, AH // 2) as i:
                    for s in range(2):
                        sp.wait_ge(k_ev, i * 2 + s + 1)
                        sp.dma_start(wq[s][:, :, 0:96], wuq[:, :, ds((i * 2 + s) * 96, 96)]).then_inc(w_in[s], 16)
                        sp.dma_start(wk[s][:, :], wukv[:, ds((i * 2 + s) * P, 64)]).then_inc(w_in[s], 16)

            @block.gpsimd
            def _(pool):
                pool.memset(zero[:, :, :], 0.0)
                pool.drain()
                with pool.Fori(0, AH // 2) as i:
                    for s in range(2):
                        pool.wait_ge(w_in[s], i * 32 + 32)
                        pool.tensor_tensor(wq[s][:, :, 96:112], zero[:, :, :], wq[s][:, :, 80:96], ALU.subtract)
                        pool.tensor_copy(wq[s][:, :, 112:128], wq[s][:, :, 64:80]).then_inc(w_ok[s], 1)

            @block.tensor
            def _(pe):
                pe.sem_inc(tT, 12)
                pe.sem_inc(pv, 8)

                def queries(h, s, i):
                    pe.wait_ge(w_ok[s], i + 1)
                    pe.wait_ge(ex, h * 8 + 7)
                    for c in range(2):
                        for k in range(2):
                            last = pe.matmul(ps[c][:, :], wq[s][:, k, :], K.CQ[:, k, c * 512:(c + 1) * 512], start=k == 0, stop=k == 1)
                    last.then_inc(item, 1)

                def keys(h, s):
                    pe.wait_ge(ex, h * 8 + 8)
                    for c in range(2):
                        last = pe.matmul(ps[2 + c][0:64, :], wk[s][:, :], K.CKV[:, c * 512:(c + 1) * 512], start=True, stop=True)
                    last.then_inc(item, 1)

                def scores(h, j):
                    t = NT - 1 - j
                    if j == 0:
                        pe.wait_ge(q_ev, h + 1)
                        pe.wait_ge(k_ev, h + 3)
                    elif j >= 2:
                        pe.wait_ge(ex, h * 8 + (j - 1 + 8))
                    q = QT[:, t * P:(t + 1) * P]
                    n = (t + 1) * P
                    S = pair(j)
                    for c in range(0, t * P, 512):
                        e = min(c + 512, t * P)
                        pe.matmul(S[:, c:e], q, K.KT[:, c:e], start=True, stop=True)
                    pe.matmul(S[:, t * P:n], q, K.KT[:, t * P:n], start=True, stop=False)
                    pe.matmul(S[:, t * P:n], mask[:, 0, :], mask[:, 1, :], start=False, stop=True).then_inc(item, 1)

                def turn(h, j):
                    t = NT - 1 - j
                    pe.wait_ge(ex, h * 8 + (j + 9))
                    for b in range(0, t + 1, 4):
                        if b == 0:
                            pe.wait_ge(tv, h * 8 + (j + 8))
                        else:
                            pe.wait_ge(ta, h * 4 + (j + 4))
                        for k in range(b, min(b + 4, t + 1)):
                            last = pe.transpose(ps[4 + b // 4][:, (k - b) * P:(k - b + 1) * P], PR[j % 2][:, k * P:(k + 1) * P], ident)
                        last.then_inc(tT, 1)

                def apply(h, j):
                    t = NT - 1 - j
                    pe.wait_ge(tv, h * 8 + (j + 9))
                    if t >= 4:
                        pe.wait_ge(ta, h * 4 + (j + 5))
                    pe.wait_ge(ov, h * 8 + (j - 1 + 8))
                    for k in range(t + 1):
                        last = pe.matmul(ps[6 + j % 2][:, 0:64], PT[j % 2][:, k * P:(k + 1) * P], K.VV[:, k, ds(h * 64, 64)],
                                         start=k == 0, stop=k == t)
                    last.then_inc(pv, 1)

                def head(h, s, i, more=True):
                    for j in range(NT + 2):
                        if j < NT:
                            scores(h, j)
                        elif more and j == NT:
                            queries(h + 1, (s + 1) % 2, i + s)
                        elif more:
                            keys(h + 1, (s + 1) % 2)
                        if 1 <= j <= NT:
                            turn(h, j - 1)
                        if j >= 2:
                            apply(h, j - 2)

                pe.wait_ge(m_ok, 1)
                queries(0, 0, 0)
                keys(0, 0)
                with pe.Fori(0, AH // 2 - 1) as i:
                    for s in range(2):
                        head(i * 2 + s, s, i)
                for s in range(2):
                    head(AH - 2 + s, s, AH // 2 - 1, s == 0)

            @block.scalar
            def _(act):
                act.sem_inc(k_ev, 2)
                act.sem_inc(ex, 8)
                act.sem_inc(ta, 4)

                def head(h):
                    act.wait_ge(item, h * 10 + 2)
                    act.activation(K.KT[0:64, :], pair(1)[0:64, :], ACT.Identity, bias=0.0).then_inc(k_ev, 1)

                    def weights(j):
                        act.wait_ge(mx, h * 8 + (j + 1))
                        act.wait_ge(tT, h * 12 + (cT[j - 2] + 12 if j >= 2 else cT[6 + j]))
                        t = NT - 1 - j
                        n = (t + 1) * P
                        act.activation(PR[j % 2][:, 0:n], pair(j)[:, 0:n], ACT.Exp, bias=nmx[:, t:t + 1], accum_out=sums[:, t:t + 1])
                        act.drain()
                        act.sem_inc(ex, 1)

                    def copy_turned(j):
                        act.wait_ge(tT, h * 12 + (cT[j] + 12))
                        act.wait_ge(pv, h * 8 + (j - 1 + 8))
                        act.activation(PT[j % 2][:, 512:(NT - j) * P], ps[5][:, 0:(4 - j) * P], ACT.Identity, bias=0.0).then_inc(ta, 1)

                    weights(0)
                    for j in range(NT):
                        if j + 1 < NT:
                            weights(j + 1)
                        if j < 4:
                            copy_turned(j)

                with act.Fori(0, AH) as h:
                    head(h)

            @block.vector
            def _(dve):
                dve.tensor_copy(mask[:, 0, :], ident)
                dve.tensor_copy(mask[:, 1, :], cst[:, C_NEG:C_NEG + P]).then_inc(m_ok, 1)
                dve.sem_inc(tv, 8)
                dve.sem_inc(ov, 8)

                def queries(h):
                    dve.wait_ge(item, h * 10 + 1)
                    dve.tensor_tensor(QT[:, :], pair(0), K.CS[:, :], ALU.mult).then_inc(q_ev, 1)

                def row_max(h, j):
                    t = NT - 1 - j
                    dve.wait_ge(item, h * 10 + (j + 3))
                    dve.tensor_reduce(mxc[:, t:t + 1], pair(j)[:, 0:(t + 1) * P], AX.X, ALU.max)
                    dve.drain()
                    dve.tensor_single_scalar(nmx[:, t:t + 1], mxc[:, t:t + 1], -1.0, ALU.mult).then_inc(mx, 1)

                def copy_turned(h, j):
                    t = NT - 1 - j
                    n = min(t + 1, 4) * P
                    dve.wait_ge(tT, h * 12 + (cT[j] + 12 - (1 if t >= 4 else 0)))
                    dve.wait_ge(pv, h * 8 + (j - 1 + 8))
                    dve.tensor_copy(PT[j % 2][:, 0:n], ps[4][:, 0:n]).then_inc(tv, 1)
                    dve.reciprocal(rs[:, t:t + 1], sums[:, t:t + 1])

                def output(h, j):
                    t = NT - 1 - j
                    dve.wait_ge(pv, h * 8 + (j + 9))
                    dve.tensor_scalar(OT[:, t, ds(h * 64, 64)], ps[6 + j % 2][:, 0:64], rs[:, t:t + 1], None, ALU.mult).then_inc(ov, 1)

                def head(h, more=True):
                    for j in range(NT + 1):
                        if j < NT:
                            row_max(h, j)
                        elif more:
                            queries(h + 1)
                        if j >= 3:
                            output(h, j - 3)
                        if j >= 1:
                            copy_turned(h, j - 1)
                    dve.drain()
                    output(h, NT - 2)
                    output(h, NT - 1)

                queries(0)
                with dve.Fori(0, AH - 1) as h:
                    head(h)
                head(AH - 1, False)


def attention_output(nc, K, A):
    O, X, ps = K.HT, K.X, K.ps
    OF = K.VV
    with ExitStack() as ctx:
        tr, ev, mm, done = (K.sem("ao_" + n) for n in ("tr", "ev", "mm", "done"))
        with nc.Block() as block:
            @block.tensor
            def _(pe):
                for n in range(2 * NT):
                    t, h = n // 2, n % 2
                    if n >= 4:
                        pe.wait_ge(ev, n - 3)
                    for k in range(4):
                        last = pe.transpose(ps[n % 4][:, k * P:(k + 1) * P], O[:, t, (4 * h + k) * P:(4 * h + k + 1) * P], K.cst[:, C_ID:C_ID + P])
                    last.then_inc(tr, 1)
                pe.wait_ge(K.wo_in, 16)
                for t in range(NT):
                    pe.wait_ge(ev, 2 * t + 2)
                    for h in range(2):
                        n = 2 * t + h
                        if n >= 4:
                            pe.wait_ge(done, n - 3)
                        for k in range(KD):
                            last = pe.matmul(ps[4 + n % 4][:, :], OF[:, k, t * P:(t + 1) * P], K.WO[:, k, h * 512:(h + 1) * 512],
                                             start=k == 0, stop=k == KD - 1)
                        last.then_inc(mm, 1)

            @block.scalar
            def _(act):
                for n in range(2 * NT):
                    t, h = n // 2, n % 2
                    act.wait_ge(tr, n + 1)
                    act.activation(OF[:, 4 * h:4 * h + 4, t * P:(t + 1) * P], ps[n % 4][:, :].rearrange("p (k q) -> p k q", q=P), ACT.Copy).then_inc(ev, 1)

            @block.vector
            def _(dve):
                for n in range(2 * NT):
                    x = X[:, n // 2, (n % 2) * 512:(n % 2) * 512 + 512]
                    dve.wait_ge(mm, n + 1)
                    dve.scalar_tensor_tensor(out=x, in0=x, scalar=ALPHA, in1=ps[4 + n % 4][:, :], op0=ALU.mult, op1=ALU.add).then_inc(done, 1)


def mla(nc, K, A):
    with ExitStack() as ctx:
        def sb(n, s, d=F32):
            return ctx.enter_context(nc.sbuf_tensor("mla_" + n, s, d))

        K.CQ, K.CKV, K.KT, K.CS = sb("CQ", [P, 2, L]), sb("CKV", [P, L]), sb("KT", [P, L]), sb("CS", [P, L])
        K.VV = sb("VV", [P, NT, D])
        K.wo_in = K.sem("mla_wo_in")
        with nc.sbuf_tensor("mla_WKV", [P, AH, P], F32) as K.WKV:
            latents(nc, K, A)
        K.WO = sb("WO", [P, KD, D])
        attention(nc, K, A)
        attention_output(nc, K, A)


def expert_weights(sp, K, A, layer, e, slot, sem):
    for j, name in enumerate(("moe_w1_2", "moe_w3_2")):
        src = A[name][layer][ds(e, 1)].rearrange("e (k p) n -> p (e k) n", p=P)
        sp.dma_start(K.W13[slot][:, :, j, :], src).then_inc(sem, 16)
    src = A["moe_w2_2"][layer][ds(e, 1)].rearrange("e (k p) n -> p (e k) n", p=P)
    sp.dma_start(K.W2[slot][:, :, :], src).then_inc(sem, 16)


def gather_buffers(K):
    return [K.hreg[:, i * D:(i + 1) * D] for i in range(2)]


def routing(nc, K, A, layer, tag):
    ps, cst = K.ps, K.cst
    NR = 8 + NE
    with ExitStack() as ctx:
        def sb(n, s, d=F32):
            return ctx.enter_context(nc.sbuf_tensor(tag + n, s, d))

        br = sb("br", [P, NR])
        LG = sb("LG", [P, NT, NR])
        g8, e8 = sb("g8", [P, NT, 8]), sb("e8", [P, NT, 8])
        gi, ei = sb("gi", [P, NT, 8], U32), sb("ei", [P, NT, 8], U32)
        gs, oh, xe, es = sb("gs", [P, NT]), sb("oh", [P, NT, 8]), sb("xe", [P, NT, 8]), sb("es", [P, NT, 8])
        big = sb("big", [P, 1024])
        ek, rk, ok_, sl, ge, r_, d_ = (sb(n, [P, 2, NT]) for n in ("ek", "rk", "ok", "sl", "ge", "r", "d"))
        Ak = [sb(f"A{k}", [P, NT, NE]) for k in range(2)]
        AS = sb("AS", [P, NT, NE], BF16)
        one64 = sb("one64", [P, NE])
        cnt, ov, oe, os_ = (sb(n, [P, NE]) for n in ("cnt", "ov", "oe", "os"))
        one, before = sb("one", [P, P], BF16), sb("before", [P, P], BF16)
        sli, rwi, bli = (sb(n, [P, 2, NT], I32) for n in ("sli", "rwi", "bli"))
        rwf, blf = sb("rwf", [P, 2, NT]), sb("blf", [P, 2, NT])
        RO = [sb(f"RO{i}", [P, P]) for i in range(4)]
        BO = [sb(f"BO{i}", [P, NB]) for i in range(4)]
        vt, v0 = sb("vt", [P, NB]), sb("v0", [P, NB])
        eo = sb("eo", [P, OVER])
        w_in, sub, exd, a_ok, rmm, oh_ok, tmm, ones_ok, vi = (K.sem(tag + n) for n in (
            "w_in", "sub", "exd", "a_ok", "rmm", "oh_ok", "tmm", "ones", "vi"))

        with nc.Block() as block:
            @block.sync
            def _(sp):
                sp.dma_start(br[:, 0:8], A["moe_b_grp_2"][layer:layer + 1, :].to_broadcast([P, 8])).then_inc(w_in, 16)
                sp.dma_start(br[:, 8:NR], A["moe_b_exp_2"][layer:layer + 1, :].to_broadcast([P, NE])).then_inc(w_in, 16)
                for s in range(4):
                    expert_weights(sp, K, A, layer, s, s, K.ew_in[s])

            @block.gpsimd
            def _(pool):
                pool.memset(one[:, :], 1.0)
                pool.tensor_copy(before[:, :], cst[:, C_SUP:C_SUP + P]).then_inc(ones_ok, 1)
                for xg in gather_buffers(K):
                    pool.memset(xg, 0.0)

            @block.tensor
            def _(pe):
                pe.wait_ge(a_ok, 1)
                pe.wait_ge(ones_ok, 1)
                pe.matmul(ps[2][:, :], before[:, :], AS[:, :, :], start=True, stop=False)
                for t in range(NT - 1):
                    pe.matmul(ps[2][:, (t + 1) * NE:NT * NE].rearrange("p (t e) -> p t e", e=NE), one[:, :],
                              AS[:, t:t + 1, :].to_broadcast([P, NT - 1 - t, NE]), start=False, stop=t == NT - 2)
                for t in range(NT):
                    last = pe.matmul(ps[3][:, 0:NE], one[:, :], AS[:, t, :], start=t == 0, stop=t == NT - 1)
                last.then_inc(rmm, 1)
                for n in range(2 * NT):
                    pe.wait_ge(oh_ok, n + 1)
                    pe.matmul(ps[6][:, 0:NB], RO[n % 4][:, :], BO[n % 4][:, :], start=n == 0, stop=n == 2 * NT - 1).then_inc(tmm, 1)

            @block.scalar
            def _(act):
                act.wait_ge(sub, 1)
                act.activation(xe[:, :, :], xe[:, :, :], ACT.Exp).then_inc(exd, 1)
                act.wait_ge(sub, 2)
                act.activation(r_[:, 0, :], r_[:, 0, :], ACT.Exp).then_inc(exd, 1)

            @block.vector
            def _(dve):
                def iota(n):
                    return cst[:, C_IOTA:C_IOTA + n]

                dve.memset(one64[:, :], 1.0)
                dve.wait_ge(w_in, 32)
                for h in range(2):
                    dve.tensor_tensor(LG[:, 4 * h:4 * h + 4, :], ps[4 + h][:, 0:4 * NR].rearrange("p (t n) -> p t n", n=NR),
                                      br[:, :].unsqueeze(1).to_broadcast([P, 4, NR]), ALU.add)
                dve.drain()
                for t in range(NT):
                    dve.max(g8[:, t, :], LG[:, t, 0:8])
                dve.drain()
                for t in range(NT):
                    dve.max_index(gi[:, t, :], g8[:, t, :], LG[:, t, 0:8])
                dve.tensor_tensor(xe[:, :, :], LG[:, :, 0:8], g8[:, :, 0:1].to_broadcast([P, NT, 8]), ALU.subtract).then_inc(sub, 1)
                dve.drain()
                dve.tensor_copy(gs[:, :], gi[:, :, 0])
                dve.drain()
                dve.tensor_tensor(oh[:, :, :], iota(8).unsqueeze(1).to_broadcast([P, NT, 8]), gs[:, :].unsqueeze(2).to_broadcast([P, NT, 8]), ALU.is_equal)
                dve.drain()
                for h in range(2):
                    ts = slice(4 * h, 4 * h + 4)
                    dve.tensor_tensor(big[:, h * 256:(h + 1) * 256].rearrange("p (t g j) -> p t g j", g=8, j=8), LG[:, ts, 8:NR].rearrange("p t (g j) -> p t g j", g=8),
                                      oh[:, ts, :].unsqueeze(3).to_broadcast([P, 4, 8, 8]), ALU.mult)
                dve.drain()
                dve.tensor_reduce(es[:, :, :], big[:, 0:512].rearrange("p (t g j) -> p t j g", g=8, j=8), AX.X, ALU.add)
                dve.drain()
                for t in range(NT):
                    dve.max(e8[:, t, :], es[:, t, :])
                dve.drain()
                for t in range(NT):
                    dve.max_index(ei[:, t, :], e8[:, t, :], es[:, t, :])
                dve.tensor_tensor(r_[:, 0, :], e8[:, :, 1], e8[:, :, 0], ALU.subtract).then_inc(sub, 1)
                dve.drain()
                dve.tensor_copy(ek[:, :, :], ei[:, :, 0:2].rearrange("p t k -> p k t"))
                dve.drain()
                for k in range(2):
                    dve.scalar_tensor_tensor(out=ek[:, k, :], in0=gs[:, :], scalar=8.0, in1=ek[:, k, :], op0=ALU.mult, op1=ALU.add)
                dve.drain()
                for k in range(2):
                    dve.tensor_tensor(Ak[k][:, :, :], iota(NE).unsqueeze(1).to_broadcast([P, NT, NE]), ek[:, k, :].unsqueeze(2).to_broadcast([P, NT, NE]), ALU.is_equal)
                dve.drain()
                dve.tensor_tensor(AS[:, :, :], Ak[0][:, :, :], Ak[1][:, :, :], ALU.add).then_inc(a_ok, 1)
                dve.wait_ge(exd, 2)
                dve.tensor_reduce(d_[:, 0, :], xe[:, :, :], AX.X, ALU.add)
                dve.tensor_single_scalar(d_[:, 1, :], r_[:, 0, :], 1.0, ALU.add)
                dve.drain()
                dve.tensor_tensor(d_[:, 0, :], d_[:, 0, :], d_[:, 1, :], ALU.mult)
                dve.drain()
                dve.reciprocal(K.GT[:, 0, :], d_[:, 0, :])
                dve.drain()
                dve.tensor_tensor(K.GT[:, 1, :], K.GT[:, 0, :], r_[:, 0, :], ALU.mult)
                dve.wait_ge(rmm, 1)
                dve.tensor_copy(cnt[:, :], ps[3][:, 0:NE])
                dve.drain()
                dve.tensor_tensor(big[:, 0:512].rearrange("p (e m) -> p e m", m=8), cnt[:, :].unsqueeze(2).to_broadcast([P, NE, 8]),
                                  cst[:, C_THR:C_THR + 8].unsqueeze(1).to_broadcast([P, NE, 8]), ALU.is_gt)
                dve.drain()
                dve.tensor_reduce(ov[:, :], big[:, 0:512].rearrange("p (e m) -> p e m", m=8), AX.X, ALU.add)
                dve.drain()
                dve.tensor_tensor_scan(oe[:, :], one64[:, :], ov[:, :], 0.0, ALU.mult, ALU.add)
                dve.drain()
                dve.tensor_tensor(os_[:, :], oe[:, :], ov[:, :], ALU.subtract)
                for k in range(2):
                    b3 = big[:, 0:512].rearrange("p (t e) -> p t e", e=NE)
                    dve.tensor_tensor(b3, Ak[k][:, :, :], ps[2][:, :].rearrange("p (t e) -> p t e", e=NE), ALU.mult)
                    dve.drain()
                    dve.tensor_reduce(rk[:, k, :], b3, AX.X, ALU.add)
                    dve.drain()
                    dve.tensor_tensor(b3, Ak[k][:, :, :], os_[:, :].unsqueeze(1).to_broadcast([P, NT, NE]), ALU.mult)
                    dve.drain()
                    dve.tensor_reduce(ok_[:, k, :], b3, AX.X, ALU.add)
                    dve.drain()
                dve.tensor_single_scalar(ek[:, :, :], ek[:, :, :], float(P), ALU.mult)
                dve.tensor_scalar(ok_[:, :, :], ok_[:, :, :], float(P), float((NE - 1) * P), ALU.mult, ALU.add)
                dve.tensor_single_scalar(ge[:, :, :], rk[:, :, :], float(P), ALU.is_ge)
                dve.drain()
                dve.tensor_tensor(ok_[:, :, :], ok_[:, :, :], ek[:, :, :], ALU.subtract)
                dve.tensor_tensor(sl[:, :, :], rk[:, :, :], ek[:, :, :], ALU.add)
                dve.drain()
                dve.tensor_tensor(ok_[:, :, :], ok_[:, :, :], ge[:, :, :], ALU.mult)
                dve.drain()
                dve.tensor_tensor(sl[:, :, :], sl[:, :, :], ok_[:, :, :], ALU.add)
                dve.drain()
                dve.tensor_copy(sli[:, :, :], sl[:, :, :])
                dve.drain()
                dve.tensor_single_scalar(rwi[:, :, :], sli[:, :, :], P - 1, ALU.bitwise_and)
                dve.tensor_single_scalar(bli[:, :, :], sli[:, :, :], 7, ALU.arith_shift_right)
                dve.drain()
                dve.tensor_copy(rwf[:, :, :], rwi[:, :, :])
                dve.tensor_copy(blf[:, :, :], bli[:, :, :])
                dve.drain()
                for n in range(2 * NT):
                    k, t = n // NT, n % NT
                    if n >= 4:
                        dve.wait_ge(tmm, n - 3)
                    dve.tensor_scalar(RO[n % 4][:, :], iota(P), rwf[:, k, t:t + 1], None, ALU.is_equal)
                    dve.tensor_scalar(BO[n % 4][:, :], iota(NB), blf[:, k, t:t + 1], cst[:, C_TOK + n:C_TOK + n + 1], ALU.is_equal, ALU.mult).then_inc(oh_ok, 1)
                dve.wait_ge(tmm, 2 * NT)
                dve.tensor_copy(vt[:, :], ps[6][:, 0:NB])
                dve.drain()
                dve.tensor_scalar(v0[:, :], vt[:, :], 0.5, 100000.0, ALU.is_lt, ALU.mult)
                dve.drain()
                dve.scalar_tensor_tensor(out=vt[:, :], in0=vt[:, :], scalar=-1.0, in1=v0[:, :], op0=ALU.add, op1=ALU.add)
                dve.drain()
                dve.tensor_copy(K.SIDX[:, :], vt[:, :])
                dve.drain()
                dve.tensor_single_scalar(K.GIDX[:, :], K.SIDX[:, :], 1, ALU.arith_shift_right)
                dve.tensor_tensor(big[:, :].rearrange("p (j e) -> p j e", e=NE), iota(OVER).unsqueeze(2).to_broadcast([P, OVER, NE]),
                                  oe[:, :].unsqueeze(1).to_broadcast([P, OVER, NE]), ALU.is_ge)
                dve.drain()
                dve.tensor_reduce(eo[:, :], big[:, :].rearrange("p (j e) -> p j e", e=NE), AX.X, ALU.add)
                dve.drain()
                dve.tensor_single_scalar(eo[:, :], eo[:, :], float(NE - 1), ALU.min)
                dve.drain()
                dve.tensor_copy(K.EO[:, 0:OVER], eo[:, :])
                dve.tensor_copy(K.EO[:, OVER:OVER + 1], oe[:, NE - 1:NE])


def experts(nc, K, A, layer, tag, first, count, w_in, w_base):
    ps, cst = K.ps, K.cst
    ident = cst[:, C_ID:C_ID + P]
    hr = K.hreg
    xg = gather_buffers(K)
    xT = [hr[:, (2 + i) * D:(3 + i) * D].rearrange("p (k r) -> p k r", r=P) for i in range(2)]
    ysb = [hr[:, (4 + i) * D:(5 + i) * D] for i in range(2)]
    sil = [hr[:, 6 * D + i * DE:6 * D + (i + 1) * DE] for i in range(2)]
    hb = [hr[:, 7 * D + i * DE:7 * D + (i + 1) * DE] for i in range(2)]
    hT = [hr[:, 8 * D + i * DE:8 * D + (i + 1) * DE].rearrange("p (k r) -> p k r", r=P) for i in range(2)]
    with ExitStack() as ctx:
        sgi = [ctx.enter_context(nc.sbuf_tensor(tag + f"gi{i}", [P, 1], I32)) for i in range(2)]
        ssi = [ctx.enter_context(nc.sbuf_tensor(tag + f"si{i}", [P, 1], I32)) for i in range(2)]
        scr = ctx.enter_context(nc.sbuf_tensor(tag + "scr", [P, 2], F32))
        ga = [K.sem(tag + f"ga{i}") for i in range(2)]
        sc = [K.sem(tag + f"sc{i}") for i in range(2)]
        (tx, txa, txv, hm, sild, hbd, th, thv, ym, ya, yv, zg, zs) = (K.sem(tag + n) for n in (
            "tx", "txa", "txv", "hm", "sild", "hbd", "th", "thv", "ym", "ya", "yv", "zg", "zs"))
        PEEL = 4

        def wait(eng, sem, b, n, least=0):
            if not isinstance(b, int) or b >= least:
                eng.wait_ge(sem, b + n)

        def every_block(eng, body):
            for b in range(PEEL):
                body(b, b % 4, b // 2, b // 4)
            with eng.Fori(1, count // 4 - 1) as i:
                for s in range(4):
                    body(i * 4 + s, s, i * 2 + s // 2, i)
            for b in range(count - PEEL, count):
                body(b, b % 4, b // 2, b // 4)

        with nc.Block() as block:
            @block.sync
            def _(sp):
                def load(b, s):
                    e = b if first == 0 else sp.value_load(K.EO[0:1, ds(b, 1)], min_val=0, max_val=NE - 1)
                    expert_weights(sp, K, A, layer, e, s, w_in[s])

                if first > 0:
                    for b in range(4):
                        load(b, b)
                with sp.Fori(1, count // 4) as i:
                    for s in range(4):
                        sp.wait_ge(ym, i * 4 + (s - 3))
                        load(i * 4 + s, s)

            @block.gpsimd
            def _(pool):
                if first > 0:
                    for i in range(2):
                        pool.memset(xg[i], 0.0)
                pool.memset(scr[:, :], 0.0)
                pool.drain()

                def carry_wait():
                    pool.tensor_tensor(scr[:, 0:1], scr[:, 1:2], scr[:, 1:2], ALU.add)

                def gather(b, p, half):
                    wait(pool, tx, b, -1, 2)
                    pool.tensor_copy(sgi[p][:, :], K.GIDX[:, ds(b + first, 1)]).then_inc(zg, 1)
                    pool.wait_ge(zg, b + 1)
                    carry_wait()
                    pool.indirect_dma_start(xg[p], None, K.xrow, bass.IndirectOffsetOnAxis(ap=sgi[p][:, :], axis=0),
                                            bounds_check=L - 1, oob_is_err=False).then_inc(ga[p], 16)

                def scatter(b, p, half):
                    if not isinstance(b, int) or b >= 2:
                        pool.wait_ge(sc[p], half * 16)
                    pool.wait_ge(ya, b + 1)
                    pool.wait_ge(yv, b + 1)
                    pool.tensor_copy(ssi[p][:, :], K.SIDX[:, ds(b + first, 1)]).then_inc(zs, 1)
                    pool.wait_ge(zs, b + 1)
                    carry_wait()
                    pool.indirect_dma_start(K.yrow, bass.IndirectOffsetOnAxis(ap=ssi[p][:, :], axis=0), ysb[p], None,
                                            bounds_check=2 * L - 1, oob_is_err=False).then_inc(sc[p], 16)

                for b in range(3):
                    gather(b, b % 2, b // 2)

                def body(b, s, half, quarter):
                    if not isinstance(b, int) or b < count - 3:
                        gather(b + 3, (s + 1) % 2, half + (1 + s % 2))
                    if not isinstance(b, int) or b >= 1:
                        scatter(b + (-1), (s + 1) % 2, half + (s % 2 - 1))

                every_block(pool, body)
                scatter(count - 1, 1, count // 2 - 1)
                for i in range(2):
                    pool.wait_ge(sc[i], 16 * count // 2)

            @block.tensor
            def _(pe):
                def turn_x(b, p, half):
                    pe.wait_ge(ga[p], half * 16 + 16)
                    wait(pe, txa, b, 0, 1)
                    wait(pe, txv, b, 0, 1)
                    for k in range(KD):
                        last = pe.transpose(ps[k // 4][:, (k % 4) * P:(k % 4 + 1) * P], xg[p][:, k * P:(k + 1) * P], ident)
                    last.then_inc(tx, 1)

                def first_product(b, s, quarter):
                    pe.wait_ge(w_in[s], quarter * 48 + w_base + 48)
                    pe.wait_ge(txa, b + 1)
                    pe.wait_ge(txv, b + 1)
                    wait(pe, hbd, b, -1, 2)
                    for k in range(KD):
                        last = pe.matmul(ps[2 + s % 2][:, :], xT[s % 2][:, k, :], K.W13[s][:, k, :, :], start=k == 0, stop=k == KD - 1)
                    last.then_inc(hm, 1)

                def turn_h(b, p):
                    pe.wait_ge(hbd, b + 1)
                    wait(pe, thv, b, 0, 1)
                    for k in range(2):
                        last = pe.transpose(ps[4][:, k * P:(k + 1) * P], hb[p][:, k * P:(k + 1) * P], ident)
                    last.then_inc(th, 1)

                def second_product(b, s):
                    pe.wait_ge(thv, b + 1)
                    wait(pe, ya, b, 0, 1)
                    wait(pe, yv, b, 0, 1)
                    for h in range(2):
                        for k in range(2):
                            last = pe.matmul(ps[5 + h][:, :], hT[s % 2][:, k, :], K.W2[s][:, k, h * 512:(h + 1) * 512], start=k == 0, stop=k == 1)
                    last.then_inc(ym, 1)

                turn_x(0, 0, 0)

                def body(b, s, half, quarter):
                    if not isinstance(b, int) or b < count - 1:
                        turn_x(b + 1, (s + 1) % 2, half + (s % 2))
                    if not isinstance(b, int) or b >= 1:
                        turn_h(b + (-1), (s + 1) % 2)
                    first_product(b, s, quarter)
                    if not isinstance(b, int) or b >= 1:
                        second_product(b + (-1), (s + 3) % 4)

                every_block(pe, body)
                turn_h(count - 1, 1)
                second_product(count - 1, 3)

            @block.scalar
            def _(act):
                def copy_x(b, p):
                    act.wait_ge(tx, b + 1)
                    wait(act, hm, b, -1, 2)
                    act.activation(xT[p][:, 0:4, :].rearrange("p k r -> p (k r)"), ps[0][:, :], ACT.Copy).then_inc(txa, 1)

                def copy_y(b, p, half_before):
                    act.wait_ge(ym, b + 1)
                    if not isinstance(b, int) or b >= 2:
                        act.wait_ge(sc[p], half_before * 16)
                    act.activation(ysb[p][:, 0:512], ps[5][:, :], ACT.Copy).then_inc(ya, 1)

                copy_x(0, 0)

                def body(b, s, half, quarter):
                    if not isinstance(b, int) or b < count - 1:
                        copy_x(b + 1, (s + 1) % 2)
                    act.wait_ge(hm, b + 1)
                    wait(act, hbd, b, -1, 2)
                    act.activation(sil[s % 2], ps[2 + s % 2][:, 0:DE], ACT.Silu).then_inc(sild, 1)
                    if not isinstance(b, int) or b >= 1:
                        copy_y(b + (-1), (s + 1) % 2, half + (s % 2 - 1))

                every_block(act, body)
                copy_y(count - 1, 1, (count - 1) // 2)

            @block.vector
            def _(dve):
                def copy_x(b, p):
                    dve.wait_ge(tx, b + 1)
                    wait(dve, hm, b, -1, 2)
                    dve.tensor_copy(xT[p][:, 4:8, :].rearrange("p k r -> p (k r)"), ps[1][:, :]).then_inc(txv, 1)

                def copy_h(b, p):
                    dve.wait_ge(th, b + 1)
                    wait(dve, ym, b, -1, 2)
                    dve.tensor_copy(hT[p].rearrange("p k r -> p (k r)"), ps[4][:, 0:DE]).then_inc(thv, 1)

                def copy_y(b, p, half_before):
                    dve.wait_ge(ym, b + 1)
                    if not isinstance(b, int) or b >= 2:
                        dve.wait_ge(sc[p], half_before * 16)
                    dve.tensor_copy(ysb[p][:, 512:1024], ps[6][:, :]).then_inc(yv, 1)

                copy_x(0, 0)

                def body(b, s, half, quarter):
                    if not isinstance(b, int) or b < count - 1:
                        copy_x(b + 1, (s + 1) % 2)
                    if not isinstance(b, int) or b >= 1:
                        copy_h(b + (-1), (s + 1) % 2)
                    dve.wait_ge(sild, b + 1)
                    wait(dve, th, b, -1, 2)
                    dve.tensor_tensor(hb[s % 2], sil[s % 2], ps[2 + s % 2][:, DE:2 * DE], ALU.mult).then_inc(hbd, 1)
                    if not isinstance(b, int) or b >= 1:
                        copy_y(b + (-1), (s + 1) % 2, half + (s % 2 - 1))

                every_block(dve, body)
                copy_h(count - 1, 1)
                copy_y(count - 1, 1, (count - 1) // 2)


def moe(nc, K, A, layer):
    with ExitStack() as ctx:
        def sb(n, s, d=F32):
            return ctx.enter_context(nc.sbuf_tensor(f"moe{layer}_" + n, s, d))

        K.W13 = [sb(f"W13_{s}", [P, KD, 2, DE]) for s in range(4)]
        K.W2 = [sb(f"W2_{s}", [P, 2, D]) for s in range(4)]
        routing(nc, K, A, layer, f"ro{layer}_")
        experts(nc, K, A, layer, f"ex{layer}_", 0, NE, K.ew_in, K.ew_base)
        K.ew_base += 48 * NE // 4
        overflow = nc.values_load(K.EO[0:1, OVER:OVER + 1], min_val=0, max_val=OVER)
        with nc.If(overflow > 0):
            experts(nc, K, A, layer, f"ov{layer}_", NE, OVER, [K.sem(f"ov{layer}_w{s}") for s in range(4)], 0)


def pool_mixer(nc, K, A):
    HT, X, ps, cst = K.HT, K.X, K.ps, K.cst
    with ExitStack() as ctx:
        def sb(n, s, d=F32):
            return ctx.enter_context(nc.sbuf_tensor("pm_" + n, s, d))

        w = sb("w", [P, 4, 2, 256])
        PM = sb("PM", [P, KD, L])
        bufs = [sb(f"b{i}", [P, 2, L]) for i in range(2)]
        bb, sc = sb("bb", [P, D]), sb("sc", [P, D])
        T = sb("T", [P, 2, D])
        w_in, pooled, mm, biased, scaled, done = (K.sem("pm_" + n) for n in ("w_in", "pooled", "mm", "biased", "scaled", "done"))

        with nc.Block() as block:
            @block.sync
            def _(sp):
                for g in range(4):
                    sp.dma_start(w[:, g], A["pool_w_2"][0, g].rearrange("(k p) n -> p k n", p=P)).then_inc(w_in, 16)
                sp.dma_start(bb[:, :], A["pool_b_2"].to_broadcast([P, D])).then_inc(w_in, 16)
                sp.dma_start(sc[:, :], A["pool_scale_2"].to_broadcast([P, D])).then_inc(w_in, 16)

            @block.vector
            def _(dve):
                for g, win in enumerate(WINS):
                    src = HT[:, 2 * g:2 * g + 2, :]
                    x, sh, n = src, 1, 0
                    while sh < win:
                        dst = bufs[n % 2]
                        dve.tensor_tensor(dst[:, :, sh:L], x[:, :, sh:L], x[:, :, 0:L - sh], ALU.add)
                        dve.tensor_copy(dst[:, :, 0:sh], x[:, :, 0:sh])
                        dve.drain()
                        x, sh, n = dst, 2 * sh, n + 1
                    dve.tensor_tensor(x[:, :, 0:win], x[:, :, 0:win], cst[:, C_POOL:C_POOL + win].unsqueeze(1).to_broadcast([P, 2, win]), ALU.mult)
                    dve.drain()
                    out = PM[:, 2 * g:2 * g + 2, :]
                    dve.scalar_tensor_tensor(out=out[:, :, win:L], in0=x[:, :, win:L], scalar=1.0 / win, in1=src[:, :, win:L], op0=ALU.mult, op1=ALU.subtract)
                    dve.tensor_tensor(out[:, :, 0:win], x[:, :, 0:win], src[:, :, 0:win], ALU.subtract)
                    dve.drain()
                    dve.sem_inc(pooled, 1)
                dve.wait_ge(w_in, 16 * 6)
                for t in range(NT + 1):
                    if t < NT:
                        dve.wait_ge(mm, t + 1)
                        if t >= 2:
                            dve.wait_ge(done, t - 1)
                        for h in range(2):
                            last = dve.tensor_tensor(T[:, t % 2, h * 512:(h + 1) * 512], ps[2 * (t % 4) + h][:, :], bb[:, h * 512:(h + 1) * 512], ALU.add)
                        last.then_inc(biased, 1)
                    if t >= 1:
                        u = t - 1
                        dve.wait_ge(scaled, u + 1)
                        dve.scalar_tensor_tensor(out=X[:, u, :], in0=X[:, u, :], scalar=ALPHA, in1=T[:, u % 2, :], op0=ALU.mult, op1=ALU.add).then_inc(done, 1)

            @block.gpsimd
            def _(pool):
                pool.wait_ge(w_in, 16 * 6)
                for t in range(NT):
                    pool.wait_ge(biased, t + 1)
                    pool.tensor_tensor(T[:, t % 2, :], T[:, t % 2, :], sc[:, :], ALU.mult).then_inc(scaled, 1)

            @block.tensor
            def _(pe):
                pe.wait_ge(w_in, 16 * 6)
                pe.wait_ge(pooled, 4)
                for t in range(NT):
                    if t >= 4:
                        pe.wait_ge(biased, t - 3)
                    for g in range(4):
                        for k in range(2):
                            last = pe.matmul(ps[2 * (t % 4) + g // 2][:, (g % 2) * 256:(g % 2 + 1) * 256], PM[:, 2 * g + k, t * P:(t + 1) * P],
                                             w[:, g, k, :], start=k == 0, stop=k == 1)
                    last.then_inc(mm, 1)


def second_block(nc, K, A):
    K.yrow = nc.dram_tensor("yrow", [2 * L, D], F32).ap()
    K.ew_in = [K.sem(f"ew_in{s}", lasting=True) for s in range(4)]
    K.ew_base = 0
    K.clear()
    with ExitStack() as ctx:
        def sb(n, s, d=F32):
            return ctx.enter_context(nc.sbuf_tensor(n, s, d))

        K.GT = sb("GT", [P, 2, NT])
        K.EO = sb("EO", [P, OVER + 1], I32)
        K.SIDX, K.GIDX = sb("SIDX", [P, NB], I32), sb("GIDX", [P, NB], I32)
        mla(nc, K, A)
        layer_norm(nc, K, A, "ln0_", 0, 0, K.xrow, router=0)
        K.clear()
        moe(nc, K, A, 0)
        K.clear()
        layer_norm(nc, K, A, "ln1_", 0, 1, None, combine=True)
        pool_mixer(nc, K, A)
        layer_norm(nc, K, A, "ln2_", 1, 0, K.xrow, router=1)
        K.clear()
        moe(nc, K, A, 1)
        layer_norm(nc, K, A, "ln3_", 1, 1, A["out"], transpose=False, combine=True)


class Memory:
    pass


def semaphore_pool(nc):
    held = []

    def sem(name, lasting=False):
        s = nc.alloc_semaphore(name=name)
        if not lasting:
            held.append(s)
        return s

    def clear():
        nc.clear_and_free_semaphores(held[:])
        nc.all_engine_barrier()
        held.clear()

    return sem, clear


def build(nc, A):
    with ExitStack() as ctx:
        def sb(n, s, d=F32):
            return ctx.enter_context(nc.sbuf_tensor(n, s, d))

        K = Memory()
        K.sem, K.clear = semaphore_pool(nc)
        K.psum = ctx.enter_context(nc.psum_tensor("psum", [P, 8, 512], F32))
        K.ps = [K.psum[:, i, :] for i in range(8)]
        K.cst = sb("cst", [P, C_W])
        K.cols = sb("cols", [P, NCOL])
        K.A1, K.B1, K.A1c, K.B1c, K.A2, K.B2 = (sb(n, [P, KD]) for n in ("A1", "B1", "A1c", "B1c", "A2", "B2"))
        K.xrow = nc.dram_tensor("xrow", [L, D], F32).ap()
        xreg = sb("xreg", [P, 10 * D])
        K.XC = xreg[:, :].rearrange("p (t n) -> p t n", n=D)
        K.X = K.XC[:, 0:NT, :]
        K.ZT = xreg[:, 0:NT * SW].rearrange("p (t n) -> p t n", n=SW)
        K.V = xreg[:, NT * SW:NT * SW + NT * 512].rearrange("p (t n) -> p t n", n=512)
        hreg = K.hreg = sb("hreg", [P, 10 * D])
        K.HT = hreg[:, 0:KD * L].rearrange("p (k t) -> p k t", t=L)
        K.HTc = hreg[:, KD * L:KD * L + KD * LC].rearrange("p (k t) -> p k t", t=LC)
        K.TOK = hreg[:, :].rearrange("p (t n) -> p t n", n=SW + 512)
        first_block(nc, K, A)
        second_block(nc, K, A)


_INS = ["x", "c", "ctx", "c_ctx", "w_ada", "b_ada", "g_pre_mix", "g_post_mix", "g_pre_ffn", "g_post_ffn", "w_in", "conv_w",
        "conv_b", "dt_bias", "a_log", "d_skip", "g_ssd", "w_out", "w_gate", "w_up", "w_down", "positions_2", "ln_g_2",
        "ln_b_2", "mla_w_in_2", "mla_q_norm_2", "mla_w_uq_2", "mla_kv_norm_2", "mla_w_ukv_2", "mla_w_o_2",
        "pool_w_2", "pool_b_2", "pool_scale_2", "moe_w_grp_2", "moe_b_grp_2", "moe_w_exp_2", "moe_b_exp_2",
        "moe_w1_2", "moe_w3_2", "moe_w2_2"]


def kernel(**inputs):
    import concourse.bacc as bacc
    from concourse.bass_utils import run_bass_kernel_spmd

    nc = bacc.Bacc("TRN2", target_bir_lowering=False, num_devices=1)
    arrays, A = {}, {}
    tables = {"consts": constant_table(), "dft": dft_table()}
    for name in _INS + list(tables):
        a = np.ascontiguousarray(tables[name] if name in tables else inputs[name])
        arrays[f"in_{name}"] = a
        A[name] = nc.dram_tensor(f"in_{name}", a.shape, mybir.dt.from_np(a.dtype), kind="ExternalInput").ap()
    out = nc.dram_tensor("out_0", (1, L, D), F32, kind="ExternalOutput").ap()
    A["out"] = out[0]
    build(nc, A)
    r = run_bass_kernel_spmd(nc, [arrays], core_ids=[0])
    return r.results[0]["out_0"]
```

```python
from contextlib import ExitStack

import numpy as np

import concourse.bass as bass
from concourse import mybir

F32 = mybir.dt.float32
F32R = mybir.dt.float32r
I32 = mybir.dt.int32
U32 = mybir.dt.uint32
BF16 = mybir.dt.bfloat16
ALU = mybir.AluOpType
ACT = mybir.ActivationFunctionType
AX = mybir.AxisListType
ds = bass.ds

P = 128
L = 1024
D = 1024
LC = 256
NT = L // P
NTC = LC // P
KD = D // P
NMOD = 6
FW = 256
SW = 768
HD = 64
NH = 12
NG = 4
HPG = NH // NG
CONV = 1792
NCV = CONV // P
TAPS = 7
HALF = TAPS // 2
ROW = 64
DT0 = FW + SW + CONV
INW = DT0 + 2 * NH
DFF = 2816
KF = DFF // P
EPS = 1e-6
LN_EPS = 1e-5
ALPHA = 4 ** 0.25
NEG = -1e30
AH = 16
QL, KVL, RD = 256, 128, 32
LAT = QL + KVL + RD
SCALE = 96.0 ** -0.5
NE = 64
DE = 256
MAIN = NE
OVER = 16
NB = MAIN + OVER
WINS = (2, 4, 8, 16)

C_ID, C_UP, C_LO, C_SUP, C_NEG, C_IOTA, C_TOK, C_CB, C_SB, C_FREQ = 0, 128, 256, 384, 512, 640, 768, 784, 912, 1040
C_POOL = 1056
C_THR = C_POOL + 16
C_W = C_THR + 8

NCOL = 8 + 8 + 8 + 8 + 6 + 2 + 1 + NCV
COL_GSSD, COL_QN, COL_KVN, COL_CB = 32, 38, 40, 41


def constant_table():
    t = np.zeros((P, C_W), np.float32)
    i = np.arange(P)
    t[:, C_ID:C_ID + P] = np.eye(P)
    t[:, C_UP:C_UP + P] = i[:, None] <= i[None]
    t[:, C_LO:C_LO + P] = i[:, None] >= i[None]
    t[:, C_SUP:C_SUP + P] = i[:, None] < i[None]
    t[:, C_NEG:C_NEG + P] = np.where(i[None] <= i[:, None], 0.0, NEG)
    t[:, C_IOTA:C_IOTA + P] = i[None]
    for k in range(2):
        for m in range(NT):
            t[:, C_TOK + k * NT + m] = 2 * (m * P + i) + k + 1
    a = 2 * np.pi * np.outer(np.arange(64), np.arange(64)) / 64
    for g in range(2):
        s = slice(64 * g, 64 * g + 64)
        t[s, C_CB + 64 * g:C_CB + 64 * g + 64] = np.cos(a) / 256
        t[s, C_SB + 64 * g:C_SB + 64 * g + 64] = -np.sin(a) / 256
    t[:, C_FREQ:C_FREQ + 16] = (10000.0 ** (-np.arange(0, 32, 2, dtype=np.float32) / np.float32(32))).astype(np.float32)
    t[:, C_POOL:C_POOL + 16] = 1.0 / (np.arange(16) + 1)
    t[:, C_THR:C_THR + 8] = P * (np.arange(8) + 1)
    return t


def dft_table():
    n = np.arange(L)
    a = 2 * np.pi * (np.outer(n, n) % L) / L
    return np.stack([np.cos(a), np.sin(a)], 1).astype(np.float32)


def modulation(nc, K, A):
    NTT = NT + NTC
    NCH, W, NBUF = NMOD * D // 512, 512, 3
    with ExitStack() as ctx:
        def sb(n, s, d=F32):
            return ctx.enter_context(nc.sbuf_tensor("ada_" + n, s, d))

        wbuf = sb("w", [P, NBUF, KD, W])
        rows = sb("rows", [NCOL, P])
        mod = sb("mod", [2, NMOD * D])
        bada = sb("bada", [2, NMOD * D])
        cT = sb("cT", [P, 16])
        modT = sb("modT", [P, 48, 2])
        small, rows_t, cols_ok, silu_ok = K.sem("small_in"), K.sem("rows_t"), K.sem("cols_ok"), K.sem("silu_ok")
        w_in = [K.sem(f"ada_w{i}") for i in range(NBUF)]
        mm, ev = K.sem("ada_mm"), K.sem("ada_ev")
        tr, br, ok = K.sem("ada_tr"), K.sem("ada_br"), K.sem("ada_ok")
        ss, rs, junk = sb("ss", [P, NTT]), sb("rs", [P, NTT]), sb("junk", [P, D])
        x_in = [K.sem(f"ada_x{t}") for t in range(NTT)]
        sq, var, root, inv = (K.sem("ada_" + n) for n in ("sq", "var", "root", "inv"))
        w_dram = A["w_ada"][0].rearrange("(k p) n -> p k n", p=P)
        vecs = [("c", 8), ("c_ctx", 8), ("g_pre_mix", 8), ("g_pre_ffn", 8), ("g_ssd", 6),
                ("mla_q_norm_2", 2), ("mla_kv_norm_2", 1), ("conv_b", NCV)]
        ident = K.cst[:, C_ID:C_ID + P]

        with nc.Block() as block:
            @block.sync
            def _(sp):
                sp.dma_start(K.cst[:, :], A["consts"]).then_inc(small, 16)
                at = 0
                for name, n in vecs:
                    v = A[name]
                    flat = v if len(v.shape) == 1 else v.rearrange("a n -> (a n)")
                    sp.dma_start(rows[at:at + n, :], flat.rearrange("(a p) -> a p", p=P)).then_inc(small, 16)
                    at += n
                for r in range(2):
                    sp.dma_start(bada[r:r + 1, :], A["b_ada"]).then_inc(small, 16)
                sp.dma_start(K.G1[:, :], A["g_post_mix"].to_broadcast([P, D])).then_inc(small, 16)
                sp.dma_start(K.G2[:, :], A["g_post_ffn"].to_broadcast([P, D])).then_inc(small, 16)

                def chunks(i):
                    for s in range(NBUF):
                        sp.wait_ge(mm, i * NBUF + s + 1)
                        sp.dma_start(wbuf[:, s], w_dram[:, :, ds((i * NBUF + s) * W, W)]).then_inc(w_in[s], 16)

                def tokens(first, last):
                    for t in range(first, last):
                        src = A["x"][0, t * P:(t + 1) * P, :] if t < NT else A["ctx"][0, (t - NT) * P:(t - NT + 1) * P, :]
                        sp.dma_start(K.XC[:, t, :], src).then_inc(x_in[t], 16)

                chunks(0)
                tokens(0, 3)
                chunks(1)
                tokens(3, NTT)
                with sp.Fori(2, NCH // NBUF) as i:
                    chunks(i)

            @block.tensor
            def _(pe):
                pe.sem_inc(mm, NBUF)
                pe.wait_ge(small, 16 * (len(vecs) + 5))
                pe.transpose(K.ps[7][:, 0:NCOL], rows[:, :], ident[0:NCOL, 0:NCOL]).then_inc(rows_t, 1)
                pe.wait_ge(silu_ok, 1)
                with pe.Fori(0, NCH // NBUF) as i:
                    for s in range(NBUF):
                        pe.wait_ge(w_in[s], 16 * (i + 1))
                        pe.wait_ge(ev, i * NBUF + s + 1)
                        for k in range(KD):
                            last = pe.matmul(K.ps[s][0:2, :], cT[:, k:16:8], wbuf[:, s, k, :], start=k == 0, stop=k == KD - 1)
                        last.then_inc(mm, 1)
                pe.wait_ge(ev, NCH + NBUF)
                for j in range(48):
                    last = pe.transpose(K.ps[4][:, 2 * j:2 * j + 2], mod[:, j * P:(j + 1) * P], ident[0:2, 0:2])
                last.then_inc(tr, 1)
                for n, (bank, src) in enumerate(((5, 2 * D), (6, 2 * D + 512), (7, 5 * D), (3, 5 * D + 512))):
                    last = pe.matmul(K.ps[bank][:, :], K.cst[0:1, C_UP:C_UP + P], mod[0:1, src:src + 512], start=True, stop=True)
                last.then_inc(br, 1)

            @block.scalar
            def _(act):
                act.wait_ge(cols_ok, 1)
                act.activation(cT[:, :], K.cols[:, 0:16], ACT.Silu).then_inc(silu_ok, 1)
                for t in range(NTT):
                    act.wait_ge(x_in[t], 16)
                    act.activation(junk[:, :], K.XC[:, t, :], ACT.Square, accum_out=ss[:, t:t + 1]).then_inc(sq, 1)
                    act.drain()
                act.wait_ge(var, 1)
                act.activation(rs[:, :], ss[:, :], ACT.Sqrt).then_inc(root, 1)
                act.wait_ge(inv, 1)
                for t in range(NTT):
                    act.activation(K.XC[:, t, :], K.XC[:, t, :], ACT.Identity, scale=rs[:, t:t + 1], bias=0.0)

            @block.vector
            def _(dve):
                dve.sem_inc(ev, NBUF)
                dve.wait_ge(rows_t, 1)
                dve.tensor_copy(K.cols[:, :], K.ps[7][:, 0:NCOL]).then_inc(cols_ok, 1)

                def chunks(i):
                    for s in range(NBUF):
                        dve.wait_ge(mm, i * NBUF + s + 1 + NBUF)
                        at = ds((i * NBUF + s) * 512, 512)
                        dve.tensor_tensor(mod[:, at], K.ps[s][0:2, :], bada[:, at], ALU.add).then_inc(ev, 1)

                chunks(0)
                chunks(1)
                chunks(2)
                dve.wait_ge(sq, NTT)
                dve.tensor_scalar(ss[:, :], ss[:, :], 1.0 / D, EPS, ALU.mult, ALU.add).then_inc(var, 1)
                dve.wait_ge(root, 1)
                dve.reciprocal(rs[:, :], rs[:, :]).then_inc(inv, 1)
                for i in range(3, NCH // NBUF):
                    chunks(i)
                dve.wait_ge(tr, 1)
                dve.tensor_copy(modT[:, :, :], K.ps[4][:, 0:96].rearrange("p (j v) -> p j v", v=2)).then_inc(ok, 1)
                dve.wait_ge(ok, 1)
                for dst, j, v, g in ((K.A1, 8, 0, 16), (K.A1c, 8, 1, 16), (K.A2, 32, 0, 24)):
                    dve.scalar_tensor_tensor(out=dst[:, :], in0=modT[:, j:j + 8, v], scalar=1.0, in1=K.cols[:, g:g + 8],
                                             op0=ALU.add, op1=ALU.mult)
                for dst, j, v in ((K.B1, 0, 0), (K.B1c, 0, 1), (K.B2, 24, 0)):
                    dve.tensor_copy(dst[:, :], modT[:, j:j + 8, v])
                dve.wait_ge(br, 1)
                for G, banks in ((K.G1, (5, 6)), (K.G2, (7, 3))):
                    for h, b in enumerate(banks):
                        dve.tensor_tensor(G[:, h * 512:(h + 1) * 512], K.ps[b][:, :], G[:, h * 512:(h + 1) * 512], ALU.mult)


def rms_to_feature_major(nc, K, tag, src, norm, jobs, store=None, split=None, ahead=None, sums=None):
    n_tiles = sum(j[1] for j in jobs)
    groups = [(k, t0, t, min(4, n - t), dst, A_, B_) for t0, n, dst, A_, B_ in jobs
              for t in range(0, n, 4) for k in range(KD)]
    NBK = 4
    with ExitStack() as ctx:
        ss = sums if sums is not None else ctx.enter_context(nc.sbuf_tensor(tag + "_ss", [P, n_tiles], F32))
        rs = ctx.enter_context(nc.sbuf_tensor(tag + "_rs", [P, n_tiles], F32))
        junk = ctx.enter_context(nc.sbuf_tensor(tag + "_junk", [P, D], F32))
        sq, var, root, inv, scaled = (K.sem(tag + n) for n in ("_sq", "_var", "_root", "_inv", "_scaled"))
        full = [ctx.enter_context(nc.sbuf_tensor(f"{tag}_full{i}", [P, 512], F32)) for i in range(4)] if split else None
        stored, s_full, s_hi, s_lo = (K.sem(tag + n) for n in ("_stored", "_full", "_hi", "_lo"))
        tr, ev_v, ev_a = K.sem(tag + "_tr"), K.sem(tag + "_ev_v"), K.sem(tag + "_ev_a")

        def bank(g):
            return K.ps[g % NBK]

        with nc.Block() as block:
            @block.sync
            def _(sp):
                if ahead:
                    ahead(sp)
                if store is not None:
                    sp.dma_start(store.rearrange("(t p) n -> p t n", p=P), src[:, 0:NT, :]).then_inc(stored, 16)
                    sp.wait_ge(stored, 16)

            @block.scalar
            def _(act):
                if src is not None:
                    for t in range(n_tiles if sums is None else 0):
                        act.activation(junk[:, :], src[:, t, :], ACT.Square, accum_out=ss[:, t:t + 1]).then_inc(sq, 1)
                        act.drain()
                    act.wait_ge(var, 1)
                    act.activation(rs[:, :], ss[:, :], ACT.Sqrt).then_inc(root, 1)
                for g, (k, t0, t, n, dst, A_, B_) in enumerate(groups):
                    if split:
                        act.wait_ge(tr, g + 1)
                        if g >= 4:
                            act.wait_ge(s_lo, g - 3)
                        act.activation(full[g % 4][:, :], bank(g), ACT.Identity, scale=A_[:, k:k + 1], bias=B_[:, k:k + 1]).then_inc(s_full, 1)
                    elif g % 2 == 1:
                        act.wait_ge(tr, g + 1)
                        act.activation(dst[:, k, t * P:(t + n) * P], bank(g)[:, 0:n * P], ACT.Identity,
                                       scale=A_[:, k:k + 1], bias=B_[:, k:k + 1]).then_inc(ev_a, 1)

            @block.vector
            def _(dve):
                if src is not None:
                    if sums is None:
                        dve.wait_ge(sq, n_tiles)
                    dve.tensor_scalar(ss[:, :], ss[:, :], 1.0 / D, EPS, ALU.mult, ALU.add).then_inc(var, 1)
                    dve.wait_ge(root, 1)
                    dve.reciprocal(rs[:, :], rs[:, :]).then_inc(inv, 1)
                    dve.wait_ge(inv, 1)
                    for t in range(n_tiles):
                        dve.tensor_scalar(norm[:, t, :], src[:, t, :], rs[:, t:t + 1], None, ALU.mult).then_inc(scaled, 1)
                for g, (k, t0, t, n, dst, A_, B_) in enumerate(groups):
                    if split:
                        dve.wait_ge(s_hi, g + 1)
                        cols = slice(t * P, (t + n) * P)
                        dve.tensor_tensor(split[1][:, k, cols], full[g % 4][:, :], split[0][:, k, cols].bitcast(F32), ALU.subtract).then_inc(s_lo, 1)
                    elif g % 2 == 0:
                        dve.wait_ge(tr, g + 1)
                        dve.tensor_scalar(dst[:, k, t * P:(t + n) * P], bank(g)[:, 0:n * P],
                                          A_[:, k:k + 1], B_[:, k:k + 1], ALU.mult, ALU.add).then_inc(ev_v, 1)

            @block.gpsimd
            def _(pool):
                if split:
                    for g, (k, t0, t, n, dst, A_, B_) in enumerate(groups):
                        pool.wait_ge(s_full, g + 1)
                        pool.tensor_copy(split[0][:, k, t * P:(t + n) * P], full[g % 4][:, :]).then_inc(s_hi, 1)

            @block.tensor
            def _(pe):
                for g, (k, t0, t, n, dst, A_, B_) in enumerate(groups):
                    if split and g >= NBK:
                        pe.wait_ge(s_full, g - NBK + 1)
                    elif g >= NBK:
                        pe.wait_ge(ev_v if g % 2 == 0 else ev_a, (g - NBK) // 2 + 1)
                    if src is not None:
                        pe.wait_ge(scaled, t0 + t + n)
                    for j in range(n):
                        last = pe.transpose(bank(g)[:, j * P:(j + 1) * P], norm[:, t0 + t + j, k * P:(k + 1) * P],
                                            K.cst[:, C_ID:C_ID + P])
                    last.then_inc(tr, 1)


def projection_weights(K):
    flat = K.XF[:, :, :].rearrange("p a b -> p (a b)")
    K.wz = flat[:, 0:6 * L].rearrange("p (k n) -> p k n", k=KD)
    K.wu = flat[:, 6 * L:8 * L].rearrange("p (k n) -> p k n", k=KD)
    K.wdt = flat[:, 10 * L:10 * L + KD * 24].rearrange("p (k n) -> p k n", k=KD)
    K.z_in, K.u_in, K.dt_in = (K.sem("pj_" + n) for n in ("z_in", "u_in", "dt_in"))


def load_projection_weights(sp, K, A):
    w_dram = A["w_in"][0].rearrange("(k p) n -> p k n", p=P)
    sp.dma_start(K.wdt, w_dram[:, :, DT0:INW]).then_inc(K.dt_in, 16)
    for h in range(2):
        ks = slice(4 * h, 4 * h + 4)
        sp.dma_start(K.wz[:, ks, :], w_dram[:, ks, FW:FW + SW]).then_inc(K.z_in, 16)
    sp.dma_start(K.wu, w_dram[:, :, 0:FW]).then_inc(K.u_in, 16)


def projections(nc, K, A):
    w_dram = A["w_in"][0].rearrange("(k p) n -> p k n", p=P)
    XF, XFc, HT, HTc, ZT, V = K.XF, K.XFc, K.HT, K.HTc, K.ZT, K.V
    ps = K.ps
    wz, wu, wdt = K.wz, K.wu, K.wdt
    uT = XF[:, 8:10, :]
    NCTX = 5
    with ExitStack() as ctx:
        def sb(n, s, d=F32):
            return ctx.enter_context(nc.sbuf_tensor("pj_" + n, s, d))

        wbuf = sb("w", [P, 2, KD, P])
        cw = sb("cw", [P, NCV, TAPS])
        cb = K.cols[:, COL_CB:COL_CB + NCV]
        RW = ROW + 2 * HALF
        pad = [sb(f"pad{s}", [P, L // ROW, RW]) for s in range(2)]
        padc = [sb(f"padc{s}", [P, LC + 2 * HALF]) for s in range(2)]
        acc = [sb(f"acc{s}", [P, L // ROW, ROW]) for s in range(2)]
        accc = [sb(f"accc{s}", [P, LC]) for s in range(2)]
        z_in, u_in, s_in = K.z_in, K.u_in, K.sem("pj_s_in")
        w_in = [K.sem(f"pj_w{s}") for s in range(2)]
        dt_mm, z_mm, z_ev, u_mm, u_ev, v_mm, v_ev = (K.sem("pj_" + n) for n in ("dtmm", "zmm", "zev", "umm", "uev", "vmm", "vev"))
        mm = [K.sem(f"pj_mm{s}") for s in range(2)]
        padded = [K.sem(f"pj_padded{s}") for s in range(2)]
        convd = [K.sem(f"pj_conv{s}") for s in range(2)]
        silud = [K.sem(f"pj_silu{s}") for s in range(2)]
        zero = K.sem("pj_zero")

        with nc.Block() as block:
            @block.sync
            def _(sp):
                sp.dma_start(cw[:, :, :], A["conv_w"][0].rearrange("(m p) t -> p m t", p=P)).then_inc(s_in, 16)
                sp.dma_start(K.dtb[:, :], A["dt_bias"].rearrange("a d n -> a (d n)").to_broadcast([P, 24])).then_inc(s_in, 16)
                sp.dma_start(K.alog[:, :], A["a_log"].rearrange("a d n -> a (d n)").to_broadcast([P, 24])).then_inc(s_in, 16)
                sp.dma_start(K.dskip[:, :], A["d_skip"].to_broadcast([P, NH])).then_inc(s_in, 16)

                def pair(i, base):
                    for s in range(2):
                        sp.wait_ge(mm[s], i + base + 1)
                        sp.dma_start(wbuf[:, s], w_dram[:, :, ds(FW + SW + (i + base) * 2 * P + s * P, P)]).then_inc(w_in[s], 16)

                with sp.Fori(0, NCTX) as i:
                    pair(i, 0)
                with sp.Fori(0, NCV // 2 - NCTX) as i:
                    pair(i, NCTX)

            @block.tensor
            def _(pe):
                for s in range(2):
                    pe.sem_inc(mm[s], 1)
                pe.wait_ge(K.dt_in, 16)
                for t in range(NT + NTC):
                    h = HT[:, :, t * P:(t + 1) * P] if t < NT else HTc[:, :, (t - NT) * P:(t - NT + 1) * P]
                    for k in range(KD):
                        last = pe.matmul(ps[6][:, t * 24:(t + 1) * 24], h[:, k, :], wdt[:, k, :], start=k == 0, stop=k == KD - 1)
                last.then_inc(dt_mm, 1)
                pe.wait_ge(z_in, 32)
                for t in range(NT):
                    if t >= 2:
                        pe.wait_ge(z_ev, t - 1)
                    for h, n in ((0, 512), (1, 256)):
                        for k in range(KD):
                            last = pe.matmul(ps[2 * (t % 2) + h][:, 0:n], HT[:, k, t * P:(t + 1) * P],
                                             wz[:, k, h * 512:h * 512 + n], start=k == 0, stop=k == KD - 1)
                    last.then_inc(z_mm, 1)
                pe.wait_ge(u_in, 16)
                pe.wait_ge(z_ev, NT)
                for m in range(2):
                    for h in range(2):
                        for k in range(KD):
                            last = pe.matmul(ps[2 * m + h][:, :], wu[:, k, m * P:(m + 1) * P], HT[:, k, h * 512:(h + 1) * 512],
                                             start=k == 0, stop=k == KD - 1)
                        last.then_inc(u_mm, 1)
                pe.wait_ge(u_ev, 4)
                for t in range(NT):
                    if t >= 2:
                        pe.wait_ge(v_ev, t - 1)
                    for m in range(2):
                        last = pe.matmul(ps[4 + t % 2][:, m * 256:(m + 1) * 256], uT[:, m, t * P:(t + 1) * P],
                                         K.cst[:, C_CB:C_CB + 256], start=True, stop=True)
                    last.then_inc(v_mm, 1)

                def pair(i, base, with_ctx):
                    for s in range(2):
                        pe.wait_ge(w_in[s], (i + base + 1) * 16)
                        pe.wait_ge(padded[s], i + base + 1)
                        for h in range(2):
                            for k in range(KD):
                                last = pe.matmul(ps[3 * s + h][:, :], wbuf[:, s, k, :], HT[:, k, h * 512:(h + 1) * 512],
                                                 start=k == 0, stop=k == KD - 1)
                        if with_ctx:
                            for k in range(KD):
                                last = pe.matmul(ps[3 * s + 2][:, 0:LC], wbuf[:, s, k, :], HTc[:, k, :],
                                                 start=k == 0, stop=k == KD - 1)
                        last.then_inc(mm[s], 1)

                with pe.Fori(0, NCTX) as i:
                    pair(i, 0, True)
                with pe.Fori(0, NCV // 2 - NCTX) as i:
                    pair(i, NCTX, False)

            @block.scalar
            def _(act):
                for t in range(NT):
                    act.wait_ge(z_mm, t + 1)
                    act.activation(ZT[:, t, 0:512], ps[2 * (t % 2)][:, :], ACT.Silu)
                    act.activation(ZT[:, t, 512:768], ps[2 * (t % 2) + 1][:, 0:256], ACT.Silu).then_inc(z_ev, 1)
                for n in range(4):
                    act.wait_ge(u_mm, n + 1)
                    act.activation(uT[:, n // 2, (n % 2) * 512:(n % 2) * 512 + 512], ps[n][:, :], ACT.Copy).then_inc(u_ev, 1)
                for t in range(NT):
                    act.wait_ge(v_mm, t + 1)
                    act.activation(V[:, t, :], ps[4 + t % 2][:, :], ACT.Copy).then_inc(v_ev, 1)
                act.wait_ge(zero, 1)
                act.wait_ge(v_ev, NT)
                for s in range(2):
                    act.sem_inc(padded[s], 1)

                def pair(i, base, with_ctx):
                    for s in range(2):
                        act.wait_ge(mm[s], i + base + 2)
                        act.wait_ge(convd[s], i + base + 1)
                        for h in range(2):
                            last = act.activation(pad[s][:, 8 * h:8 * h + 8, HALF:HALF + ROW],
                                                  ps[3 * s + h][:, :].rearrange("p (r n) -> p r n", n=ROW), ACT.Copy)
                        if with_ctx:
                            last = act.activation(padc[s][:, HALF:HALF + LC], ps[3 * s + 2][:, 0:LC], ACT.Copy)
                        last.then_inc(padded[s], 1)
                        act.wait_ge(convd[s], i + base + 2)
                        m = (i + base) * 2 + s
                        last = act.activation(XF[:, ds(m, 1), :], acc[s][:, :, :].rearrange("p (o r) n -> p o (r n)", o=1), ACT.Silu)
                        if with_ctx:
                            last = act.activation(XFc[:, ds(m, 1), :], accc[s][:, :].rearrange("p (o n) -> p o n", o=1), ACT.Silu)
                        last.then_inc(silud[s], 1)

                with act.Fori(0, NCTX) as i:
                    pair(i, 0, True)
                with act.Fori(0, NCV // 2 - NCTX) as i:
                    pair(i, NCTX, False)

            @block.gpsimd
            def _(pool):
                for s in range(2):
                    pool.memset(pad[s][:, :, :], 0.0)
                    last = pool.memset(padc[s][:, :], 0.0)
                pool.drain()
                pool.sem_inc(zero, 1)

            @block.vector
            def _(dve):
                dve.wait_ge(s_in, 16 * 4)
                dve.wait_ge(dt_mm, 1)
                dve.tensor_copy(K.dtr[:, :, :], ps[6][:, 0:240].rearrange("p (t n) -> p t n", n=24))
                for s in range(2):
                    dve.sem_inc(convd[s], 1)
                    dve.sem_inc(silud[s], 1)

                def pair(i, base, with_ctx):
                    for s in range(2):
                        m = (i + base) * 2 + s
                        dve.wait_ge(padded[s], i + base + 2)
                        dve.wait_ge(silud[s], i + base + 1)
                        for tap in range(TAPS):
                            w = cw[:, ds(m, 1), tap]
                            if tap == 0:
                                last = dve.tensor_scalar(acc[s][:, :, :], pad[s][:, :, 0:ROW], w, cb[:, ds(m, 1)], ALU.mult, ALU.add)
                                if with_ctx:
                                    last = dve.tensor_scalar(accc[s][:, :], padc[s][:, 0:LC], w, cb[:, ds(m, 1)], ALU.mult, ALU.add)
                            else:
                                last = dve.scalar_tensor_tensor(out=acc[s][:, :, :], in0=pad[s][:, :, tap:tap + ROW], scalar=w,
                                                         in1=acc[s][:, :, :], op0=ALU.mult, op1=ALU.add)
                                if with_ctx:
                                    last = dve.scalar_tensor_tensor(out=accc[s][:, :], in0=padc[s][:, tap:tap + LC], scalar=w,
                                                             in1=accc[s][:, :], op0=ALU.mult, op1=ALU.add)
                            if tap < TAPS - 1:
                                dve.drain()
                        last.then_inc(convd[s], 1)

                with dve.Fori(0, NCTX) as i:
                    pair(i, 0, True)
                with dve.Fori(0, NCV // 2 - NCTX) as i:
                    pair(i, NCTX, False)


def ssd(nc, K, A):
    XF, XFc, TOK, ps, cst = K.XF, K.XFc, K.TOK, K.ps, K.cst
    Y = XF[:, 0:6, :].rearrange("p a b -> p (a b)").rearrange("p (t n) -> p t n", n=SW)
    K.Y = Y
    ident = cst[:, C_ID:C_ID + P]
    xfc = XFc[:, :, :].rearrange("p a b -> p (a b)")
    NTT = NT + NTC
    fwd = [NT + c for c in range(NTC)] + list(range(NT))
    bwd = [NT + c for c in reversed(range(NTC))] + list(reversed(range(NT)))
    units = [(d, (fwd, bwd)[d][i]) for i in range(NTT) for d in range(2)]
    NU, NUC = len(units), 2 * NTC
    turns = [(NT + c, c) for c in range(NTC)] + [(t, t) for t in range(NTC, NT)] + [(t, t) for t in range(NTC)]

    def slot(t):
        return t - NT if t >= NT else t

    with ExitStack() as ctx:
        def sb(n, s, d=F32):
            return ctx.enter_context(nc.sbuf_tensor("sd_" + n, s, d))

        dt, dA, cs, ecs, W, Eend = (sb(n, [P, NTT, 24]) for n in ("dt", "dA", "cs", "ecs", "W", "Eend"))
        ones = sb("ones", [P, P])
        E = [sb("E0", [P, NH, P]), xfc[:, 0:NH * P].rearrange("p (h q) -> p h q", q=P)]
        SCM = [xfc[:, NH * P + 512 * i:NH * P + 512 * i + 512].rearrange("p (g q) -> p g q", q=P) for i in range(2)]
        M = sb("M", [P, NH, P])
        Hs = [sb(f"H{d}", [P, SW]) for d in range(2)]
        tmp = sb("tmp", [P, SW])
        XW = [sb(f"xw{i}", [P, NH, HD]) for i in range(2)]
        XDT = sb("xdt", [P, NH, HD])
        (tr, ev_a, ev_v, pre, pre_a, one, csmm, ready, hz, a_mm, a_v, e_ok, m_ok, xw_ok, xd_ok, st_mm, yo_mm, yd_mm,
         st_v, yo_v, yd_v, dec, y0, y2) = (K.sem("sd_" + n) for n in (
             "tr", "eva", "evv", "pre", "prea", "one", "csmm", "ready", "hz", "amm", "av", "eok", "mok", "xwok", "xdok",
             "stmm", "yomm", "ydmm", "stv", "yov", "ydv", "dec", "y0", "y2"))

        def feat(t, f):
            return XF[:, f, t * P:(t + 1) * P] if t < NT else XFc[:, f, (t - NT) * P:(t - NT + 1) * P]

        def per_head(a, d, t, n):
            return a[:, t, d * NH:(d + 1) * NH].unsqueeze(2).to_broadcast([P, NH, n])

        def xi(u):
            return u - NUC

        with nc.Block() as block:
            @block.tensor
            def _(pe):
                def to_tokens(n):
                    t, sl = turns[n]
                    if n >= 2:
                        pe.wait_ge(ev_a, n - 1)
                        pe.wait_ge(ev_v, n - 1)
                    for f in range(10):
                        last = pe.transpose(ps[3 * (n % 2) + f // 4][:, (f % 4) * P:(f % 4 + 1) * P], feat(t, f), ident)
                    last.then_inc(tr, 1)

                def stage_a(u):
                    d, t = units[u]
                    tri = cst[:, (C_UP, C_LO)[d]:(C_UP, C_LO)[d] + P]
                    for b in range(4):
                        n = 4 * xi(u) + b
                        if n >= 2:
                            pe.wait_ge(a_v, n - 1)
                        if b == 0:
                            for g in range(NG):
                                last = pe.matmul(ps[n % 2][:, g * P:(g + 1) * P], feat(t, 6 + g), feat(t, 10 + g), start=True, stop=True)
                        else:
                            for j in range(4):
                                h = d * NH + 4 * (b - 1) + j
                                last = pe.matmul(ps[n % 2][:, j * P:(j + 1) * P], dA[:, t, h:h + 1].to_broadcast([P, P]), tri, start=True, stop=True)
                        last.then_inc(a_mm, 1)

                def stage_b(u):
                    d, t = units[u]
                    pe.wait_ge(xw_ok, u + 1)
                    if u >= 1:
                        pe.wait_ge(st_v, u)
                    for g in range(NG):
                        last = pe.matmul(ps[6 + g // 2][:, (g % 2) * 192:(g % 2) * 192 + 192], TOK[:, slot(t), SW + g * P:SW + (g + 1) * P],
                                         XW[u % 2][:, :, :].rearrange("p h e -> p (h e)")[:, g * 192:(g + 1) * 192], start=True, stop=True)
                    last.then_inc(st_mm, 1)
                    if u < NUC:
                        return
                    pe.wait_ge(st_v, u - 1)
                    if xi(u) >= 1:
                        pe.wait_ge(yo_v, xi(u))
                    for g in range(NG):
                        last = pe.matmul(ps[4 + g // 2][:, (g % 2) * 192:(g % 2) * 192 + 192], feat(t, 10 + g),
                                         Hs[d][:, g * 192:(g + 1) * 192], start=True, stop=True)
                    last.then_inc(yo_mm, 1)
                    pe.wait_ge(m_ok, xi(u) + 1)
                    pe.wait_ge(xd_ok, xi(u) + 1)
                    if xi(u) >= 1:
                        pe.wait_ge(yd_v, xi(u))
                    for h in range(NH):
                        last = pe.matmul(ps[2 + h // 6][:, (h % 6) * HD:(h % 6 + 1) * HD], M[:, h, :], XDT[:, h, :], start=True, stop=True)
                    last.then_inc(yd_mm, 1)

                for n in range(NT):
                    to_tokens(n)
                pe.wait_ge(pre, 5)
                pe.wait_ge(one, 1)
                pe.matmul(ps[6][:, 0:120], cst[:, C_UP:C_UP + P], dA[:, :, 0:NH], start=True, stop=True)
                pe.matmul(ps[6][:, 120:240], cst[:, C_LO:C_LO + P], dA[:, :, NH:24], start=True, stop=True)
                pe.matmul(ps[6][:, 240:480], ones[:, :], dA[:, :, :], start=True, stop=True).then_inc(csmm, 1)
                for u in range(NUC):
                    stage_b(u)
                for n in range(NT, NTT):
                    to_tokens(n)
                pe.wait_ge(ev_a, NTT)
                pe.wait_ge(ev_v, NTT)
                for u in range(NUC, NU + 1):
                    if u < NU:
                        stage_a(u)
                    if u > NUC:
                        stage_b(u - 1)

            @block.scalar
            def _(act):
                act.activation(W[:, 0, :], K.alog[:, :], ACT.Exp).then_inc(pre_a, 1)
                act.wait_ge(pre, 2)
                act.activation(ecs[:, :, :], dA[:, :, :], ACT.Exp)
                act.drain()
                act.activation(ecs[:, :, :], ecs[:, :, :], ACT.Ln, bias=1.0).then_inc(pre_a, 1)

                def to_tokens(n):
                    act.wait_ge(tr, n + 1)
                    for b in range(2):
                        last = act.activation(TOK[:, turns[n][1], b * 512:(b + 1) * 512], ps[3 * (n % 2) + b][:, :], ACT.Copy)
                    last.then_inc(ev_a, 1)

                for n in range(NT):
                    to_tokens(n)
                act.wait_ge(ready, 2)
                act.activation(ecs[:, :, :], cs[:, :, :], ACT.Exp)
                act.activation(W[:, :, :], W[:, :, :], ACT.Exp)
                act.activation(Eend[:, :, :], Eend[:, :, :], ACT.Exp).then_inc(pre_a, 1)
                for n in range(NT, NTT):
                    to_tokens(n)
                for u in range(NUC, NU):
                    act.wait_ge(a_v, 4 * xi(u) + 4)
                    act.activation(E[u % 2][:, :, :], E[u % 2][:, :, :], ACT.Relu, scale=-1.0)
                    act.drain()
                    act.activation(E[u % 2][:, :, :], E[u % 2][:, :, :], ACT.Exp, scale=-1.0).then_inc(e_ok, 1)

            @block.gpsimd
            def _(pool):
                pool.memset(ones[:, :], 1.0).then_inc(one, 1)
                for d in range(2):
                    last = pool.memset(Hs[d][:, :], 0.0)
                pool.drain()
                pool.wait_ge(ready, 3)
                pool.wait_ge(ev_a, NTC)
                pool.wait_ge(ev_v, NTC)
                for u, (d, t) in enumerate(units):
                    if u == NUC:
                        pool.wait_ge(ready, 4)
                        pool.wait_ge(ev_a, NTT)
                    xs = TOK[:, slot(t), 0:SW].rearrange("p (h e) -> p h e", e=HD)
                    if u >= 2:
                        pool.wait_ge(st_mm, u - 1)
                    pool.tensor_tensor(XW[u % 2][:, :, :], xs, per_head(W, d, t, HD), ALU.mult).then_inc(xw_ok, 1)
                    if u >= NUC:
                        if xi(u) >= 1:
                            pool.wait_ge(yd_mm, xi(u))
                        pool.tensor_tensor(XDT[:, :, :], xs, per_head(dt, d, t, HD), ALU.mult).then_inc(xd_ok, 1)
                        pool.wait_ge(yo_mm, xi(u) + 1)
                    if u >= 2:
                        pool.wait_ge(st_v, u - 1)
                    h3 = Hs[d][:, :].rearrange("p (h e) -> p h e", e=HD)
                    pool.tensor_tensor(h3, h3, per_head(Eend, d, t, HD), ALU.mult).then_inc(dec, 1)
                    if u >= NUC:
                        pool.wait_ge(yo_v, xi(u) + 1)
                        pool.wait_ge(yd_v, xi(u) + 1)
                        pool.tensor_tensor(Y[:, t, :], Y[:, t, :], tmp[:, :], ALU.add).then_inc(y2, 1)

            @block.vector
            def _(dve):
                n24 = [P, NTT, 24]
                dve.tensor_tensor(dt[:, :, :], K.dtr[:, :, :], K.dtb[:, :].unsqueeze(1).to_broadcast(n24), ALU.add).then_inc(pre, 1)
                dve.wait_ge(pre, 1)
                dve.scalar_tensor_tensor(out=dA[:, :, :], in0=dt[:, :, :], scalar=-1.0, in1=dt[:, :, :],
                                         op0=ALU.mult, op1=ALU.min).then_inc(pre, 1)
                dve.wait_ge(pre, 2)
                dve.tensor_single_scalar(dt[:, :, :], dt[:, :, :], 0.0, ALU.max).then_inc(pre, 1)
                dve.wait_ge(pre_a, 2)
                dve.wait_ge(pre, 3)
                dve.tensor_tensor(dt[:, :, :], dt[:, :, :], ecs[:, :, :], ALU.add).then_inc(pre, 1)
                dve.wait_ge(pre, 4)
                dve.scalar_tensor_tensor(out=dA[:, :, :], in0=dt[:, :, :], scalar=-1.0,
                                         in1=W[:, 0, :].unsqueeze(1).to_broadcast(n24), op0=ALU.mult, op1=ALU.mult).then_inc(pre, 1)

                def to_tokens(n):
                    dve.wait_ge(tr, n + 1)
                    dve.tensor_copy(TOK[:, turns[n][1], 1024:1280], ps[3 * (n % 2) + 2][:, 0:256]).then_inc(ev_v, 1)

                for n in range(NT):
                    to_tokens(n)
                dve.wait_ge(csmm, 1)
                for d in range(2):
                    dve.tensor_copy(cs[:, :, d * NH:(d + 1) * NH], ps[6][:, d * 120:d * 120 + 120].rearrange("p (t h) -> p t h", h=NH))
                dve.tensor_copy(Eend[:, :, :], ps[6][:, 240:480].rearrange("p (t h) -> p t h", h=24)).then_inc(ready, 1)
                dve.drain()
                dve.tensor_tensor(W[:, :, :], Eend[:, :, :], cs[:, :, :], ALU.subtract).then_inc(ready, 1)
                dve.wait_ge(pre_a, 3)
                dve.tensor_tensor(W[:, :, :], W[:, :, :], dt[:, :, :], ALU.mult).then_inc(ready, 1)
                def stage_a(u):
                    d, t = units[u]
                    for b in range(4):
                        n = 4 * xi(u) + b
                        dve.wait_ge(a_mm, n + 1)
                        if b == 0:
                            tri = cst[:, (C_UP, C_LO)[d]:(C_UP, C_LO)[d] + P].unsqueeze(1).to_broadcast([P, NG, P])
                            dve.tensor_tensor(SCM[u % 2], ps[n % 2][:, :].rearrange("p (g q) -> p g q", q=P), tri, ALU.mult).then_inc(a_v, 1)
                        else:
                            h = 4 * (b - 1)
                            dve.tensor_tensor(E[u % 2][:, h:h + 4, :], ps[n % 2][:, :].rearrange("p (g q) -> p g q", q=P),
                                              cs[:, t, d * NH + h:d * NH + h + 4].unsqueeze(2).to_broadcast([P, 4, P]), ALU.subtract).then_inc(a_v, 1)

                def state(u):
                    d, t = units[u]
                    dve.wait_ge(st_mm, u + 1)
                    dve.wait_ge(dec, u + 1)
                    for b in range(2):
                        last = dve.tensor_tensor(Hs[d][:, b * 384:(b + 1) * 384], ps[6 + b][:, 0:384], Hs[d][:, b * 384:(b + 1) * 384], ALU.add)
                    last.then_inc(st_v, 1)

                def stage_b(u):
                    d, t = units[u]
                    dve.wait_ge(e_ok, xi(u) + 1)
                    if xi(u) >= 1:
                        dve.wait_ge(yd_mm, xi(u))
                    dve.tensor_tensor(M[:, :, :].rearrange("p (g r) q -> p g r q", r=HPG), E[u % 2][:, :, :].rearrange("p (g r) q -> p g r q", r=HPG),
                                      SCM[u % 2].unsqueeze(2).to_broadcast([P, NG, HPG, P]), ALU.mult).then_inc(m_ok, 1)
                    dve.wait_ge(yo_mm, xi(u) + 1)
                    if xi(u) >= 1:
                        dve.wait_ge(y2, xi(u))
                    for b in range(2):
                        last = dve.tensor_tensor(tmp[:, b * 384:(b + 1) * 384].rearrange("p (h e) -> p h e", e=HD),
                                                 ps[4 + b][:, 0:384].rearrange("p (h e) -> p h e", e=HD),
                                                 ecs[:, t, d * NH + 6 * b:d * NH + 6 * b + 6].unsqueeze(2).to_broadcast([P, 6, HD]), ALU.mult)
                    last.then_inc(yo_v, 1)
                    state(u)
                    dve.wait_ge(yd_mm, xi(u) + 1)
                    for b in range(2):
                        last = dve.tensor_tensor(Y[:, t, b * 384:(b + 1) * 384], ps[2 + b][:, 0:384], Y[:, t, b * 384:(b + 1) * 384], ALU.add)
                    last.then_inc(yd_v, 1)

                for u in range(NUC):
                    state(u)
                for n in range(NT, NTT):
                    to_tokens(n)
                dve.wait_ge(ev_a, NTT)
                for t in range(NT):
                    last = dve.tensor_tensor(Y[:, t, :].rearrange("p (h e) -> p h e", e=HD), TOK[:, t, 0:SW].rearrange("p (h e) -> p h e", e=HD),
                                             K.dskip[:, :].unsqueeze(2).to_broadcast([P, NH, HD]), ALU.mult)
                last.then_inc(ready, 1)
                for u in range(NUC, NU + 1):
                    if u < NU:
                        stage_a(u)
                    if u > NUC:
                        stage_b(u - 1)


def mixer_output(nc, K, A):
    Y, ZT, V, HT, X, ps = K.Y, K.ZT, K.V, K.HT, K.X, K.ps
    ident = K.cst[:, C_ID:C_ID + P]
    wo = K.XF[:, 6:14, :]
    NJ = SW // P
    with ExitStack() as ctx:
        def sb(n, s, d=F32):
            return ctx.enter_context(nc.sbuf_tensor("mo_" + n, s, d))

        dft = sb("dft", [P, 2, 2, L])
        junk = sb("junk", [P, D])
        st = sb("st", [P, 3, NT])
        xin = sb("xin", [P, 2, D])
        dft_in = [K.sem(f"mo_dft{s}") for s in range(2)]
        x_in = [K.sem(f"mo_x{s}") for s in range(2)]
        (wo_in, four, gat, sq, sqd, rt, inv, nrm, tr, eva, evv, f_ev, mm, cpy, sq2, var2, rt2, fin, addd) = (K.sem("mo_" + n) for n in (
            "woin", "four", "gat", "sq", "sqd", "rt", "inv", "nrm", "tr", "eva", "evv", "fev", "mm", "cpy", "sq2", "var2", "rt2", "fin", "addd"))
        dft_dram = A["dft"].rearrange("(t p) c k -> t p (c k)", p=P)

        with nc.Block() as block:
            @block.sync
            def _(sp):
                for t in range(NT):
                    if t >= 2:
                        sp.wait_ge(four, t - 1)
                    sp.dma_start(dft[:, t % 2], dft_dram[t]).then_inc(dft_in[t % 2], 16)
                    if t == 1:
                        sp.dma_start(wo, A["w_out"][0].rearrange("(k p) n -> p k n", p=P)).then_inc(wo_in, 16)
                for t in range(NT):
                    if t >= 2:
                        sp.wait_ge(addd, t - 1)
                    sp.dma_start(xin[:, t % 2], A["x"][0, t * P:(t + 1) * P, :]).then_inc(x_in[t % 2], 16)

            @block.tensor
            def _(pe):
                for t in range(NT):
                    pe.wait_ge(dft_in[t % 2], 16 * (t // 2 + 1))
                    for m in range(2):
                        for c in range(2):
                            for h in range(2):
                                last = pe.matmul(ps[2 * m + h][:, :], V[:, t, m * 256 + c * P:m * 256 + (c + 1) * P],
                                                 dft[:, t % 2, c, h * 512:(h + 1) * 512], start=t == 0 and c == 0, stop=t == NT - 1 and c == 1)
                    last.then_inc(four, 1)
                for g in range(2 * NJ):
                    j, half = g // 2, g % 2
                    if g >= 4:
                        pe.wait_ge(eva if g % 2 == 0 else evv, (g - 4) // 2 + 1)
                    pe.wait_ge(nrm, 4 * half + 4)
                    for i in range(4):
                        last = pe.transpose(ps[4 + g % 4][:, i * P:(i + 1) * P], Y[:, 4 * half + i, j * P:(j + 1) * P], ident)
                    last.then_inc(tr, 1)
                pe.wait_ge(wo_in, 16)
                pe.wait_ge(f_ev, 4)
                pe.wait_ge(eva, NJ)
                pe.wait_ge(evv, NJ)
                for t in range(NT):
                    if t >= 4:
                        pe.wait_ge(cpy, t - 3)
                    for h in range(2):
                        for k in range(KD):
                            last = pe.matmul(ps[2 * (t % 4) + h][:, :], HT[:, k, t * P:(t + 1) * P], wo[:, k, h * 512:(h + 1) * 512],
                                             start=k == 0, stop=k == KD - 1)
                    last.then_inc(mm, 1)

            @block.scalar
            def _(act):
                for t in range(NT):
                    act.wait_ge(gat, t + 1)
                    act.activation(junk[:, 0:SW], Y[:, t, :], ACT.Square, accum_out=st[:, 0, t:t + 1]).then_inc(sq, 1)
                    act.drain()
                act.wait_ge(sqd, 1)
                act.activation(st[:, 1, :], st[:, 0, :], ACT.Sqrt).then_inc(rt, 1)
                act.wait_ge(four, NT)
                for n in range(4):
                    act.activation(HT[:, n // 2, (n % 2) * 512:(n % 2) * 512 + 512], ps[n][:, :], ACT.Copy).then_inc(f_ev, 1)
                for g in range(0, 2 * NJ, 2):
                    act.wait_ge(tr, g + 1)
                    act.activation(HT[:, 2 + g // 2, 0:512], ps[4 + g % 4][:, :], ACT.Identity,
                                   scale=K.cols[:, COL_GSSD + g // 2:COL_GSSD + g // 2 + 1], bias=0.0).then_inc(eva, 1)
                for t in range(NT + 1):
                    if t < NT:
                        act.wait_ge(cpy, t + 1)
                        act.activation(junk[:, :], X[:, t, :], ACT.Square, accum_out=st[:, 2, t:t + 1]).then_inc(sq2, 1)
                        act.drain()
                        act.wait_ge(var2, t + 1)
                        act.activation(st[:, 1, t:t + 1], st[:, 0, t:t + 1], ACT.Sqrt).then_inc(rt2, 1)
                    if t >= 1:
                        act.wait_ge(addd, t)
                        act.activation(junk[:, :], X[:, t - 1, :], ACT.Square, accum_out=K.x_ss[:, t - 1:t])
                        act.drain()

            @block.vector
            def _(dve):
                for t in range(NT):
                    dve.tensor_tensor(Y[:, t, :], Y[:, t, :], ZT[:, t, :], ALU.mult).then_inc(gat, 1)
                dve.wait_ge(sq, NT)
                dve.tensor_scalar(st[:, 0, :], st[:, 0, :], 1.0 / SW, EPS, ALU.mult, ALU.add).then_inc(sqd, 1)
                dve.wait_ge(rt, 1)
                dve.reciprocal(st[:, 1, :], st[:, 1, :]).then_inc(inv, 1)
                dve.wait_ge(inv, 1)
                for t in range(NT):
                    dve.tensor_scalar(Y[:, t, :], Y[:, t, :], st[:, 1, t:t + 1], None, ALU.mult).then_inc(nrm, 1)
                for g in range(1, 2 * NJ, 2):
                    dve.wait_ge(tr, g + 1)
                    dve.tensor_scalar(HT[:, 2 + g // 2, 512:1024], ps[4 + g % 4][:, :],
                                      K.cols[:, COL_GSSD + g // 2:COL_GSSD + g // 2 + 1], None, ALU.mult).then_inc(evv, 1)
                for t in range(NT):
                    dve.wait_ge(mm, t + 1)
                    for h in range(2):
                        last = dve.tensor_copy(X[:, t, h * 512:(h + 1) * 512], ps[2 * (t % 4) + h][:, :])
                    last.then_inc(cpy, 1)
                    dve.wait_ge(sq2, t + 1)
                    dve.tensor_scalar(st[:, 0, t:t + 1], st[:, 2, t:t + 1], 1.0 / D, EPS, ALU.mult, ALU.add).then_inc(var2, 1)
                    dve.wait_ge(rt2, t + 1)
                    dve.reciprocal(st[:, 1, t:t + 1], st[:, 1, t:t + 1]).then_inc(inv, 1)
                    dve.wait_ge(inv, t + 2)
                    dve.scalar_tensor_tensor(out=X[:, t, :], in0=X[:, t, :], scalar=st[:, 1, t:t + 1], in1=K.G1[:, :],
                                             op0=ALU.mult, op1=ALU.mult).then_inc(fin, 1)

            @block.gpsimd
            def _(pool):
                for t in range(NT):
                    pool.wait_ge(fin, t + 1)
                    pool.wait_ge(x_in[t % 2], 16 * (t // 2 + 1))
                    pool.tensor_tensor(X[:, t, :], X[:, t, :], xin[:, t % 2, :], ALU.add).then_inc(addd, 1)


def load_gate_up(sp, A, w_raw, w_in, i, s, free=None):
    for j, name in enumerate(("w_gate", "w_up")):
        if free:
            free(j)
        src = A[name][0].rearrange("(k p) n -> p k n", p=P)
        sp.dma_start(w_raw[j][:, :, :], src[:, :, ds(i * 2 * P + s * P, P)]).then_inc(w_in[j], 16)


def gate_up(nc, K, A, HH, HL, w_raw, w_in, mid, d_raw, d_in):
    ps = K.ps
    UNITS = 2 * KF
    wd_dram = A["w_down"][0].rearrange("(f p) n -> p f n", p=P)
    with ExitStack() as ctx:
        def sb(n, s, d=F32):
            return ctx.enter_context(nc.sbuf_tensor("gu_" + n, s, d))

        w_hi = [sb(f"hi{j}", [P, KD, P], F32R) for j in range(2)]
        w_lo = [sb(f"lo{j}", [P, KD, P], F32R) for j in range(2)]
        u_hi, u_lo, u_mm = (K.sem("gu_" + n) for n in ("uhi", "ulo", "umm"))
        gate = [K.sem(f"gu_gate{s}") for s in range(2)]
        up = [K.sem(f"gu_up{s}") for s in range(2)]

        with nc.Block() as block:
            @block.sync
            def _(sp):
                load_gate_up(sp, A, w_raw, w_in, 0, 1, lambda j: sp.wait_ge(u_lo, j + 3))
                with sp.Fori(1, KF // 2) as i:
                    load_gate_up(sp, A, w_raw, w_in, i, 0, lambda j: sp.wait_ge(u_lo, i * 4 + (j + 1)))
                    load_gate_up(sp, A, w_raw, w_in, i, 1, lambda j: sp.wait_ge(u_lo, i * 4 + (j + 3)))
                for f in range(4):
                    sp.dma_start(d_raw[f], wd_dram[:, f:f + 1, :]).then_inc(d_in[f], 16)

            @block.tensor
            def _(pe):
                pe.sem_inc(u_mm, 2)
                with pe.Fori(0, KF // 2) as i:
                    for s in range(2):
                        for j in range(2):
                            pe.wait_ge(u_lo, i * 4 + (2 * s + j + 3))
                            if j == 0:
                                pe.wait_ge(gate[s], i + 1)
                                pe.wait_ge(up[s], i + 1)
                            for k in range(KD):
                                for w, x, n in ((w_hi, HH, 0), (w_hi, HL, 1), (w_lo, HH, 2)):
                                    for h in range(2):
                                        last = pe.matmul(ps[4 * s + 2 * j + h][:, :], w[j][:, k, :], x[:, k, h * 512:(h + 1) * 512],
                                                         start=k == 0 and n == 0, stop=k == KD - 1 and n == 2)
                            last.then_inc(u_mm, 1)

            @block.scalar
            def _(act):
                for s in range(2):
                    act.sem_inc(gate[s], 1)

                def split(i, s, j):
                    act.wait_ge(w_in[j], i * 32 + (16 * s + 16))
                    act.wait_ge(u_mm, i * 4 + (2 * s + j + 1))
                    act.activation(w_hi[j][:, :, :], w_raw[j][:, :, :], ACT.Copy).then_inc(u_hi, 1)

                def tile(i, s, more=True):
                    if more:
                        split(i + s, 1 - s, 0)
                    act.wait_ge(u_mm, i * 4 + (2 * s + 3))
                    for h in range(2):
                        last = act.activation(mid[:, ds(i * 2 + s, 1), h * 512:(h + 1) * 512], ps[4 * s + h][:, :].unsqueeze(1), ACT.Silu)
                    last.then_inc(gate[s], 1)
                    if more:
                        split(i + s, 1 - s, 1)

                split(0, 0, 0)
                split(0, 0, 1)
                with act.Fori(0, KF // 2 - 1) as i:
                    for s in range(2):
                        tile(i, s)
                for s in range(2):
                    tile(KF // 2 - 1, s, s == 0)

            @block.vector
            def _(dve):
                for s in range(2):
                    dve.sem_inc(up[s], 1)
                dve.sem_inc(u_lo, 2)

                def split(i, s, j):
                    dve.wait_ge(u_hi, i * 4 + (2 * s + j + 1))
                    dve.tensor_tensor(w_lo[j][:, :, :], w_raw[j][:, :, :], w_hi[j][:, :, :].bitcast(F32), ALU.subtract).then_inc(u_lo, 1)

                def tile(i, s, more=True):
                    if more:
                        split(i + s, 1 - s, 0)
                    dve.wait_ge(gate[s], i + 2)
                    dve.wait_ge(u_mm, i * 4 + (2 * s + 4))
                    for h in range(2):
                        m = mid[:, ds(i * 2 + s, 1), h * 512:(h + 1) * 512]
                        last = dve.tensor_tensor(m, m, ps[4 * s + 2 + h][:, :].unsqueeze(1), ALU.mult)
                    last.then_inc(up[s], 1)
                    if more:
                        split(i + s, 1 - s, 1)

                split(0, 0, 0)
                split(0, 0, 1)
                with dve.Fori(0, KF // 2 - 1) as i:
                    for s in range(2):
                        tile(i, s)
                for s in range(2):
                    tile(KF // 2 - 1, s, s == 0)


def down(nc, K, A, mid, d_raw, d_in):
    ps, X = K.ps, K.X
    GRP, HALFL = 4, 512
    wd_dram = A["w_down"][0].rearrange("(f p) n -> p f n", p=P)
    with ExitStack() as ctx:
        def sb(n, s, d=F32):
            return ctx.enter_context(nc.sbuf_tensor("dn_" + n, s, d))

        dh = [sb(f"dh{s}", [P, D], F32R) for s in range(4)]
        dl = [sb(f"dl{s}", [P, D], F32R) for s in range(4)]
        mh = [sb(f"mh{s}", [P, 1, HALFL], F32R) for s in range(4)]
        ml = [sb(f"ml{s}", [P, 1, HALFL], F32R) for s in range(4)]
        T = sb("T", [P, 2, D])
        st = sb("st", [P, 4, NT])
        junk = K.G1
        prod, d_hi, d_lo, x_in, sq, var, rt, inv, fin, scl = (K.sem("dn_" + n) for n in (
            "prod", "dhi", "dlo", "xin", "sq", "var", "rt", "inv", "fin", "scl"))

        def steps(eng, body, q, first, last):
            def one(f, i, s):
                body(q, f, i * 4 + (q * KF + s), (q * KF + s) % 4, i + (q * KF + s) // 4)

            f = first
            while f < last:
                if f == 4 and last == KF:
                    with eng.Fori(0, (KF - 6) // 4) as i:
                        for s in range(4):
                            one(i * 4 + (4 + s), i, 4 + s)
                    f = KF - 2
                one(f, 0, f)
                f += 1

        with nc.Block() as block:
            @block.sync
            def _(sp):
                sp.dma_start(X, K.xrow.rearrange("(t p) n -> p t n", p=P)).then_inc(x_in, 16)

                def load(q, f, n, slot, occ):
                    sp.wait_ge(d_lo, n + (-3))
                    sp.dma_start(d_raw[slot], wd_dram[:, ds(f, 1), :]).then_inc(d_in[slot], 16)

                steps(sp, load, 0, 4, KF)
                steps(sp, load, 1, 0, KF)

            @block.tensor
            def _(pe):
                pe.sem_inc(prod, 4)

                def product(q, f, n, slot, occ):
                    first, last = isinstance(f, int) and f == 0, isinstance(f, int) and f == KF - 1
                    pe.wait_ge(d_lo, n + 1)
                    for t in range(GRP):
                        if q == 1 and first:
                            pe.wait_ge(fin, t + 1)
                        for m, w, z in ((mh, dh, 0), (mh, dl, 1), (ml, dh, 2)):
                            for h in range(2):
                                done = pe.matmul(ps[2 * t + h][:, :], m[slot][:, 0, t * P:(t + 1) * P], w[slot][:, h * 512:(h + 1) * 512],
                                                 start=first and z == 0, stop=last and z == 2)
                    done.then_inc(prod, 1)

                steps(pe, product, 0, 0, KF)
                steps(pe, product, 1, 0, KF)

            @block.scalar
            def _(act):
                def split(q, f, n, slot, occ):
                    act.wait_ge(d_in[slot], occ * 16 + 16)
                    act.wait_ge(prod, n + 1)
                    act.activation(dh[slot][:, :], d_raw[slot][:, 0, :], ACT.Copy)
                    act.activation(mh[slot][:, :, :], mid[:, ds(f, 1), q * HALFL:(q + 1) * HALFL], ACT.Copy).then_inc(d_hi, 1)

                def square_sums(q):
                    act.wait_ge(prod, KF * (q + 1) + 4)
                    for t in range(q * GRP, (q + 1) * GRP):
                        for h in range(2):
                            act.activation(junk[:, h * 512:(h + 1) * 512], ps[2 * (t % GRP) + h][:, :], ACT.Square, accum_out=st[:, h, t:t + 1])
                        act.drain()
                        act.sem_inc(sq, 1)
                        act.wait_ge(var, 2 * t + 2)
                        act.activation(st[:, 3, t:t + 1], st[:, 2, t:t + 1], ACT.Sqrt).then_inc(rt, 1)

                steps(act, split, 0, 0, KF)
                steps(act, split, 1, 0, 4)
                square_sums(0)
                steps(act, split, 1, 4, KF)
                square_sums(1)

            @block.vector
            def _(dve):
                def split(q, f, n, slot, occ):
                    dve.wait_ge(d_hi, n + 1)
                    dve.tensor_tensor(dl[slot][:, :], d_raw[slot][:, 0, :], dh[slot][:, :].bitcast(F32), ALU.subtract)
                    dve.tensor_tensor(ml[slot][:, :, :], mid[:, ds(f, 1), q * HALFL:(q + 1) * HALFL], mh[slot][:, :, :].bitcast(F32), ALU.subtract).then_inc(d_lo, 1)

                def finish(q):
                    for t in range(q * GRP, (q + 1) * GRP):
                        dve.wait_ge(sq, t + 1)
                        dve.tensor_tensor(st[:, 2, t:t + 1], st[:, 0, t:t + 1], st[:, 1, t:t + 1], ALU.add).then_inc(var, 1)
                        dve.wait_ge(var, 2 * t + 1)
                        dve.tensor_scalar(st[:, 2, t:t + 1], st[:, 2, t:t + 1], 1.0 / D, EPS, ALU.mult, ALU.add).then_inc(var, 1)
                        dve.wait_ge(rt, t + 1)
                        dve.reciprocal(st[:, 3, t:t + 1], st[:, 3, t:t + 1]).then_inc(inv, 1)
                        dve.wait_ge(inv, t + 1)
                        if t >= 2:
                            dve.wait_ge(scl, t - 1)
                        for h in range(2):
                            last = dve.scalar_tensor_tensor(out=T[:, t % 2, h * 512:(h + 1) * 512], in0=ps[2 * (t % GRP) + h][:, :],
                                                            scalar=st[:, 3, t:t + 1], in1=K.G2[:, h * 512:(h + 1) * 512], op0=ALU.mult, op1=ALU.mult)
                        last.then_inc(fin, 1)

                steps(dve, split, 0, 0, KF)
                steps(dve, split, 1, 0, 4)
                finish(0)
                steps(dve, split, 1, 4, KF)
                finish(1)

            @block.gpsimd
            def _(pool):
                pool.wait_ge(x_in, 16)
                for t in range(NT):
                    pool.wait_ge(fin, t + 1)
                    pool.tensor_tensor(X[:, t, :], X[:, t, :], T[:, t % 2, :], ALU.add).then_inc(scl, 1)


def first_block(nc, K, A, lasting):
    with ExitStack() as ctx, ExitStack() as x_ctx, ExitStack() as h_ctx, ExitStack() as mid_ctx:
        def right(stack, n, s, d=F32):
            return stack.enter_context(nc.sbuf_tensor(n, s, d, side="right"))

        K.x_ss = right(ctx, "x_ss", [P, NT])
        K.G1, K.G2 = right(ctx, "G1", [P, D]), right(ctx, "G2", [P, D])
        xreg = right(x_ctx, "x1", [P, 10 * D])
        K.XC = xreg[:, :].rearrange("p (t n) -> p t n", n=D)
        K.X = K.XC[:, 0:NT, :]
        K.ZT = xreg[:, 0:NT * SW].rearrange("p (t n) -> p t n", n=SW)
        K.V = xreg[:, NT * SW:NT * SW + NT * 512].rearrange("p (t n) -> p t n", n=512)
        hreg = right(h_ctx, "h1", [P, 10 * D])
        K.HT = hreg[:, 0:KD * L].rearrange("p (k t) -> p k t", t=L)
        K.HTc = hreg[:, KD * L:KD * L + KD * LC].rearrange("p (k t) -> p k t", t=LC)
        K.TOK = hreg[:, :].rearrange("p (t n) -> p t n", n=SW + 512)
        modulation(nc, K, A)

        with ExitStack() as ssd_ctx:
            def sb2(n, s, d=F32):
                return ssd_ctx.enter_context(nc.sbuf_tensor(n, s, d))

            K.XF, K.XFc = sb2("XF", [P, NCV, L]), sb2("XFc", [P, 10, LC])
            K.dtr, K.dtb, K.alog, K.dskip = sb2("dtr", [P, NT + NTC, 24]), sb2("dtb", [P, 24]), sb2("alog", [P, 24]), sb2("dskip", [P, NH])
            projection_weights(K)
            rms_to_feature_major(nc, K, "pre", None, K.XC, [(0, NT, K.HT, K.A1, K.B1), (NT, NTC, K.HTc, K.A1c, K.B1c)],
                                 ahead=lambda sp: load_projection_weights(sp, K, A))
            projections(nc, K, A)
            ssd(nc, K, A)
            mixer_output(nc, K, A)
        h_ctx.close()
        with ExitStack() as h_split:
            HH, HL = (h_split.enter_context(nc.sbuf_tensor(n, [P, KD, L], F32R)) for n in ("h_hi", "h_lo"))
            w_raw = [h_split.enter_context(nc.sbuf_tensor(f"gu_raw{j}", [P, KD, P], F32)) for j in range(2)]
            w_in = [K.sem(f"gu_w{j}") for j in range(2)]
            with nc.sbuf_tensor("ffn_norm", [P, NT, D], F32) as xn:
                rms_to_feature_major(nc, K, "ffn", K.X, xn, [(0, NT, None, K.A2, K.B2)], store=K.xrow, split=(HH, HL), sums=K.x_ss,
                                     ahead=lambda sp: load_gate_up(sp, A, w_raw, w_in, 0, 0))
            x_ctx.close()
            mid = right(mid_ctx, "mid", [P, KF, L])
            d_raw = [right(mid_ctx, f"draw{s}", [P, 1, D])[:, :, :] for s in range(4)]
            d_in = [K.sem(f"dn_in{s}") for s in range(4)]
            gate_up(nc, K, A, HH, HL, w_raw, w_in, mid, d_raw, d_in)
        K.X = lasting.enter_context(nc.sbuf_tensor("x2", [P, NT, D], F32))[:, :, :]
        down(nc, K, A, mid, d_raw, d_in)


def layer_norm(nc, K, A, tag, i, j, store, transpose=True, combine=False, router=None):
    X, HT, ps = K.X, K.HT, K.ps
    NR = 8 + NE
    with ExitStack() as ctx:
        def sb(n, s, d=F32):
            return ctx.enter_context(nc.sbuf_tensor(tag + n, s, d))

        g, b = sb("g", [P, D]), sb("b", [P, D])
        stats = sb("stats", [P, NT, 2, 6])
        mv = sb("mv", [P, NT, 2])
        sd, nm = sb("sd", [P, NT]), sb("nm", [P, NT])
        NY = 3
        y = sb("y", [P, NY, 2, D]) if combine else None
        wr = sb("wr", [P, KD, NR]) if router is not None else None
        gb_in, var, root, rstd, normed, scaled, bd, stored, tr, ev, g0, used, wr_in, lg = (K.sem(tag + n) for n in (
            "gb_in", "var", "root", "rstd", "normed", "scaled", "bd", "stored", "tr", "ev", "g0", "used", "wr_in", "lg"))
        y_in = [K.sem(tag + f"y_in{s}") for s in range(NY)]

        with nc.Block() as block:
            @block.sync
            def _(sp):
                if combine:
                    src = K.yrow.rearrange("(t p c) n -> t p c n", p=P, c=2)
                    for t in range(NY):
                        sp.dma_start(y[:, t], src[t]).then_inc(y_in[t], 16)
                sp.dma_start(g[:, :], A["ln_g_2"][i, j:j + 1, :].to_broadcast([P, D])).then_inc(gb_in, 16)
                sp.dma_start(b[:, :], A["ln_b_2"][i, j:j + 1, :].to_broadcast([P, D])).then_inc(gb_in, 16)
                if router is not None:
                    sp.dma_start(wr[:, :, 0:8], A["moe_w_grp_2"][router].rearrange("(k p) n -> p k n", p=P)).then_inc(wr_in, 16)
                    sp.dma_start(wr[:, :, 8:NR], A["moe_w_exp_2"][router].rearrange("(k p) n -> p k n", p=P)).then_inc(wr_in, 16)
                for t in range(NT):
                    if combine and t + NY < NT:
                        sp.wait_ge(used, t + 1)
                        sp.dma_start(y[:, t % NY], src[t + NY]).then_inc(y_in[t % NY], 16)
                    if store is not None and t >= 2:
                        sp.wait_ge(bd, t - 1)
                        sp.dma_start(store[(t - 2) * P:(t - 1) * P, :], X[:, t - 2, :]).then_inc(stored, 16)
                if store is not None:
                    for t in range(NT - 2, NT):
                        sp.wait_ge(bd, t + 1)
                        sp.dma_start(store[t * P:(t + 1) * P, :], X[:, t, :]).then_inc(stored, 16)
                    sp.wait_ge(stored, 16 * NT)

            @block.vector
            def _(dve):
                def moments(t):
                    if combine:
                        dve.wait_ge(g0, t + 1)
                        dve.scalar_tensor_tensor(out=X[:, t, :], in0=X[:, t, :], scalar=ALPHA, in1=y[:, t % NY, 0, :], op0=ALU.mult, op1=ALU.add)
                        dve.drain()
                        dve.scalar_tensor_tensor(out=X[:, t, :], in0=y[:, t % NY, 1, :], scalar=K.GT[:, 1, t:t + 1], in1=X[:, t, :],
                                                 op0=ALU.mult, op1=ALU.add).then_inc(used, 1)
                        dve.drain()
                    for h in range(2):
                        dve.bn_stats(stats[:, t, h, :], X[:, t, h * 512:(h + 1) * 512])
                    dve.drain()
                    dve.bn_aggr(mv[:, t, :], stats[:, t, :, :].rearrange("p h c -> p (h c)"))
                    dve.drain()
                    dve.tensor_single_scalar(mv[:, t, 1:2], mv[:, t, 1:2], LN_EPS, ALU.add).then_inc(var, 1)

                def reciprocal(t):
                    dve.wait_ge(root, t + 1)
                    dve.reciprocal(sd[:, t:t + 1], sd[:, t:t + 1])
                    dve.drain()
                    dve.scalar_tensor_tensor(out=nm[:, t:t + 1], in0=mv[:, t, 0:1], scalar=-1.0, in1=sd[:, t:t + 1], op0=ALU.mult, op1=ALU.mult).then_inc(rstd, 1)

                def add_bias(t):
                    dve.wait_ge(scaled, t + 1)
                    dve.tensor_tensor(X[:, t, :], X[:, t, :], b[:, :], ALU.add).then_inc(bd, 1)

                for t in range(NT + 2):
                    if t < NT:
                        moments(t)
                    if 1 <= t <= NT:
                        reciprocal(t - 1)
                    if t == 2:
                        dve.wait_ge(gb_in, 32)
                    if t >= 2:
                        add_bias(t - 2)

            @block.gpsimd
            def _(pool):
                pool.wait_ge(gb_in, 32)
                for t in range(NT):
                    pool.wait_ge(normed, t + 1)
                    pool.tensor_tensor(X[:, t, :], X[:, t, :], g[:, :], ALU.mult).then_inc(scaled, 1)

            @block.scalar
            def _(act):
                def copy_turned(t):
                    for h in range(2):
                        n = 2 * t + h
                        act.wait_ge(tr, n + 1)
                        act.activation(HT[:, 4 * h:4 * h + 4, t * P:(t + 1) * P], ps[n % 4][:, :].rearrange("p (k q) -> p k q", q=P), ACT.Copy).then_inc(ev, 1)

                def gate(t):
                    act.wait_ge(y_in[t % NY], 16 * (t // NY + 1))
                    act.activation(y[:, t % NY, 0, :], y[:, t % NY, 0, :], ACT.Identity, scale=K.GT[:, 0, t:t + 1], bias=0.0).then_inc(g0, 1)

                if combine:
                    gate(0)
                for t in range(NT + 3):
                    if combine and t + 1 < NT:
                        gate(t + 1)
                    if t < NT:
                        act.wait_ge(var, t + 1)
                        act.activation(sd[:, t:t + 1], mv[:, t, 1:2], ACT.Sqrt).then_inc(root, 1)
                    if 1 <= t <= NT:
                        u = t - 1
                        act.wait_ge(rstd, u + 1)
                        act.activation(X[:, u, :], X[:, u, :], ACT.Identity, scale=sd[:, u:u + 1], bias=nm[:, u:u + 1]).then_inc(normed, 1)
                    if transpose and t >= 3:
                        copy_turned(t - 3)

            @block.tensor
            def _(pe):
                def logits(t):
                    if t == 0:
                        pe.wait_ge(wr_in, 32)
                    pe.wait_ge(ev, 2 * t + 2)
                    for k in range(KD):
                        last = pe.matmul(ps[4 + t // 4][:, (t % 4) * NR:(t % 4 + 1) * NR], HT[:, k, t * P:(t + 1) * P], wr[:, k, :],
                                         start=k == 0, stop=k == KD - 1)
                    last.then_inc(lg, 1)

                if transpose:
                    for t in range(NT):
                        pe.wait_ge(bd, t + 1)
                        if t >= 2:
                            pe.wait_ge(ev, 2 * t - 2)
                        for h in range(2):
                            for k in range(4):
                                last = pe.transpose(ps[(2 * t + h) % 4][:, k * P:(k + 1) * P], X[:, t, (4 * h + k) * P:(4 * h + k + 1) * P], K.cst[:, C_ID:C_ID + P])
                            last.then_inc(tr, 1)
                        if router is not None and t >= 1:
                            logits(t - 1)
                    if router is not None:
                        logits(NT - 1)


def latents(nc, K, A):
    X, HT, ps, cst = K.X, K.HT, K.ps, K.cst
    ident = cst[:, C_ID:C_ID + P]
    TWO_PI_HI = 6.28125
    TWO_PI_LO = 2 * np.pi - TWO_PI_HI
    PI = 3.1415925
    with ExitStack() as ctx:
        def sb(n, s, d=F32):
            return ctx.enter_context(nc.sbuf_tensor("la_" + n, s, d))

        w = sb("w", [P, KD, LAT])
        lat = sb("lat", [P, NT, LAT])
        T3, KR = sb("T3", [P, NT, P]), sb("KR", [P, NT, P])
        junk = sb("junk", [P, QL])
        ss = sb("ss", [P, 2, NT])
        posr, posi = sb("posr", [NT, P]), sb("posi", [NT, P], I32)
        pos = sb("pos", [P, NT])
        ang, turn, co, si, tm = (sb(n, [P, NT, 16]) for n in ("ang", "turn", "co", "si", "tm"))
        ki = sb("ki", [P, NT, 16], I32)
        (w_in, p_in, pr, tr0, ev0, mm, ev, sq, var, rt, rc, nm, rope, sins, tr, eva, evv, vmm, ve, one) = (K.sem("la_" + n) for n in (
            "w_in", "p_in", "pr", "tr0", "ev0", "mm", "ev", "sq", "var", "rt", "rc", "nm", "rope", "sins", "tr", "eva", "evv", "vmm", "ve", "one"))
        src = [(lat, 0), (lat, P), (lat, QL), (KR, 0), (T3, 0)]

        with nc.Block() as block:
            @block.sync
            def _(sp):
                sp.dma_start(posi[:, :], A["positions_2"][0].rearrange("(a p) -> a p", p=P)).then_inc(p_in, 16)
                sp.dma_start(w[:, :, :], A["mla_w_in_2"][0].rearrange("(k p) n -> p k n", p=P)).then_inc(w_in, 16)
                sp.dma_start(K.WKV[:, :, :], A["mla_w_ukv_2"][0].rearrange("p (h n) -> p h n", n=P)).then_inc(w_in, 16)

            @block.tensor
            def _(pe):
                for n in range(2 * NT):
                    t, h = n // 2, n % 2
                    if n >= 4:
                        pe.wait_ge(ev0, n - 3)
                    for k in range(4):
                        last = pe.transpose(ps[n % 4][:, k * P:(k + 1) * P], X[:, t, (4 * h + k) * P:(4 * h + k + 1) * P], ident)
                    last.then_inc(tr0, 1)
                pe.wait_ge(pr, 1)
                pe.transpose(ps[6][:, 0:NT], posr[:, :], ident[0:NT, 0:NT]).then_inc(pr, 1)
                pe.wait_ge(w_in, 32)
                for t in range(NT):
                    pe.wait_ge(ev0, 2 * t + 2)
                    if t >= 2:
                        pe.wait_ge(ev, t - 1)
                    for k in range(KD):
                        last = pe.matmul(ps[4 + t % 2][:, 0:LAT], HT[:, k, t * P:(t + 1) * P], w[:, k, :], start=k == 0, stop=k == KD - 1)
                    last.then_inc(mm, 1)
                pe.wait_ge(nm, 2)
                pe.wait_ge(rope, 1)
                for n in range(10):
                    s, c = src[n // 2]
                    if n >= 4:
                        pe.wait_ge(eva if n % 2 == 0 else evv, (n - 4) // 2 + 1)
                    for i in range(4):
                        last = pe.transpose(ps[n % 4][:, i * P:(i + 1) * P], s[:, 4 * (n % 2) + i, c:c + P], ident)
                    last.then_inc(tr, 1)
                pe.wait_ge(eva, 5)
                pe.wait_ge(evv, 5)
                for n in range(2 * NT):
                    t, h = n // 2, n % 2
                    if n >= 4:
                        pe.wait_ge(ve, n - 3)
                    pe.matmul(ps[4 + n % 4][:, :], K.CKV[:, t * P:(t + 1) * P], K.WKV[:, 8 * h:8 * h + 8, 64:P],
                              start=True, stop=True).then_inc(vmm, 1)

            @block.scalar
            def _(act):
                for n in range(2 * NT):
                    t, h = n // 2, n % 2
                    act.wait_ge(tr0, n + 1)
                    act.activation(HT[:, 4 * h:4 * h + 4, t * P:(t + 1) * P], ps[n % 4][:, :].rearrange("p (k q) -> p k q", q=P), ACT.Copy).then_inc(ev0, 1)
                act.wait_ge(sins, 1)
                act.activation(si[:, :, :], si[:, :, :], ACT.Sin)
                act.activation(co[:, :, :], co[:, :, :], ACT.Sin).then_inc(sins, 1)
                for t in range(NT):
                    act.wait_ge(mm, t + 1)
                    act.activation(lat[:, t, :], ps[4 + t % 2][:, 0:LAT], ACT.Copy).then_inc(ev, 1)
                    act.drain()
                    act.activation(junk[:, :], lat[:, t, 0:QL], ACT.Square, accum_out=ss[:, 0, t:t + 1])
                    act.drain()
                    act.activation(junk[:, 0:KVL], lat[:, t, QL:QL + KVL], ACT.Square, accum_out=ss[:, 1, t:t + 1]).then_inc(sq, 1)
                    act.drain()
                act.wait_ge(var, 1)
                act.activation(ss[:, :, :], ss[:, :, :], ACT.Sqrt).then_inc(rt, 1)
                scales = [K.cols[:, COL_QN:COL_QN + 1], K.cols[:, COL_QN + 1:COL_QN + 2], K.cols[:, COL_KVN:COL_KVN + 1]]
                for n in range(0, 10, 2):
                    act.wait_ge(tr, n + 1)
                    f = n // 2
                    if f < 3:
                        dst = K.CQ[:, f, 0:512] if f < 2 else K.CKV[:, 0:512]
                        act.activation(dst, ps[n % 4][:, :], ACT.Identity, scale=scales[f], bias=0.0).then_inc(eva, 1)
                    elif f == 3:
                        act.activation(K.KT[64:P, 0:512], ps[n % 4][64:P, :], ACT.Copy).then_inc(eva, 1)
                    else:
                        act.activation(K.CS[:, 0:512], ps[n % 4][:, :], ACT.Copy).then_inc(eva, 1)
                for n in range(2 * NT):
                    act.wait_ge(vmm, n + 1)
                    act.activation(K.VV[:, n // 2, (n % 2) * 512:(n % 2) * 512 + 512], ps[4 + n % 4][:, :], ACT.Copy).then_inc(ve, 1)

            @block.gpsimd
            def _(pool):
                pool.memset(T3[:, :, 0:64], SCALE)
                pool.memset(KR[:, :, 0:64], 0.0).then_inc(one, 1)

            @block.vector
            def _(dve):
                f16 = [P, NT, 16]
                dve.wait_ge(p_in, 16)
                dve.tensor_copy(posr[:, :], posi[:, :]).then_inc(pr, 1)
                dve.wait_ge(pr, 2)
                dve.tensor_copy(pos[:, :], ps[6][:, 0:NT])
                dve.drain()
                dve.tensor_tensor(ang[:, :, :], pos[:, :].unsqueeze(2).to_broadcast(f16), cst[:, C_FREQ:C_FREQ + 16].unsqueeze(1).to_broadcast(f16), ALU.mult)
                dve.drain()
                dve.tensor_single_scalar(turn[:, :, :], ang[:, :, :], 1 / (2 * np.pi), ALU.mult)
                dve.drain()
                dve.tensor_copy(ki[:, :, :], turn[:, :, :])
                dve.drain()
                dve.tensor_copy(turn[:, :, :], ki[:, :, :])
                dve.drain()
                for part in (TWO_PI_HI, TWO_PI_LO):
                    dve.scalar_tensor_tensor(out=ang[:, :, :], in0=turn[:, :, :], scalar=-part, in1=ang[:, :, :], op0=ALU.mult, op1=ALU.add)
                    dve.drain()
                dve.tensor_scalar(si[:, :, :], ang[:, :, :], PI, -PI, ALU.min, ALU.max)
                dve.tensor_single_scalar(co[:, :, :], ang[:, :, :], np.pi / 2, ALU.add)
                dve.drain()
                dve.tensor_scalar(tm[:, :, :], co[:, :, :], PI, 2 * np.pi, ALU.is_gt, ALU.mult)
                dve.drain()
                dve.tensor_tensor(co[:, :, :], co[:, :, :], tm[:, :, :], ALU.subtract)
                dve.drain()
                dve.tensor_scalar(co[:, :, :], co[:, :, :], PI, -PI, ALU.min, ALU.max).then_inc(sins, 1)
                dve.wait_ge(sins, 2)
                dve.wait_ge(one, 1)
                for r in range(2):
                    dve.tensor_single_scalar(T3[:, :, 64 + 16 * r:80 + 16 * r], co[:, :, :], SCALE, ALU.mult)
                    dve.tensor_single_scalar(T3[:, :, 96 + 16 * r:112 + 16 * r], si[:, :, :], SCALE, ALU.mult)
                dve.wait_ge(ev, NT)
                x1, x2 = lat[:, :, QL + KVL:QL + KVL + 16], lat[:, :, QL + KVL + 16:LAT]
                dve.tensor_tensor(KR[:, :, 64:80], x1, co[:, :, :], ALU.mult)
                dve.tensor_tensor(KR[:, :, 80:96], x2, co[:, :, :], ALU.mult)
                dve.tensor_tensor(tm[:, :, :], x2, si[:, :, :], ALU.mult)
                dve.tensor_tensor(ang[:, :, :], x1, si[:, :, :], ALU.mult)
                dve.drain()
                dve.tensor_tensor(KR[:, :, 64:80], KR[:, :, 64:80], tm[:, :, :], ALU.subtract)
                dve.tensor_tensor(KR[:, :, 80:96], KR[:, :, 80:96], ang[:, :, :], ALU.add)
                dve.drain()
                dve.tensor_copy(KR[:, :, 96:128], KR[:, :, 64:96]).then_inc(rope, 1)
                dve.wait_ge(sq, NT)
                dve.tensor_scalar(ss[:, 0, :], ss[:, 0, :], 1.0 / QL, EPS, ALU.mult, ALU.add)
                dve.tensor_scalar(ss[:, 1, :], ss[:, 1, :], 1.0 / KVL, EPS, ALU.mult, ALU.add).then_inc(var, 1)
                dve.wait_ge(rt, 1)
                dve.reciprocal(ss[:, :, :], ss[:, :, :]).then_inc(rc, 1)
                dve.wait_ge(rc, 1)
                dve.tensor_tensor(lat[:, :, 0:QL], lat[:, :, 0:QL], ss[:, 0, :].unsqueeze(2).to_broadcast([P, NT, QL]), ALU.mult).then_inc(nm, 1)
                dve.tensor_tensor(lat[:, :, QL:QL + KVL], lat[:, :, QL:QL + KVL], ss[:, 1, :].unsqueeze(2).to_broadcast([P, NT, KVL]), ALU.mult).then_inc(nm, 1)
                for n in range(1, 10, 2):
                    dve.wait_ge(tr, n + 1)
                    f = n // 2
                    if f < 3:
                        dst = K.CQ[:, f, 512:1024] if f < 2 else K.CKV[:, 512:1024]
                        c = COL_QN + f if f < 2 else COL_KVN
                        dve.tensor_scalar(dst, ps[n % 4][:, :], K.cols[:, c:c + 1], None, ALU.mult).then_inc(evv, 1)
                    elif f == 3:
                        dve.tensor_copy(K.KT[64:P, 512:1024], ps[n % 4][64:P, :]).then_inc(evv, 1)
                    else:
                        dve.tensor_copy(K.CS[:, 512:1024], ps[n % 4][:, :]).then_inc(evv, 1)


def attention(nc, K, A):
    ps, cst = K.ps, K.cst
    ident = cst[:, C_ID:C_ID + P]
    OT = K.HT
    cT = [2, 4, 6, 8, 9, 10, 11, 12]
    with ExitStack() as ctx:
        def sb(n, s, d=F32):
            return ctx.enter_context(nc.sbuf_tensor("at_" + n, s, d))

        wq = [sb(f"wq{s}", [P, 2, P]) for s in range(2)]
        wk = [sb(f"wk{s}", [P, 64]) for s in range(2)]
        QT = sb("QT", [P, L])
        zero = sb("zero", [P, 2, 16])
        mask = sb("mask", [P, 2, P], mybir.dt.bfloat16)
        m_ok = K.sem("at_mask")
        PR = [sb(f"PR{i}", [P, L]) for i in range(2)]
        PT = [sb(f"PT{i}", [P, L]) for i in range(2)]
        mxc, nmx, sums, rs = (sb(n, [P, NT]) for n in ("mxc", "nmx", "sums", "rs"))
        w_in = [K.sem(f"at_w{s}") for s in range(2)]
        w_ok = [K.sem(f"at_wok{s}") for s in range(2)]
        item, q_ev, k_ev, mx, ex, tT, tv, ta, pv, ov = (K.sem("at_" + n) for n in ("item", "qev", "kev", "mx", "ex", "tT", "tv", "ta", "pv", "ov"))
        wuq = A["mla_w_uq_2"][0].rearrange("(k p) n -> p k n", p=P)
        wukv = A["mla_w_ukv_2"][0]

        def pair(j):
            return K.psum[:, 2 * (j % 2):2 * (j % 2) + 2, :].rearrange("p b n -> p (b n)")

        with nc.Block() as block:
            @block.sync
            def _(sp):
                sp.dma_start(K.WO[:, :, :], A["mla_w_o_2"][0].rearrange("(k p) n -> p k n", p=P)).then_inc(K.wo_in, 16)
                with sp.Fori(0, AH // 2) as i:
                    for s in range(2):
                        sp.wait_ge(q_ev, i * 4 + (2 * s + 2))
                        sp.dma_start(wq[s][:, :, 0:96], wuq[:, :, ds((i * 2 + s) * 96, 96)]).then_inc(w_in[s], 16)
                        sp.dma_start(wk[s][:, :], wukv[:, ds((i * 2 + s) * P, 64)]).then_inc(w_in[s], 16)

            @block.gpsimd
            def _(pool):
                pool.memset(zero[:, :, :], 0.0)
                pool.drain()
                with pool.Fori(0, AH // 2) as i:
                    for s in range(2):
                        pool.wait_ge(w_in[s], i * 32 + 32)
                        pool.tensor_tensor(wq[s][:, :, 96:112], zero[:, :, :], wq[s][:, :, 80:96], ALU.subtract)
                        pool.tensor_copy(wq[s][:, :, 112:128], wq[s][:, :, 64:80]).then_inc(w_ok[s], 1)

            @block.tensor
            def _(pe):
                pe.sem_inc(tT, 12)
                pe.sem_inc(pv, 8)

                def queries(h, s):
                    pe.wait_ge(ex, h * 8 + 8)
                    for c in (1, 0):
                        for k in range(2):
                            last = pe.matmul(ps[2 + c][:, :], wq[s][:, k, :], K.CQ[:, k, c * 512:(c + 1) * 512], start=k == 0, stop=k == 1)
                        last.then_inc(item, 1)

                def keys(h, s, i):
                    pe.wait_ge(w_ok[s], i + 1)
                    pe.wait_ge(ex, h * 8 + 7)
                    for c in range(2):
                        last = pe.matmul(ps[c][0:64, :], wk[s][:, :], K.CKV[:, c * 512:(c + 1) * 512], start=True, stop=True)
                    last.then_inc(item, 1)

                def scores(h, j):
                    t = NT - 1 - j
                    if j == 0:
                        pe.wait_ge(q_ev, h * 2 + 5)
                        pe.wait_ge(k_ev, h + 3)
                    elif j == 1:
                        pe.wait_ge(q_ev, h * 2 + 6)
                    elif j >= 2:
                        pe.wait_ge(ex, h * 8 + (j - 1 + 8))
                    q = QT[:, t * P:(t + 1) * P]
                    n = (t + 1) * P
                    S = pair(j)
                    for c in range(0, t * P, 512):
                        e = min(c + 512, t * P)
                        pe.matmul(S[:, c:e], q, K.KT[:, c:e], start=True, stop=True)
                    pe.matmul(S[:, t * P:n], q, K.KT[:, t * P:n], start=True, stop=False)
                    pe.matmul(S[:, t * P:n], mask[:, 0, :], mask[:, 1, :], start=False, stop=True).then_inc(item, 1)

                def turn(h, j):
                    t = NT - 1 - j
                    pe.wait_ge(ex, h * 8 + (j + 9))
                    for b in range(0, t + 1, 4):
                        if b == 0:
                            pe.wait_ge(tv, h * 8 + (j + 8))
                        else:
                            pe.wait_ge(ta, h * 4 + (j + 4))
                        for k in range(b, min(b + 4, t + 1)):
                            last = pe.transpose(ps[4 + b // 4][:, (k - b) * P:(k - b + 1) * P], PR[j % 2][:, k * P:(k + 1) * P], ident)
                        last.then_inc(tT, 1)

                def apply(h, j):
                    t = NT - 1 - j
                    pe.wait_ge(tv, h * 8 + (j + 9))
                    if t >= 4:
                        pe.wait_ge(ta, h * 4 + (j + 5))
                    pe.wait_ge(ov, h * 8 + (j - 1 + 8))
                    for k in range(t + 1):
                        last = pe.matmul(ps[6 + j % 2][:, 0:64], PT[j % 2][:, k * P:(k + 1) * P], K.VV[:, k, ds(h * 64, 64)],
                                         start=k == 0, stop=k == t)
                    last.then_inc(pv, 1)

                def head(h, s, i, more=True):
                    for j in range(NT + 2):
                        if j < NT:
                            scores(h, j)
                        elif more and j == NT:
                            keys(h + 1, (s + 1) % 2, i + s)
                        elif more:
                            queries(h + 1, (s + 1) % 2)
                        if 1 <= j <= NT:
                            turn(h, j - 1)
                        if j >= 2:
                            apply(h, j - 2)

                pe.wait_ge(m_ok, 1)
                keys(0, 0, 0)
                queries(0, 0)
                with pe.Fori(0, AH // 2 - 1) as i:
                    for s in range(2):
                        head(i * 2 + s, s, i)
                for s in range(2):
                    head(AH - 2 + s, s, AH // 2 - 1, s == 0)

            @block.scalar
            def _(act):
                act.sem_inc(k_ev, 2)
                act.sem_inc(ex, 8)
                act.sem_inc(ta, 4)

                def head(h):
                    act.wait_ge(item, h * 11 + 1)
                    act.activation(K.KT[0:64, :], pair(0)[0:64, :], ACT.Identity, bias=0.0).then_inc(k_ev, 1)

                    def weights(j):
                        act.wait_ge(mx, h * 8 + (j + 1))
                        act.wait_ge(tT, h * 12 + (cT[j - 2] + 12 if j >= 2 else cT[6 + j]))
                        t = NT - 1 - j
                        n = (t + 1) * P
                        act.activation(PR[j % 2][:, 0:n], pair(j)[:, 0:n], ACT.Exp, bias=nmx[:, t:t + 1], accum_out=sums[:, t:t + 1])
                        act.drain()
                        act.sem_inc(ex, 1)

                    def copy_turned(j):
                        act.wait_ge(tT, h * 12 + (cT[j] + 12))
                        act.wait_ge(pv, h * 8 + (j - 1 + 8))
                        act.activation(PT[j % 2][:, 512:(NT - j) * P], ps[5][:, 0:(4 - j) * P], ACT.Identity, bias=0.0).then_inc(ta, 1)

                    weights(0)
                    for j in range(NT):
                        if j + 1 < NT:
                            weights(j + 1)
                        if j < 4:
                            copy_turned(j)

                with act.Fori(0, AH) as h:
                    head(h)

            @block.vector
            def _(dve):
                dve.tensor_copy(mask[:, 0, :], ident)
                dve.tensor_copy(mask[:, 1, :], cst[:, C_NEG:C_NEG + P]).then_inc(m_ok, 1)
                dve.sem_inc(q_ev, 4)
                dve.sem_inc(tv, 8)
                dve.sem_inc(ov, 8)

                def queries(h):
                    for c in (1, 0):
                        dve.wait_ge(item, h * 11 + (3 - c))
                        n = slice(c * 512, (c + 1) * 512)
                        dve.tensor_tensor(QT[:, n], pair(1)[:, n], K.CS[:, n], ALU.mult).then_inc(q_ev, 1)

                def row_max(h, j):
                    t = NT - 1 - j
                    dve.wait_ge(item, h * 11 + (j + 4))
                    dve.tensor_reduce(mxc[:, t:t + 1], pair(j)[:, 0:(t + 1) * P], AX.X, ALU.max)
                    dve.drain()
                    dve.tensor_single_scalar(nmx[:, t:t + 1], mxc[:, t:t + 1], -1.0, ALU.mult).then_inc(mx, 1)

                def copy_turned(h, j):
                    t = NT - 1 - j
                    n = min(t + 1, 4) * P
                    dve.wait_ge(tT, h * 12 + (cT[j] + 12 - (1 if t >= 4 else 0)))
                    dve.wait_ge(pv, h * 8 + (j - 1 + 8))
                    dve.tensor_copy(PT[j % 2][:, 0:n], ps[4][:, 0:n]).then_inc(tv, 1)
                    dve.reciprocal(rs[:, t:t + 1], sums[:, t:t + 1])

                def output(h, j):
                    t = NT - 1 - j
                    dve.wait_ge(pv, h * 8 + (j + 9))
                    dve.tensor_scalar(OT[:, t, ds(h * 64, 64)], ps[6 + j % 2][:, 0:64], rs[:, t:t + 1], None, ALU.mult).then_inc(ov, 1)

                def head(h, more=True):
                    for j in range(NT + 1):
                        if j < NT:
                            row_max(h, j)
                        if j >= 3:
                            output(h, j - 3)
                        if j >= 1:
                            copy_turned(h, j - 1)
                    dve.drain()
                    output(h, NT - 2)
                    if more:
                        queries(h + 1)
                    output(h, NT - 1)

                queries(0)
                with dve.Fori(0, AH - 1) as h:
                    head(h)
                head(AH - 1, False)


def attention_output(nc, K, A):
    O, X, ps = K.HT, K.X, K.ps
    OF = K.VV
    with ExitStack() as ctx:
        tr, ev, mm, done = (K.sem("ao_" + n) for n in ("tr", "ev", "mm", "done"))
        with nc.Block() as block:
            @block.tensor
            def _(pe):
                for n in range(2 * NT):
                    t, h = n // 2, n % 2
                    if n >= 4:
                        pe.wait_ge(ev, n - 3)
                    for k in range(4):
                        last = pe.transpose(ps[n % 4][:, k * P:(k + 1) * P], O[:, t, (4 * h + k) * P:(4 * h + k + 1) * P], K.cst[:, C_ID:C_ID + P])
                    last.then_inc(tr, 1)
                pe.wait_ge(K.wo_in, 16)
                for t in range(NT):
                    pe.wait_ge(ev, 2 * t + 2)
                    for h in range(2):
                        n = 2 * t + h
                        if n >= 4:
                            pe.wait_ge(done, n - 3)
                        for k in range(KD):
                            last = pe.matmul(ps[4 + n % 4][:, :], OF[:, k, t * P:(t + 1) * P], K.WO[:, k, h * 512:(h + 1) * 512],
                                             start=k == 0, stop=k == KD - 1)
                        last.then_inc(mm, 1)

            @block.scalar
            def _(act):
                for n in range(2 * NT):
                    t, h = n // 2, n % 2
                    act.wait_ge(tr, n + 1)
                    act.activation(OF[:, 4 * h:4 * h + 4, t * P:(t + 1) * P], ps[n % 4][:, :].rearrange("p (k q) -> p k q", q=P), ACT.Copy).then_inc(ev, 1)

            @block.vector
            def _(dve):
                for n in range(2 * NT):
                    x = X[:, n // 2, (n % 2) * 512:(n % 2) * 512 + 512]
                    dve.wait_ge(mm, n + 1)
                    dve.scalar_tensor_tensor(out=x, in0=x, scalar=ALPHA, in1=ps[4 + n % 4][:, :], op0=ALU.mult, op1=ALU.add).then_inc(done, 1)


def mla(nc, K, A):
    with ExitStack() as ctx:
        def sb(n, s, d=F32):
            return ctx.enter_context(nc.sbuf_tensor("mla_" + n, s, d))

        K.CQ, K.CKV, K.KT, K.CS = sb("CQ", [P, 2, L]), sb("CKV", [P, L]), sb("KT", [P, L]), sb("CS", [P, L])
        K.VV = sb("VV", [P, NT, D])
        K.wo_in = K.sem("mla_wo_in")
        with nc.sbuf_tensor("mla_WKV", [P, AH, P], F32) as K.WKV:
            latents(nc, K, A)
        K.WO = sb("WO", [P, KD, D])
        attention(nc, K, A)
        attention_output(nc, K, A)


def expert_weights(sp, K, A, layer, e, slot, sem):
    for j, name in enumerate(("moe_w1_2", "moe_w3_2")):
        src = A[name][layer][ds(e, 1)].rearrange("e (k p) n -> p (e k) n", p=P)
        sp.dma_start(K.W13[slot][:, :, j, :], src).then_inc(sem, 16)
    src = A["moe_w2_2"][layer][ds(e, 1)].rearrange("e (k p) n -> p (e k) n", p=P)
    sp.dma_start(K.W2[slot][:, :, :], src).then_inc(sem, 16)


def gather_buffers(K):
    return [K.hreg[:, i * D:(i + 1) * D] for i in range(2)]


def routing(nc, K, A, layer, tag):
    ps, cst = K.ps, K.cst
    NR = 8 + NE
    with ExitStack() as ctx:
        def sb(n, s, d=F32):
            return ctx.enter_context(nc.sbuf_tensor(tag + n, s, d))

        br = sb("br", [P, NR])
        LG = sb("LG", [P, NT, NR])
        g8, e8 = sb("g8", [P, NT, 8]), sb("e8", [P, NT, 8])
        gi, ei = sb("gi", [P, NT, 8], U32), sb("ei", [P, NT, 8], U32)
        gs, oh, xe, es = sb("gs", [P, NT]), sb("oh", [P, NT, 8]), sb("xe", [P, NT, 8]), sb("es", [P, NT, 8])
        big = sb("big", [P, 1024])
        ek, rk, ok_, sl, ge, r_, d_ = (sb(n, [P, 2, NT]) for n in ("ek", "rk", "ok", "sl", "ge", "r", "d"))
        Ak = [sb(f"A{k}", [P, NT, NE]) for k in range(2)]
        AS = sb("AS", [P, NT, NE], BF16)
        one64 = sb("one64", [P, NE])
        cnt, ov, oe, os_ = (sb(n, [P, NE]) for n in ("cnt", "ov", "oe", "os"))
        one, before = sb("one", [P, P], BF16), sb("before", [P, P], BF16)
        sli, rwi, bli = (sb(n, [P, 2, NT], I32) for n in ("sli", "rwi", "bli"))
        rwf, blf = sb("rwf", [P, 2, NT]), sb("blf", [P, 2, NT])
        RO = [sb(f"RO{i}", [P, P]) for i in range(4)]
        BO = [sb(f"BO{i}", [P, NB]) for i in range(4)]
        vt, v0 = sb("vt", [P, NB]), sb("v0", [P, NB])
        eo = sb("eo", [P, OVER])
        w_in, sub, exd, a_ok, rmm, oh_ok, tmm, ones_ok, vi = (K.sem(tag + n) for n in (
            "w_in", "sub", "exd", "a_ok", "rmm", "oh_ok", "tmm", "ones", "vi"))

        with nc.Block() as block:
            @block.sync
            def _(sp):
                sp.dma_start(br[:, 0:8], A["moe_b_grp_2"][layer:layer + 1, :].to_broadcast([P, 8])).then_inc(w_in, 16)
                sp.dma_start(br[:, 8:NR], A["moe_b_exp_2"][layer:layer + 1, :].to_broadcast([P, NE])).then_inc(w_in, 16)
                for s in range(4):
                    expert_weights(sp, K, A, layer, s, s, K.ew_in[s])

            @block.gpsimd
            def _(pool):
                pool.memset(one[:, :], 1.0)
                pool.tensor_copy(before[:, :], cst[:, C_SUP:C_SUP + P]).then_inc(ones_ok, 1)
                for xg in gather_buffers(K):
                    pool.memset(xg, 0.0)

            @block.tensor
            def _(pe):
                pe.wait_ge(a_ok, 1)
                pe.wait_ge(ones_ok, 1)
                pe.matmul(ps[2][:, :], before[:, :], AS[:, :, :], start=True, stop=False)
                for t in range(NT - 1):
                    pe.matmul(ps[2][:, (t + 1) * NE:NT * NE].rearrange("p (t e) -> p t e", e=NE), one[:, :],
                              AS[:, t:t + 1, :].to_broadcast([P, NT - 1 - t, NE]), start=False, stop=t == NT - 2)
                for t in range(NT):
                    last = pe.matmul(ps[3][:, 0:NE], one[:, :], AS[:, t, :], start=t == 0, stop=t == NT - 1)
                last.then_inc(rmm, 1)
                for n in range(2 * NT):
                    pe.wait_ge(oh_ok, n + 1)
                    pe.matmul(ps[6][:, 0:NB], RO[n % 4][:, :], BO[n % 4][:, :], start=n == 0, stop=n == 2 * NT - 1).then_inc(tmm, 1)

            @block.scalar
            def _(act):
                act.wait_ge(sub, 1)
                act.activation(xe[:, :, :], xe[:, :, :], ACT.Exp).then_inc(exd, 1)
                act.wait_ge(sub, 2)
                act.activation(r_[:, 0, :], r_[:, 0, :], ACT.Exp).then_inc(exd, 1)

            @block.vector
            def _(dve):
                def iota(n):
                    return cst[:, C_IOTA:C_IOTA + n]

                dve.memset(one64[:, :], 1.0)
                dve.wait_ge(w_in, 32)
                for h in range(2):
                    dve.tensor_tensor(LG[:, 4 * h:4 * h + 4, :], ps[4 + h][:, 0:4 * NR].rearrange("p (t n) -> p t n", n=NR),
                                      br[:, :].unsqueeze(1).to_broadcast([P, 4, NR]), ALU.add)
                dve.drain()
                for t in range(NT):
                    dve.max(g8[:, t, :], LG[:, t, 0:8])
                dve.drain()
                for t in range(NT):
                    dve.max_index(gi[:, t, :], g8[:, t, :], LG[:, t, 0:8])
                dve.tensor_tensor(xe[:, :, :], LG[:, :, 0:8], g8[:, :, 0:1].to_broadcast([P, NT, 8]), ALU.subtract).then_inc(sub, 1)
                dve.drain()
                dve.tensor_copy(gs[:, :], gi[:, :, 0])
                dve.drain()
                dve.tensor_tensor(oh[:, :, :], iota(8).unsqueeze(1).to_broadcast([P, NT, 8]), gs[:, :].unsqueeze(2).to_broadcast([P, NT, 8]), ALU.is_equal)
                dve.drain()
                for h in range(2):
                    ts = slice(4 * h, 4 * h + 4)
                    dve.tensor_tensor(big[:, h * 256:(h + 1) * 256].rearrange("p (t g j) -> p t g j", g=8, j=8), LG[:, ts, 8:NR].rearrange("p t (g j) -> p t g j", g=8),
                                      oh[:, ts, :].unsqueeze(3).to_broadcast([P, 4, 8, 8]), ALU.mult)
                dve.drain()
                dve.tensor_reduce(es[:, :, :], big[:, 0:512].rearrange("p (t g j) -> p t j g", g=8, j=8), AX.X, ALU.add)
                dve.drain()
                for t in range(NT):
                    dve.max(e8[:, t, :], es[:, t, :])
                dve.drain()
                for t in range(NT):
                    dve.max_index(ei[:, t, :], e8[:, t, :], es[:, t, :])
                dve.tensor_tensor(r_[:, 0, :], e8[:, :, 1], e8[:, :, 0], ALU.subtract).then_inc(sub, 1)
                dve.drain()
                dve.tensor_copy(ek[:, :, :], ei[:, :, 0:2].rearrange("p t k -> p k t"))
                dve.drain()
                for k in range(2):
                    dve.scalar_tensor_tensor(out=ek[:, k, :], in0=gs[:, :], scalar=8.0, in1=ek[:, k, :], op0=ALU.mult, op1=ALU.add)
                dve.drain()
                for k in range(2):
                    dve.tensor_tensor(Ak[k][:, :, :], iota(NE).unsqueeze(1).to_broadcast([P, NT, NE]), ek[:, k, :].unsqueeze(2).to_broadcast([P, NT, NE]), ALU.is_equal)
                dve.drain()
                dve.tensor_tensor(AS[:, :, :], Ak[0][:, :, :], Ak[1][:, :, :], ALU.add).then_inc(a_ok, 1)
                dve.wait_ge(exd, 2)
                dve.tensor_reduce(d_[:, 0, :], xe[:, :, :], AX.X, ALU.add)
                dve.tensor_single_scalar(d_[:, 1, :], r_[:, 0, :], 1.0, ALU.add)
                dve.drain()
                dve.tensor_tensor(d_[:, 0, :], d_[:, 0, :], d_[:, 1, :], ALU.mult)
                dve.drain()
                dve.reciprocal(K.GT[:, 0, :], d_[:, 0, :])
                dve.drain()
                dve.tensor_tensor(K.GT[:, 1, :], K.GT[:, 0, :], r_[:, 0, :], ALU.mult)
                dve.wait_ge(rmm, 1)
                dve.tensor_copy(cnt[:, :], ps[3][:, 0:NE])
                dve.drain()
                dve.tensor_tensor(big[:, 0:512].rearrange("p (e m) -> p e m", m=8), cnt[:, :].unsqueeze(2).to_broadcast([P, NE, 8]),
                                  cst[:, C_THR:C_THR + 8].unsqueeze(1).to_broadcast([P, NE, 8]), ALU.is_gt)
                dve.drain()
                dve.tensor_reduce(ov[:, :], big[:, 0:512].rearrange("p (e m) -> p e m", m=8), AX.X, ALU.add)
                dve.drain()
                dve.tensor_tensor_scan(oe[:, :], one64[:, :], ov[:, :], 0.0, ALU.mult, ALU.add)
                dve.drain()
                dve.tensor_tensor(os_[:, :], oe[:, :], ov[:, :], ALU.subtract)
                for k in range(2):
                    b3 = big[:, 0:512].rearrange("p (t e) -> p t e", e=NE)
                    dve.tensor_tensor(b3, Ak[k][:, :, :], ps[2][:, :].rearrange("p (t e) -> p t e", e=NE), ALU.mult)
                    dve.drain()
                    dve.tensor_reduce(rk[:, k, :], b3, AX.X, ALU.add)
                    dve.drain()
                    dve.tensor_tensor(b3, Ak[k][:, :, :], os_[:, :].unsqueeze(1).to_broadcast([P, NT, NE]), ALU.mult)
                    dve.drain()
                    dve.tensor_reduce(ok_[:, k, :], b3, AX.X, ALU.add)
                    dve.drain()
                dve.tensor_single_scalar(ek[:, :, :], ek[:, :, :], float(P), ALU.mult)
                dve.tensor_scalar(ok_[:, :, :], ok_[:, :, :], float(P), float((NE - 1) * P), ALU.mult, ALU.add)
                dve.tensor_single_scalar(ge[:, :, :], rk[:, :, :], float(P), ALU.is_ge)
                dve.drain()
                dve.tensor_tensor(ok_[:, :, :], ok_[:, :, :], ek[:, :, :], ALU.subtract)
                dve.tensor_tensor(sl[:, :, :], rk[:, :, :], ek[:, :, :], ALU.add)
                dve.drain()
                dve.tensor_tensor(ok_[:, :, :], ok_[:, :, :], ge[:, :, :], ALU.mult)
                dve.drain()
                dve.tensor_tensor(sl[:, :, :], sl[:, :, :], ok_[:, :, :], ALU.add)
                dve.drain()
                dve.tensor_copy(sli[:, :, :], sl[:, :, :])
                dve.drain()
                dve.tensor_single_scalar(rwi[:, :, :], sli[:, :, :], P - 1, ALU.bitwise_and)
                dve.tensor_single_scalar(bli[:, :, :], sli[:, :, :], 7, ALU.arith_shift_right)
                dve.drain()
                dve.tensor_copy(rwf[:, :, :], rwi[:, :, :])
                dve.tensor_copy(blf[:, :, :], bli[:, :, :])
                dve.drain()
                for n in range(2 * NT):
                    k, t = n // NT, n % NT
                    if n >= 4:
                        dve.wait_ge(tmm, n - 3)
                    dve.tensor_scalar(RO[n % 4][:, :], iota(P), rwf[:, k, t:t + 1], None, ALU.is_equal)
                    dve.tensor_scalar(BO[n % 4][:, :], iota(NB), blf[:, k, t:t + 1], cst[:, C_TOK + n:C_TOK + n + 1], ALU.is_equal, ALU.mult).then_inc(oh_ok, 1)
                dve.wait_ge(tmm, 2 * NT)
                dve.tensor_copy(vt[:, :], ps[6][:, 0:NB])
                dve.drain()
                dve.tensor_scalar(v0[:, :], vt[:, :], 0.5, 100000.0, ALU.is_lt, ALU.mult)
                dve.drain()
                dve.scalar_tensor_tensor(out=vt[:, :], in0=vt[:, :], scalar=-1.0, in1=v0[:, :], op0=ALU.add, op1=ALU.add)
                dve.drain()
                dve.tensor_copy(K.SIDX[:, :], vt[:, :])
                dve.drain()
                dve.tensor_single_scalar(K.GIDX[:, :], K.SIDX[:, :], 1, ALU.arith_shift_right)
                dve.tensor_tensor(big[:, :].rearrange("p (j e) -> p j e", e=NE), iota(OVER).unsqueeze(2).to_broadcast([P, OVER, NE]),
                                  oe[:, :].unsqueeze(1).to_broadcast([P, OVER, NE]), ALU.is_ge)
                dve.drain()
                dve.tensor_reduce(eo[:, :], big[:, :].rearrange("p (j e) -> p j e", e=NE), AX.X, ALU.add)
                dve.drain()
                dve.tensor_single_scalar(eo[:, :], eo[:, :], float(NE - 1), ALU.min)
                dve.drain()
                dve.tensor_copy(K.EO[:, 0:OVER], eo[:, :])
                dve.tensor_copy(K.EO[:, OVER:OVER + 1], oe[:, NE - 1:NE])


def experts(nc, K, A, layer, tag, first, count, w_in, w_base):
    ps, cst = K.ps, K.cst
    ident = cst[:, C_ID:C_ID + P]
    hr = K.hreg
    xg = gather_buffers(K)
    xT = [hr[:, (2 + i) * D:(3 + i) * D].rearrange("p (k r) -> p k r", r=P) for i in range(2)]
    ysb = [hr[:, (4 + i) * D:(5 + i) * D] for i in range(2)]
    sil = [hr[:, 6 * D + i * DE:6 * D + (i + 1) * DE] for i in range(2)]
    hb = [hr[:, 7 * D + i * DE:7 * D + (i + 1) * DE] for i in range(2)]
    hT = [hr[:, 8 * D + i * DE:8 * D + (i + 1) * DE].rearrange("p (k r) -> p k r", r=P) for i in range(2)]
    with ExitStack() as ctx:
        sgi = [ctx.enter_context(nc.sbuf_tensor(tag + f"gi{i}", [P, 1], I32)) for i in range(2)]
        ssi = [ctx.enter_context(nc.sbuf_tensor(tag + f"si{i}", [P, 1], I32)) for i in range(2)]
        scr = ctx.enter_context(nc.sbuf_tensor(tag + "scr", [P, 2], F32))
        ga = [K.sem(tag + f"ga{i}") for i in range(2)]
        sc = [K.sem(tag + f"sc{i}") for i in range(2)]
        (tx, txa, txv, hm, sild, hbd, th, thv, ym, ya, yv, zg, zs) = (K.sem(tag + n) for n in (
            "tx", "txa", "txv", "hm", "sild", "hbd", "th", "thv", "ym", "ya", "yv", "zg", "zs"))
        PEEL = 4

        def wait(eng, sem, b, n, least=0):
            if not isinstance(b, int) or b >= least:
                eng.wait_ge(sem, b + n)

        def every_block(eng, body):
            for b in range(PEEL):
                body(b, b % 4, b // 2, b // 4)
            with eng.Fori(1, count // 4 - 1) as i:
                for s in range(4):
                    body(i * 4 + s, s, i * 2 + s // 2, i)
            for b in range(count - PEEL, count):
                body(b, b % 4, b // 2, b // 4)

        with nc.Block() as block:
            @block.sync
            def _(sp):
                def load(b, s):
                    e = b if first == 0 else sp.value_load(K.EO[0:1, ds(b, 1)], min_val=0, max_val=NE - 1)
                    expert_weights(sp, K, A, layer, e, s, w_in[s])

                if first > 0:
                    for b in range(4):
                        load(b, b)
                with sp.Fori(1, count // 4) as i:
                    for s in range(4):
                        sp.wait_ge(ym, i * 4 + (s - 3))
                        load(i * 4 + s, s)

            @block.gpsimd
            def _(pool):
                if first > 0:
                    for i in range(2):
                        pool.memset(xg[i], 0.0)
                pool.memset(scr[:, :], 0.0)
                pool.drain()

                def carry_wait():
                    pool.tensor_tensor(scr[:, 0:1], scr[:, 1:2], scr[:, 1:2], ALU.add)

                def gather(b, p, half):
                    wait(pool, tx, b, -1, 2)
                    pool.tensor_copy(sgi[p][:, :], K.GIDX[:, ds(b + first, 1)]).then_inc(zg, 1)
                    pool.wait_ge(zg, b + 1)
                    carry_wait()
                    pool.indirect_dma_start(xg[p], None, K.xrow, bass.IndirectOffsetOnAxis(ap=sgi[p][:, :], axis=0),
                                            bounds_check=L - 1, oob_is_err=False).then_inc(ga[p], 16)

                def scatter(b, p, half):
                    if not isinstance(b, int) or b >= 2:
                        pool.wait_ge(sc[p], half * 16)
                    pool.wait_ge(ya, b + 1)
                    pool.wait_ge(yv, b + 1)
                    pool.tensor_copy(ssi[p][:, :], K.SIDX[:, ds(b + first, 1)]).then_inc(zs, 1)
                    pool.wait_ge(zs, b + 1)
                    carry_wait()
                    pool.indirect_dma_start(K.yrow, bass.IndirectOffsetOnAxis(ap=ssi[p][:, :], axis=0), ysb[p], None,
                                            bounds_check=2 * L - 1, oob_is_err=False).then_inc(sc[p], 16)

                for b in range(3):
                    gather(b, b % 2, b // 2)

                def body(b, s, half, quarter):
                    if not isinstance(b, int) or b < count - 3:
                        gather(b + 3, (s + 1) % 2, half + (1 + s % 2))
                    if not isinstance(b, int) or b >= 1:
                        scatter(b + (-1), (s + 1) % 2, half + (s % 2 - 1))

                every_block(pool, body)
                scatter(count - 1, 1, count // 2 - 1)
                for i in range(2):
                    pool.wait_ge(sc[i], 16 * count // 2)

            @block.tensor
            def _(pe):
                def turn_x(b, p, half):
                    pe.wait_ge(ga[p], half * 16 + 16)
                    wait(pe, txa, b, 0, 1)
                    wait(pe, txv, b, 0, 1)
                    for k in range(KD):
                        last = pe.transpose(ps[k // 4][:, (k % 4) * P:(k % 4 + 1) * P], xg[p][:, k * P:(k + 1) * P], ident)
                    last.then_inc(tx, 1)

                def first_product(b, s, quarter):
                    pe.wait_ge(w_in[s], quarter * 48 + w_base + 48)
                    pe.wait_ge(txa, b + 1)
                    pe.wait_ge(txv, b + 1)
                    wait(pe, hbd, b, -1, 2)
                    for k in range(KD):
                        last = pe.matmul(ps[2 + s % 2][:, :], xT[s % 2][:, k, :], K.W13[s][:, k, :, :], start=k == 0, stop=k == KD - 1)
                    last.then_inc(hm, 1)

                def turn_h(b, p):
                    pe.wait_ge(hbd, b + 1)
                    wait(pe, thv, b, 0, 1)
                    for k in range(2):
                        last = pe.transpose(ps[4][:, k * P:(k + 1) * P], hb[p][:, k * P:(k + 1) * P], ident)
                    last.then_inc(th, 1)

                def second_product(b, s):
                    pe.wait_ge(thv, b + 1)
                    wait(pe, ya, b, 0, 1)
                    wait(pe, yv, b, 0, 1)
                    for h in range(2):
                        for k in range(2):
                            last = pe.matmul(ps[5 + h][:, :], hT[s % 2][:, k, :], K.W2[s][:, k, h * 512:(h + 1) * 512], start=k == 0, stop=k == 1)
                    last.then_inc(ym, 1)

                turn_x(0, 0, 0)

                def body(b, s, half, quarter):
                    if not isinstance(b, int) or b < count - 1:
                        turn_x(b + 1, (s + 1) % 2, half + (s % 2))
                    if not isinstance(b, int) or b >= 1:
                        turn_h(b + (-1), (s + 1) % 2)
                    first_product(b, s, quarter)
                    if not isinstance(b, int) or b >= 1:
                        second_product(b + (-1), (s + 3) % 4)

                every_block(pe, body)
                turn_h(count - 1, 1)
                second_product(count - 1, 3)

            @block.scalar
            def _(act):
                def copy_x(b, p):
                    act.wait_ge(tx, b + 1)
                    wait(act, hm, b, -1, 2)
                    act.activation(xT[p][:, 0:4, :].rearrange("p k r -> p (k r)"), ps[0][:, :], ACT.Copy).then_inc(txa, 1)

                def copy_y(b, p, half_before):
                    act.wait_ge(ym, b + 1)
                    if not isinstance(b, int) or b >= 2:
                        act.wait_ge(sc[p], half_before * 16)
                    act.activation(ysb[p][:, 0:512], ps[5][:, :], ACT.Copy).then_inc(ya, 1)

                copy_x(0, 0)

                def body(b, s, half, quarter):
                    if not isinstance(b, int) or b < count - 1:
                        copy_x(b + 1, (s + 1) % 2)
                    act.wait_ge(hm, b + 1)
                    wait(act, hbd, b, -1, 2)
                    act.activation(sil[s % 2], ps[2 + s % 2][:, 0:DE], ACT.Silu).then_inc(sild, 1)
                    if not isinstance(b, int) or b >= 1:
                        copy_y(b + (-1), (s + 1) % 2, half + (s % 2 - 1))

                every_block(act, body)
                copy_y(count - 1, 1, (count - 1) // 2)

            @block.vector
            def _(dve):
                def copy_x(b, p):
                    dve.wait_ge(tx, b + 1)
                    wait(dve, hm, b, -1, 2)
                    dve.tensor_copy(xT[p][:, 4:8, :].rearrange("p k r -> p (k r)"), ps[1][:, :]).then_inc(txv, 1)

                def copy_h(b, p):
                    dve.wait_ge(th, b + 1)
                    wait(dve, ym, b, -1, 2)
                    dve.tensor_copy(hT[p].rearrange("p k r -> p (k r)"), ps[4][:, 0:DE]).then_inc(thv, 1)

                def copy_y(b, p, half_before):
                    dve.wait_ge(ym, b + 1)
                    if not isinstance(b, int) or b >= 2:
                        dve.wait_ge(sc[p], half_before * 16)
                    dve.tensor_copy(ysb[p][:, 512:1024], ps[6][:, :]).then_inc(yv, 1)

                copy_x(0, 0)

                def body(b, s, half, quarter):
                    if not isinstance(b, int) or b < count - 1:
                        copy_x(b + 1, (s + 1) % 2)
                    if not isinstance(b, int) or b >= 1:
                        copy_h(b + (-1), (s + 1) % 2)
                    dve.wait_ge(sild, b + 1)
                    wait(dve, th, b, -1, 2)
                    dve.tensor_tensor(hb[s % 2], sil[s % 2], ps[2 + s % 2][:, DE:2 * DE], ALU.mult).then_inc(hbd, 1)
                    if not isinstance(b, int) or b >= 1:
                        copy_y(b + (-1), (s + 1) % 2, half + (s % 2 - 1))

                every_block(dve, body)
                copy_h(count - 1, 1)
                copy_y(count - 1, 1, (count - 1) // 2)


def moe(nc, K, A, layer):
    with ExitStack() as ctx:
        def sb(n, s, d=F32):
            return ctx.enter_context(nc.sbuf_tensor(f"moe{layer}_" + n, s, d))

        K.W13 = [sb(f"W13_{s}", [P, KD, 2, DE]) for s in range(4)]
        K.W2 = [sb(f"W2_{s}", [P, 2, D]) for s in range(4)]
        routing(nc, K, A, layer, f"ro{layer}_")
        experts(nc, K, A, layer, f"ex{layer}_", 0, NE, K.ew_in, K.ew_base)
        K.ew_base += 48 * NE // 4
        overflow = nc.values_load(K.EO[0:1, OVER:OVER + 1], min_val=0, max_val=OVER)
        with nc.If(overflow > 0):
            experts(nc, K, A, layer, f"ov{layer}_", NE, OVER, [K.sem(f"ov{layer}_w{s}") for s in range(4)], 0)


def pool_mixer(nc, K, A):
    HT, X, ps, cst = K.HT, K.X, K.ps, K.cst
    with ExitStack() as ctx:
        def sb(n, s, d=F32):
            return ctx.enter_context(nc.sbuf_tensor("pm_" + n, s, d))

        w = sb("w", [P, 4, 2, 256])
        PM = sb("PM", [P, KD, L])
        bufs = [sb(f"b{i}", [P, 2, L]) for i in range(2)]
        bb, sc = sb("bb", [P, D]), sb("sc", [P, D])
        T = sb("T", [P, 2, D])
        w_in, pooled, mm, biased, scaled, done = (K.sem("pm_" + n) for n in ("w_in", "pooled", "mm", "biased", "scaled", "done"))

        with nc.Block() as block:
            @block.sync
            def _(sp):
                for g in range(4):
                    sp.dma_start(w[:, g], A["pool_w_2"][0, g].rearrange("(k p) n -> p k n", p=P)).then_inc(w_in, 16)
                sp.dma_start(bb[:, :], A["pool_b_2"].to_broadcast([P, D])).then_inc(w_in, 16)
                sp.dma_start(sc[:, :], A["pool_scale_2"].to_broadcast([P, D])).then_inc(w_in, 16)

            @block.vector
            def _(dve):
                for g, win in enumerate(WINS):
                    src = HT[:, 2 * g:2 * g + 2, :]
                    x, sh, n = src, 1, 0
                    while sh < win:
                        dst = bufs[n % 2]
                        dve.tensor_tensor(dst[:, :, sh:L], x[:, :, sh:L], x[:, :, 0:L - sh], ALU.add)
                        dve.tensor_copy(dst[:, :, 0:sh], x[:, :, 0:sh])
                        dve.drain()
                        x, sh, n = dst, 2 * sh, n + 1
                    dve.tensor_tensor(x[:, :, 0:win], x[:, :, 0:win], cst[:, C_POOL:C_POOL + win].unsqueeze(1).to_broadcast([P, 2, win]), ALU.mult)
                    dve.drain()
                    out = PM[:, 2 * g:2 * g + 2, :]
                    dve.scalar_tensor_tensor(out=out[:, :, win:L], in0=x[:, :, win:L], scalar=1.0 / win, in1=src[:, :, win:L], op0=ALU.mult, op1=ALU.subtract)
                    dve.tensor_tensor(out[:, :, 0:win], x[:, :, 0:win], src[:, :, 0:win], ALU.subtract)
                    dve.drain()
                    dve.sem_inc(pooled, 1)
                dve.wait_ge(w_in, 16 * 6)
                for t in range(NT + 1):
                    if t < NT:
                        dve.wait_ge(mm, t + 1)
                        if t >= 2:
                            dve.wait_ge(done, t - 1)
                        for h in range(2):
                            last = dve.tensor_tensor(T[:, t % 2, h * 512:(h + 1) * 512], ps[2 * (t % 4) + h][:, :], bb[:, h * 512:(h + 1) * 512], ALU.add)
                        last.then_inc(biased, 1)
                    if t >= 1:
                        u = t - 1
                        dve.wait_ge(scaled, u + 1)
                        dve.scalar_tensor_tensor(out=X[:, u, :], in0=X[:, u, :], scalar=ALPHA, in1=T[:, u % 2, :], op0=ALU.mult, op1=ALU.add).then_inc(done, 1)

            @block.gpsimd
            def _(pool):
                pool.wait_ge(w_in, 16 * 6)
                for t in range(NT):
                    pool.wait_ge(biased, t + 1)
                    pool.tensor_tensor(T[:, t % 2, :], T[:, t % 2, :], sc[:, :], ALU.mult).then_inc(scaled, 1)

            @block.tensor
            def _(pe):
                pe.wait_ge(w_in, 16 * 6)
                pe.wait_ge(pooled, 4)
                for t in range(NT):
                    if t >= 4:
                        pe.wait_ge(biased, t - 3)
                    for g in range(4):
                        for k in range(2):
                            last = pe.matmul(ps[2 * (t % 4) + g // 2][:, (g % 2) * 256:(g % 2 + 1) * 256], PM[:, 2 * g + k, t * P:(t + 1) * P],
                                             w[:, g, k, :], start=k == 0, stop=k == 1)
                    last.then_inc(mm, 1)


def second_block(nc, K, A, lasting):
    K.yrow = nc.dram_tensor("yrow", [2 * L, D], F32).ap()
    K.ew_in = [K.sem(f"ew_in{s}", lasting=True) for s in range(4)]
    K.ew_base = 0
    K.clear()
    K.hreg = lasting.enter_context(nc.sbuf_tensor("hreg", [P, 9 * D], F32))[:, :]
    K.HT = K.hreg[:, 0:KD * L].rearrange("p (k t) -> p k t", t=L)
    with ExitStack() as ctx:
        def sb(n, s, d=F32):
            return ctx.enter_context(nc.sbuf_tensor(n, s, d))

        K.GT = sb("GT", [P, 2, NT])
        K.EO = sb("EO", [P, OVER + 1], I32)
        K.SIDX, K.GIDX = sb("SIDX", [P, NB], I32), sb("GIDX", [P, NB], I32)
        mla(nc, K, A)
        layer_norm(nc, K, A, "ln0_", 0, 0, K.xrow, router=0)
        K.clear()
        moe(nc, K, A, 0)
        K.clear()
        layer_norm(nc, K, A, "ln1_", 0, 1, None, combine=True)
        pool_mixer(nc, K, A)
        layer_norm(nc, K, A, "ln2_", 1, 0, K.xrow, router=1)
        K.clear()
        moe(nc, K, A, 1)
        layer_norm(nc, K, A, "ln3_", 1, 1, A["out"], transpose=False, combine=True)


class Memory:
    pass


def semaphore_pool(nc):
    held = []

    def sem(name, lasting=False):
        s = nc.alloc_semaphore(name=name)
        if not lasting:
            held.append(s)
        return s

    def clear():
        nc.clear_and_free_semaphores(held[:])
        nc.all_engine_barrier()
        held.clear()

    return sem, clear


def build(nc, A):
    with ExitStack() as ctx:
        def sb(n, s, d=F32):
            return ctx.enter_context(nc.sbuf_tensor(n, s, d))

        K = Memory()
        K.sem, K.clear = semaphore_pool(nc)
        K.psum = ctx.enter_context(nc.psum_tensor("psum", [P, 8, 512], F32))
        K.ps = [K.psum[:, i, :] for i in range(8)]
        K.cst = sb("cst", [P, C_W])
        K.cols = sb("cols", [P, NCOL])
        K.A1, K.B1, K.A1c, K.B1c, K.A2, K.B2 = (sb(n, [P, KD]) for n in ("A1", "B1", "A1c", "B1c", "A2", "B2"))
        K.xrow = nc.dram_tensor("xrow", [L, D], F32).ap()
        first_block(nc, K, A, ctx)
        second_block(nc, K, A, ctx)


_INS = ["x", "c", "ctx", "c_ctx", "w_ada", "b_ada", "g_pre_mix", "g_post_mix", "g_pre_ffn", "g_post_ffn", "w_in", "conv_w",
        "conv_b", "dt_bias", "a_log", "d_skip", "g_ssd", "w_out", "w_gate", "w_up", "w_down", "positions_2", "ln_g_2",
        "ln_b_2", "mla_w_in_2", "mla_q_norm_2", "mla_w_uq_2", "mla_kv_norm_2", "mla_w_ukv_2", "mla_w_o_2",
        "pool_w_2", "pool_b_2", "pool_scale_2", "moe_w_grp_2", "moe_b_grp_2", "moe_w_exp_2", "moe_b_exp_2",
        "moe_w1_2", "moe_w3_2", "moe_w2_2"]


def kernel(**inputs):
    import concourse.bacc as bacc
    from concourse.bass_utils import run_bass_kernel_spmd

    nc = bacc.Bacc("TRN2", target_bir_lowering=False, num_devices=1)
    arrays, A = {}, {}
    tables = {"consts": constant_table(), "dft": dft_table()}
    for name in _INS + list(tables):
        a = np.ascontiguousarray(tables[name] if name in tables else inputs[name])
        arrays[f"in_{name}"] = a
        A[name] = nc.dram_tensor(f"in_{name}", a.shape, mybir.dt.from_np(a.dtype), kind="ExternalInput").ap()
    out = nc.dram_tensor("out_0", (1, L, D), F32, kind="ExternalOutput").ap()
    A["out"] = out[0]
    build(nc, A)
    r = run_bass_kernel_spmd(nc, [arrays], core_ids=[0])
    return r.results[0]["out_0"]
```
